# Optimizing a Trainium2 kernel written in Bass

```python
import math
import jax
import jax.numpy as jnp
from jax import lax
import numpy as np
import jax, jax.numpy as jnp

D_MODEL = 1024
BATCH = 1
SEQ = 512
DEPTH = 2

CTX_LEN = 256
GRID_W = 64
MIX_W = D_MODEL
FOURIER_W = MIX_W // 4
FOURIER_GROUPS = 4
FOURIER_GD = FOURIER_W // FOURIER_GROUPS
POOL_W = MIX_W // 4
POOL_WINDOWS = (2, 4, 8, 16)
POOL_GD = POOL_W // len(POOL_WINDOWS)
ATTN_W = MIX_W - FOURIER_W - POOL_W
QK_DIM = 64
V_DIM = 2 * QK_DIM
N_HEADS = ATTN_W // V_DIM
QK_W = N_HEADS * 2 * QK_DIM
Q_BLOCK = 128
ROPE_THETA = 10000.0
EPS = 1e-6

A_OFF = 0
B_OFF = A_OFF + FOURIER_W
Q_OFF = B_OFF + POOL_W
K_OFF = Q_OFF + QK_W
V_OFF = K_OFF + QK_W
G_OFF = V_OFF + ATTN_W
IN_W = G_OFF + MIX_W


def rms_norm(t, g):
    tf = t.astype(jnp.float32)
    y = tf * lax.rsqrt(jnp.mean(tf * tf, axis=-1, keepdims=True) + EPS)
    return (y * g.astype(jnp.float32)).astype(t.dtype)

def axial_rope_tables(rows):
    row = jnp.repeat(jnp.arange(rows), GRID_W).astype(jnp.float32)
    col = jnp.tile(jnp.arange(GRID_W), rows).astype(jnp.float32)
    half = QK_DIM // 2
    inv_freq = ROPE_THETA ** (-jnp.arange(0, half, 2, dtype=jnp.float32) / half)
    ang_r = row[:, None] * inv_freq[None, :]
    ang_c = col[:, None] * inv_freq[None, :]
    ang = jnp.concatenate([ang_r, ang_r, ang_c, ang_c], axis=-1)
    return jnp.cos(ang), jnp.sin(ang)

def apply_rope(t, cos, sin):
    tr = t.reshape(t.shape[:-1] + (2, 2, QK_DIM // 4))
    rot = jnp.stack([-tr[..., 1, :], tr[..., 0, :]], axis=-2).reshape(t.shape)
    return (t * cos + rot * sin).astype(t.dtype)

def centred_window_mean(u, w):
    L = u.shape[1]
    lo = w // 2
    hi = w - lo - 1
    cs = jnp.pad(jnp.cumsum(u.astype(jnp.float32), axis=1), ((0, 0), (1, 0), (0, 0)))
    t = jnp.arange(L)
    a = jnp.clip(t - lo, 0, L - 1)
    b = jnp.clip(t + hi, 0, L - 1)
    s = cs[:, b + 1] - cs[:, a]
    cnt = (b - a + 1).astype(jnp.float32)
    return (s / cnt[None, :, None]).astype(u.dtype)

def fourier_mix(a, w_fourier):
    B_, L = a.shape[:2]
    ag = a.reshape(B_, L, FOURIER_GROUPS, FOURIER_GD).astype(jnp.float32)
    f = jnp.fft.fftn(ag, axes=(1, 3), norm='ortho').real.astype(a.dtype)
    y = jnp.einsum('blgc,gcd->blgd', f, w_fourier)
    return y.reshape(B_, L, FOURIER_W)

def pool_mix(b, w_pool, pool_scale):
    B_, L = b.shape[:2]
    bg = b.reshape(B_, L, len(POOL_WINDOWS), POOL_GD)
    pooled = jnp.stack([centred_window_mean(bg[:, :, gi], w) for gi, w in enumerate(POOL_WINDOWS)], axis=2) - bg
    y = jnp.einsum('blgc,gcd->blgd', pooled, w_pool).reshape(B_, L, POOL_W)
    return y * pool_scale

def split_heads_qk(t):
    B_, L = t.shape[:2]
    return t.reshape(B_, L, N_HEADS, 2, QK_DIM).transpose(0, 2, 3, 1, 4)

def split_heads_v(t):
    B_, L = t.shape[:2]
    return t.reshape(B_, L, N_HEADS, V_DIM).transpose(0, 2, 1, 3)

def diff_attend(q, k, v, lam):
    s = jnp.einsum('bhmqd,bhmkd->bhmqk', q, k).astype(jnp.float32) * (QK_DIM ** -0.5)
    p = jax.nn.softmax(s, axis=-1)
    p = p[:, :, 0] - lam * p[:, :, 1]
    return jnp.einsum('bhqk,bhkd->bhqd', p.astype(v.dtype), v)

def attn_post(o, subln_g, lam_init):
    o = rms_norm(o, subln_g) * (1.0 - lam_init)
    B_, H, L, dv = o.shape
    return o.transpose(0, 2, 1, 3).reshape(B_, L, H * dv)

def mixer_out(a_in, b_in, attn, gate, w_fourier, w_pool, pool_scale, w_out):
    y = jnp.concatenate([fourier_mix(a_in, w_fourier), pool_mix(b_in, w_pool, pool_scale), attn], axis=-1)
    return (y * jax.nn.silu(gate)) @ w_out

def mixer_layer(layer_idx, x, ctx, c, c_ctx, norm_g, w_mod, b_mod, w_in, w_fourier, w_pool,
                pool_scale, qk_norm_g, lam_vecs, subln_g, w_out, rope_cos, rope_sin, update_ctx):
    shift, scale, gate = jnp.split(jax.nn.silu(c) @ w_mod + b_mod, 3, axis=-1)
    shift_c, scale_c, gate_c = jnp.split(jax.nn.silu(c_ctx) @ w_mod + b_mod, 3, axis=-1)
    h = rms_norm(x, norm_g) * (1 + scale[:, None]) + shift[:, None]
    hc = rms_norm(ctx, norm_g) * (1 + scale_c) + shift_c

    lam_init = 0.8 - 0.6 * math.exp(-0.3 * layer_idx)
    lv = lam_vecs.astype(jnp.float32)
    lam = jnp.exp(jnp.sum(lv[0] * lv[1])) - jnp.exp(jnp.sum(lv[2] * lv[3])) + lam_init

    p = h @ w_in
    a_in, b_in = p[..., A_OFF:B_OFF], p[..., B_OFF:Q_OFF]
    q, k, v, g = p[..., Q_OFF:K_OFF], p[..., K_OFF:V_OFF], p[..., V_OFF:G_OFF], p[..., G_OFF:]

    if update_ctx:
        pc = hc @ w_in
        kc, vc = pc[..., K_OFF:V_OFF], pc[..., V_OFF:G_OFF]
    else:
        pkv = hc @ w_in[:, K_OFF:G_OFF]
        kc, vc = pkv[..., :QK_W], pkv[..., QK_W:]

    q_lat = apply_rope(rms_norm(split_heads_qk(q), qk_norm_g[0]), rope_cos, rope_sin)
    k_lat = apply_rope(rms_norm(split_heads_qk(k), qk_norm_g[1]), rope_cos, rope_sin)
    k_ctx = rms_norm(split_heads_qk(kc), qk_norm_g[1])
    v_ctx = split_heads_v(vc)
    k_all = jnp.concatenate([k_ctx, k_lat], axis=3)
    v_all = jnp.concatenate([v_ctx, split_heads_v(v)], axis=2)

    B_, H, _, L, d = q_lat.shape
    nb = L // Q_BLOCK
    qb = jnp.moveaxis(q_lat.reshape(B_, H, 2, nb, Q_BLOCK, d), 3, 0)
    ob = lax.map(lambda qblk: diff_attend(qblk, k_all, v_all, lam), qb)
    o = jnp.moveaxis(ob, 0, 2).reshape(B_, H, L, V_DIM)
    attn = attn_post(o, subln_g, lam_init)

    x_new = x + gate[:, None] * mixer_out(a_in, b_in, attn, g, w_fourier, w_pool, pool_scale, w_out)

    if update_ctx:
        qc = rms_norm(split_heads_qk(pc[..., Q_OFF:K_OFF]), qk_norm_g[0])
        attn_c = attn_post(diff_attend(qc, k_ctx, v_ctx, lam), subln_g, lam_init)
        ctx = ctx + gate_c * mixer_out(pc[..., A_OFF:B_OFF], pc[..., B_OFF:Q_OFF], attn_c,
                                       pc[..., G_OFF:], w_fourier, w_pool, pool_scale, w_out)
    return x_new, ctx

def first_inputs(seed: int = 0) -> dict:
    key = jax.random.key(seed)
    ks = jax.random.split(key, 16)
    f32 = jnp.float32
    nrm = lambda k, shape: jax.random.normal(k, shape, dtype=f32)
    return {
        'x': nrm(ks[0], (BATCH, SEQ, D_MODEL)),
        'c': nrm(ks[1], (BATCH, D_MODEL)),
        'ctx': nrm(ks[2], (BATCH, CTX_LEN, D_MODEL)),
        'c_ctx': nrm(ks[3], (D_MODEL,)),
        'norm_g': 1.0 + 0.02 * nrm(ks[4], (DEPTH, D_MODEL)),
        'w_mod': nrm(ks[5], (DEPTH, D_MODEL, 3 * D_MODEL)) * D_MODEL ** -0.5,
        'b_mod': 0.02 * nrm(ks[6], (DEPTH, 3 * D_MODEL)),
        'w_in': nrm(ks[7], (DEPTH, D_MODEL, IN_W)) * D_MODEL ** -0.5,
        'w_fourier': nrm(ks[8], (DEPTH, FOURIER_GROUPS, FOURIER_GD, FOURIER_GD)) * FOURIER_GD ** -0.5,
        'w_pool': nrm(ks[9], (DEPTH, len(POOL_WINDOWS), POOL_GD, POOL_GD)) * POOL_GD ** -0.5,
        'pool_scale': 1.0 + 0.1 * nrm(ks[10], (DEPTH, POOL_W)),
        'qk_norm_g': 1.0 + 0.02 * nrm(ks[11], (DEPTH, 2, QK_DIM)),
        'lam_vecs': 0.1 * nrm(ks[12], (DEPTH, 4, QK_DIM)),
        'subln_g': 1.0 + 0.02 * nrm(ks[13], (DEPTH, V_DIM)),
        'w_out': nrm(ks[14], (DEPTH, MIX_W, D_MODEL)) * MIX_W ** -0.5,
    }

def first_block(x, c, ctx, c_ctx, norm_g, w_mod, b_mod, w_in, w_fourier, w_pool, pool_scale,
              qk_norm_g, lam_vecs, subln_g, w_out):
    rows = x.shape[1] // GRID_W
    rope_cos, rope_sin = axial_rope_tables(rows)
    for l in range(DEPTH):
        x, ctx = mixer_layer(l, x, ctx, c, c_ctx, norm_g[l], w_mod[l], b_mod[l], w_in[l],
                             w_fourier[l], w_pool[l], pool_scale[l], qk_norm_g[l], lam_vecs[l],
                             subln_g[l], w_out[l], rope_cos, rope_sin, l < DEPTH - 1)
    return x


HEAD_DIM = 128
RET_HEADS = D_MODEL // (2 * HEAD_DIM)
RET_DK = HEAD_DIM
RET_DV = HEAD_DIM
HGRN_HEADS = D_MODEL // (2 * HEAD_DIM)
HGRN_DK = HEAD_DIM
HGRN_DV = HEAD_DIM
RET_WIDTH = RET_HEADS * RET_DV
HGRN_WIDTH = HGRN_HEADS * HGRN_DV
MIX_WIDTH = RET_WIDTH + HGRN_WIDTH
RET_QK_W = RET_HEADS * RET_DK
HGRN_QK_W = HGRN_HEADS * HGRN_DK
SPLIT_SIZES = (RET_QK_W, RET_QK_W, RET_WIDTH, RET_WIDTH,
               HGRN_QK_W, HGRN_QK_W, HGRN_WIDTH, HGRN_WIDTH)
IN_COLS = sum(SPLIT_SIZES)
D_FF = 2816
CONV_WIDTH = 3
CHUNK = 64
ROPE_BASE = 10000.0
N_MOD = 6


def rms_norm_2(x, w):
    xf = x.astype(jnp.float32)
    y = xf * lax.rsqrt(jnp.mean(xf * xf, axis=-1, keepdims=True) + EPS)
    return (y * w.astype(jnp.float32)).astype(x.dtype)

def head_norm(o, w):
    H, D = o.shape[-2], o.shape[-1]
    y = o * lax.rsqrt(jnp.mean(o * o, axis=-1, keepdims=True) + EPS)
    return y * w.astype(jnp.float32).reshape(H, D)

def rotary(x, cos, sin):
    x1, x2 = jnp.split(x, 2, axis=-1)
    c = cos[None, :, None, :]
    s = sin[None, :, None, :]
    return jnp.concatenate([x1 * c - x2 * s, x1 * s + x2 * c], axis=-1)

def to_chunks(t):
    B, S, H, D = t.shape
    n = S // CHUNK
    return t.astype(jnp.float32).reshape(B, n, CHUNK, H, D).transpose(1, 0, 3, 2, 4)

def from_chunks(t):
    n, B, H, C, D = t.shape
    return t.transpose(1, 0, 3, 2, 4).reshape(B, n * C, H, D)

def retention_chunkwise(q, k, v, log_gamma):
    qc, kc, vc = to_chunks(q), to_chunks(k), to_chunks(v)
    B, H, DK, DV = qc.shape[1], qc.shape[2], qc.shape[4], vc.shape[4]
    pos = jnp.arange(CHUNK, dtype=jnp.float32)
    lg = log_gamma.astype(jnp.float32)[:, None]
    rel = pos[:, None] - pos[None, :]
    decay_mask = jnp.where(rel[None] >= 0, jnp.exp(lg[:, :, None] * jnp.maximum(rel, 0.0)[None]), 0.0)
    q_decay = jnp.exp(lg * (pos + 1.0))[None, :, :, None]
    k_decay = jnp.exp(lg * (CHUNK - 1.0 - pos))[None, :, :, None]
    chunk_decay = jnp.exp(lg[:, 0] * CHUNK)[None, :, None, None]

    def step(state, inp):
        qi, ki, vi = inp
        scores = jnp.einsum('bhid,bhjd->bhij', qi, ki) * decay_mask[None]
        intra = jnp.einsum('bhij,bhjv->bhiv', scores, vi)
        inter = jnp.einsum('bhid,bhdv->bhiv', qi, state) * q_decay
        new_state = state * chunk_decay + jnp.einsum('bhjd,bhjv->bhdv', ki * k_decay, vi)
        return new_state, intra + inter

    init = jnp.zeros((B, H, DK, DV), jnp.float32)
    _, out = lax.scan(step, init, (qc, kc, vc))
    return from_chunks(out)

def hgrn2_chunkwise(q, log_f, k, v):
    qc, lfc, kc, vc = to_chunks(q), to_chunks(log_f), to_chunks(k), to_chunks(v)
    B, H, DK, DV = qc.shape[1], qc.shape[2], qc.shape[4], vc.shape[4]
    causal = jnp.tril(jnp.ones((CHUNK, CHUNK), dtype=bool))[:, :, None]

    def step(state, inp):
        qi, lfi, ki, vi = inp
        b = jnp.cumsum(lfi, axis=-2)
        diff = b[:, :, :, None, :] - b[:, :, None, :, :]
        decay = jnp.where(causal, jnp.exp(jnp.where(causal, diff, 0.0)), 0.0)
        scores = jnp.sum(qi[:, :, :, None, :] * ki[:, :, None, :, :] * decay, axis=-1)
        intra = jnp.einsum('bhij,bhjv->bhiv', scores, vi)
        inter = jnp.einsum('bhid,bhdv->bhiv', qi * jnp.exp(b), state)
        b_last = b[:, :, -1:, :]
        new_state = state * jnp.exp(b_last)[:, :, 0, :, None] + jnp.einsum('bhjd,bhjv->bhdv', ki * jnp.exp(b_last - b), vi)
        return new_state, intra + inter

    init = jnp.zeros((B, H, DK, DV), jnp.float32)
    _, out = lax.scan(step, init, (qc, lfc, kc, vc))
    return from_chunks(out)

def hybrid_mixer(h, w_in, w_out, ret_norm_w, hgrn_norm_w, lb, cos, sin, log_gamma):
    B, S, _ = h.shape
    proj = h @ w_in
    idx = np.cumsum(SPLIT_SIZES)[:-1].tolist()
    rq, rk, rv, rg, hq, hf, hi, hg = jnp.split(proj, idx, axis=-1)

    rq = rotary(rq.reshape(B, S, RET_HEADS, RET_DK).astype(jnp.float32), cos, sin)
    rk = rotary(rk.reshape(B, S, RET_HEADS, RET_DK).astype(jnp.float32), cos, sin) * (RET_DK ** -0.5)
    rv = rv.reshape(B, S, RET_HEADS, RET_DV)
    r_out = retention_chunkwise(rq, rk, rv, log_gamma)
    r_out = head_norm(r_out, ret_norm_w) * jax.nn.silu(rg.astype(jnp.float32).reshape(B, S, RET_HEADS, RET_DV))

    z = hf.astype(jnp.float32).reshape(B, S, HGRN_HEADS, HGRN_DK)
    lbh = lb.astype(jnp.float32).reshape(HGRN_HEADS, HGRN_DK)
    log_f = jax.nn.log_sigmoid(z) + jnp.log1p(lbh * jnp.exp(-z))
    k_in = (1.0 - lbh) * jax.nn.sigmoid(-z)
    q_h = jax.nn.silu(hq.astype(jnp.float32).reshape(B, S, HGRN_HEADS, HGRN_DK))
    v_h = hi.reshape(B, S, HGRN_HEADS, HGRN_DV)
    g_out = hgrn2_chunkwise(q_h, log_f, k_in, v_h)
    g_out = head_norm(g_out, hgrn_norm_w) * jax.nn.silu(hg.astype(jnp.float32).reshape(B, S, HGRN_HEADS, HGRN_DV))

    merged = jnp.concatenate([r_out.reshape(B, S, RET_WIDTH), g_out.reshape(B, S, HGRN_WIDTH)], axis=-1)
    return merged.astype(h.dtype) @ w_out

def conv_ffn(h, w_gate, w_val, conv_w, conv_b, w_down):
    a = h @ w_gate
    S = a.shape[1]
    ap = jnp.pad(a, ((0, 0), (CONV_WIDTH - 1, 0), (0, 0)))
    acc = conv_b[None, None, :] + ap[:, 0:S] * conv_w[0]
    for j in range(1, CONV_WIDTH):
        acc = acc + ap[:, j:j + S] * conv_w[j]
    return (jax.nn.silu(acc) * (h @ w_val)) @ w_down

def second_inputs(seed: int = 0) -> dict:
    key = jax.random.key(seed)
    ks = jax.random.split(key, 20)
    f32 = jnp.float32
    nrm = lambda k, shape, s: (jax.random.normal(k, shape, f32) * s).astype(f32)
    return {
        'x': nrm(ks[0], (BATCH, SEQ, D_MODEL), 1.0),
        'c': nrm(ks[1], (BATCH, D_MODEL), 1.0),
        'w_in': nrm(ks[2], (DEPTH, D_MODEL, IN_COLS), D_MODEL ** -0.5),
        'w_out': nrm(ks[3], (DEPTH, MIX_WIDTH, D_MODEL), MIX_WIDTH ** -0.5),
        'ret_norm_w': 1.0 + nrm(ks[4], (DEPTH, RET_WIDTH), 0.02),
        'hgrn_norm_w': 1.0 + nrm(ks[5], (DEPTH, HGRN_WIDTH), 0.02),
        'hgrn_lb_logits': nrm(ks[6], (DEPTH, HGRN_HEADS * HGRN_DK), 0.1),
        'norm1_w': 1.0 + nrm(ks[7], (DEPTH, D_MODEL), 0.02),
        'norm2_w': 1.0 + nrm(ks[8], (DEPTH, D_MODEL), 0.02),
        'ada_w': nrm(ks[9], (DEPTH, D_MODEL, N_MOD * D_MODEL), 0.5 * D_MODEL ** -0.5),
        'ada_b': nrm(ks[10], (DEPTH, N_MOD * D_MODEL), 0.01),
        'w_gate': nrm(ks[11], (DEPTH, D_MODEL, D_FF), D_MODEL ** -0.5),
        'w_val': nrm(ks[12], (DEPTH, D_MODEL, D_FF), D_MODEL ** -0.5),
        'conv_w': nrm(ks[13], (DEPTH, CONV_WIDTH, D_FF), CONV_WIDTH ** -0.5),
        'conv_b': nrm(ks[14], (DEPTH, D_FF), 0.01),
        'w_down': nrm(ks[15], (DEPTH, D_FF, D_MODEL), D_FF ** -0.5),
        'final_norm_w': 1.0 + nrm(ks[16], (D_MODEL,), 0.02),
    }

def second_block(x, c, w_in, w_out, ret_norm_w, hgrn_norm_w, hgrn_lb_logits, norm1_w, norm2_w,
              ada_w, ada_b, w_gate, w_val, conv_w, conv_b, w_down, final_norm_w):
    S = x.shape[1]
    pos = jnp.arange(S, dtype=jnp.float32)
    inv_freq = ROPE_BASE ** (-jnp.arange(0, RET_DK, 2, dtype=jnp.float32) / RET_DK)
    ang = pos[:, None] * inv_freq[None, :]
    cos, sin = jnp.cos(ang), jnp.sin(ang)
    log_gamma = jnp.log(1.0 - jnp.exp2(-5.0 - jnp.arange(RET_HEADS, dtype=jnp.float32)))
    p = jax.nn.softmax(hgrn_lb_logits.astype(jnp.float32), axis=0)
    lower_bounds = jnp.cumsum(p, axis=0) - p[0:1]
    c_act = jax.nn.silu(c)

    for l in range(DEPTH):
        mod = (c_act @ ada_w[l] + ada_b[l])[:, None, :]
        sh1, sc1, g1, sh2, sc2, g2 = jnp.split(mod, N_MOD, axis=-1)
        h = rms_norm_2(x, norm1_w[l]) * (1.0 + sc1) + sh1
        x = x + g1 * hybrid_mixer(h, w_in[l], w_out[l], ret_norm_w[l], hgrn_norm_w[l],
                                  lower_bounds[l], cos, sin, log_gamma)
        h = rms_norm_2(x, norm2_w[l]) * (1.0 + sc2) + sh2
        x = x + g2 * conv_ffn(h, w_gate[l], w_val[l], conv_w[l], conv_b[l], w_down[l])

    return rms_norm_2(x, final_norm_w)


def setup_inputs(seed=0):
    out = dict(first_inputs(seed))
    for name, value in second_inputs(seed + 1).items():
        if name != "x":
            out[name + "_2"] = value
    return out


def reference(
    x, c, ctx, c_ctx, norm_g, w_mod, b_mod, w_in, w_fourier, w_pool, pool_scale, qk_norm_g,
    lam_vecs, subln_g, w_out, c_2, w_in_2, w_out_2, ret_norm_w_2, hgrn_norm_w_2,
    hgrn_lb_logits_2, norm1_w_2, norm2_w_2, ada_w_2, ada_b_2, w_gate_2, w_val_2, conv_w_2,
    conv_b_2, w_down_2, final_norm_w_2,
):
    x = first_block(
        x, c, ctx, c_ctx, norm_g, w_mod, b_mod, w_in, w_fourier, w_pool, pool_scale, qk_norm_g,
        lam_vecs, subln_g, w_out,
    )
    return second_block(
        x, c_2, w_in_2, w_out_2, ret_norm_w_2, hgrn_norm_w_2, hgrn_lb_logits_2, norm1_w_2,
        norm2_w_2, ada_w_2, ada_b_2, w_gate_2, w_val_2, conv_w_2, conv_b_2, w_down_2,
        final_norm_w_2,
    )


_drawn_inputs = setup_inputs


def setup_inputs(seed=0):
    import zlib

    import numpy as np

    out = dict(_drawn_inputs(seed))
    spreads = {}
    factors = {'norm_g': 3.99,
     'qk_norm_g': 8.0,
     'lam_vecs': 4.487,
     'subln_g': 7.383,
     'ret_norm_w_2': 26.189,
     'hgrn_norm_w_2': 27.146,
     'hgrn_lb_logits_2': 8.0,
     'norm1_w_2': 6.784,
     'norm2_w_2': 7.677,
     'ada_b_2': 3.791,
     'conv_b_2': 47.022,
     'final_norm_w_2': 7.33}
    for name, (base, spread) in spreads.items():
        noise = np.random.default_rng([zlib.crc32(name.encode()), seed]).standard_normal(out[name].shape)
        drawn = base * np.exp(spread * noise) if base else spread * noise
        out[name] = jnp.asarray(drawn.astype(out[name].dtype))
    for name, factor in factors.items():
        out[name] = (out[name] * factor).astype(out[name].dtype)
    return out
```

```python
import math
from contextlib import contextmanager

import numpy as np
import concourse.bass as bass
from concourse import mybir

F32 = mybir.dt.float32
F32R = mybir.dt.float32r
I32 = mybir.dt.int32
ALU = mybir.AluOpType
ACT = mybir.ActivationFunctionType
AX = mybir.AxisListType.X
ET = mybir.EngineType

P = 128
D = 1024
KT = D // P
TX = 512
TC = 256
TA = TX + TC
EPS = 1e-6
GRID_W = 64
QK = 64
HEADS = 4
FF = 2816
FFH = FF // P // 2
CHUNK_COLS = 256
LEVELS = (1, 2, 4, 8, 16, 32, 64)
SLOT = FFH * P


def tables():
    t = {}
    eye = np.eye(P, dtype=np.float32)
    t["ident"] = eye
    t["ones"] = np.ones((P, P), np.float32)
    half = np.kron(np.eye(2), np.ones((QK, QK)))
    t["ones_half"] = half.astype(np.float32)
    rot = np.zeros((P, P), np.float32)
    for base in range(0, P, 32):
        for i in range(16):
            rot[base + 16 + i, base + i] = -1.0
            rot[base + i, base + 16 + i] = 1.0
    t["rot_axial"] = rot
    rot = np.zeros((P, P), np.float32)
    for i in range(64):
        rot[64 + i, i] = -1.0
        rot[i, 64 + i] = 1.0
    t["rot_half"] = rot
    n = np.arange(64)
    ang = 2 * np.pi * np.outer(n, n) / 64
    t["dft_c"] = np.kron(np.eye(2), np.cos(ang) / 8).astype(np.float32)
    t["dft_ns"] = np.kron(np.eye(2), -np.sin(ang) / 8).astype(np.float32)
    square = ["ident", "ones", "ones_half", "rot_axial", "rot_half", "dft_c", "dft_ns"]
    out = {"squares": np.stack([t[k] for k in square], 1)}

    f4 = np.float32
    rows = TX // GRID_W
    row = np.repeat(np.arange(rows), GRID_W).astype(f4)
    col = np.tile(np.arange(GRID_W), rows).astype(f4)
    inv = (f4(10000.0) ** (-np.arange(0, 32, 2, dtype=f4) / f4(32))).astype(f4)
    ar, ac = row[:, None] * inv[None], col[:, None] * inv[None]
    ang = np.concatenate([ar, ar, ac, ac], -1).astype(f4)
    cs = np.stack([np.cos(ang).T, np.sin(ang).T], 1)
    out["rope_axial"] = np.concatenate([cs, cs], 0).astype(f4)

    def dft(length):
        k = np.arange(length)
        a = 2 * np.pi * (np.outer(k, k) % length) / length
        c = np.stack([np.cos(a), np.sin(a)]) / math.sqrt(length)
        return c.reshape(2, length // P, P, length).transpose(2, 0, 1, 3).astype(f4)
    out["dft_x"] = dft(TX)
    out["dft_ctx"] = dft(TC)

    def inv_counts(length):
        t_ = np.arange(length)
        r = []
        for w in (2, 4, 8, 16):
            lo, hi = w // 2, w - w // 2 - 1
            a, b = np.clip(t_ - lo, 0, length - 1), np.clip(t_ + hi, 0, length - 1)
            r.append(1.0 / (b - a + 1))
        r = np.array(r)
        return np.repeat(r.reshape(2, 2, 1, length), 64, 2).reshape(2, P, length).transpose(1, 0, 2)
    inv = (f4(10000.0) ** (-np.arange(0, P, 2, dtype=f4) / f4(P))).astype(f4)
    ang = (np.arange(TX, dtype=f4)[:, None] * inv[None]).astype(f4).T
    cs = np.stack([np.cos(ang), np.sin(ang)], 1)
    out["rope_half"] = np.concatenate([cs, cs], 0).astype(f4)
    gamma = 1.0 - 2.0 ** (-5.0 - np.arange(HEADS))
    dist = np.arange(TX)[None, :] - np.arange(P)[:, None]
    decay = np.where(dist[:, None] >= 0, gamma[None, :, None] ** np.maximum(dist[:, None], 0), 0.0)
    out["decay"] = (decay * P ** -0.5).astype(f4)
    k_, q_ = np.arange(P)[:, None], np.arange(P)[None, :]
    masks = [k_ == q_]
    for half in LEVELS:
        masks.append((k_ // (2 * half) == q_ // (2 * half)) & (k_ // half % 2 == 0) & (q_ // half % 2 == 1))
    out["level_masks"] = np.stack(masks, 1).astype(np.int32)
    out["inv_count"] = np.concatenate([inv_counts(TX), inv_counts(TC)], -1).astype(f4)
    return out


class Engine:

    def __init__(self, nc, e, kind, name, hold=False):
        self.e, self.kind, self.sem, self.n, self.pass_ = e, kind, nc.alloc_semaphore(name), 0, None
        self.hold = nc.alloc_semaphore(name + "_holds") if hold else None

    def wait(self, *tokens):
        for sem, value in tokens:
            self.e.wait_ge(sem, value)
        if self.hold and any(not isinstance(value, int) for _, value in tokens):
            self.e.sem_inc(self.hold, 1)
        return self.e

    def now(self):
        if self.pass_ is None:
            return (self.sem, self.n)
        i, per, base = self.pass_
        return (self.sem, i * per + (base + self.n))

    def did(self, instruction):
        instruction.then_inc(self.sem, 1)
        self.n += 1
        return self.now()


@contextmanager
def passes(nc, n, counts):
    with nc.Fori(0, n, engines=[e.kind for e in counts]) as i:
        for e, per in counts.items():
            e.pass_, e.n = (i, per, e.n), 0
        yield i
        for e, per in counts.items():
            assert e.n == per, (e.kind, "marks in a pass:", e.n, "declared", per)
            e.n, e.pass_ = e.pass_[2] + n * per, None


class Program:

    def __init__(self, nc, dram):
        self.nc, self.dram = nc, dram
        self.T = Engine(nc, nc.tensor, ET.PE, "tensor_progress")
        self.V = Engine(nc, nc.vector, ET.DVE, "vector_progress")
        self.A = Engine(nc, nc.scalar, ET.Activation, "scalar_progress", hold=True)
        self.G = Engine(nc, nc.gpsimd, ET.Pool, "gpsimd_progress")
        self.S = Engine(nc, nc.sync, ET.SP, "sync_progress", hold=True)
        self.top = 16640
        sem = nc.alloc_semaphore
        self.consts_in = sem("consts_landed")
        self.x_in = sem("x_landed")
        self.out_stored = sem("out_stored")
        self.landed = [sem(f"weight_landed{j}") for j in (0, 1)]
        self.rounded = [sem(f"weight_rounded{j}") for j in (0, 1)]
        self.split = [sem(f"weight_split{j}") for j in (0, 1)]
        self.used = [sem(f"weight_used{j}") for j in (0, 1)]
        self.freed = [sem(f"bank_freed{j}") for j in (0, 1)]
        self.uses = 0
        self.mod_landed = [sem(f"mod_landed{j}") for j in (0, 1)]
        self.mod_summed = [sem(f"mod_summed{j}") for j in (0, 1)]
        self.mod_turned = [sem(f"mod_turned{j}") for j in (0, 1)]
        self.mod_uses = [0, 0]
        self.layer_sems = [*self.landed, *self.rounded, *self.split, *self.used, *self.freed]

        self.xT = self.place("xT", [P, KT, TA])
        self.lower = self.top
        self.h_hi = self.place("h_hi", [P, KT, TA], F32R)
        self.h_lo = self.place("h_lo", [P, KT, TA], F32R)
        self.squares = self.place("squares", [P, 7, P])
        (self.ident, self.ones, self.ones_half, self.rot_axial, self.rot_half,
         self.dft_c, self.dft_ns) = (self.squares[:, k, :] for k in range(7))
        self.cols = self.place("cols", [P, 5, P])
        self.colsf = self.cols[:, :, :].rearrange("p a b -> p (a b)")
        self.mod1 = self.place("mod1", [P, 2, 2, 24])
        self.mod2 = self.place("mod2", [P, 96])
        self.act_c = self.place("act_c", [P, 24])
        self.eps = self.place("eps", [P, 1])
        self.small = self.place("small", [P, 64])
        self.rope = self.place("rope", [P, 2, TX])
        self.ring_base = self.top
        self.place_ring("first", D)
        self.ps = nc.alloc_psum_tensor("ps", [P, 8, 512], F32)

    def place_ring(self, tag, floats):
        self.top = self.ring_base
        self.raw = [self.place(f"w_raw_{tag}{j}", [P, floats]) for j in (0, 1)]
        self.hi = [self.place(f"w_hi_{tag}{j}", [P, floats], F32R) for j in (0, 1)]
        self.lo = [self.place(f"w_lo_{tag}{j}", [P, floats], F32R) for j in (0, 1)]

    def place(self, name, shape, dt=F32, at=None):
        size = 4
        for s in shape[1:]:
            size *= s
        t = self.nc.alloc_sbuf_tensor_at(name, shape, dt, offset=self.top if at is None else at)
        if at is None:
            self.top += (size + 31) // 32 * 32
        return t

    def banks(self, b, n):
        return self.ps[:, :, :].rearrange("p b n -> p (b n)")[:, b * 512:b * 512 + n]

    def load_vectors(self):
        nc, d = self.nc, self.dram
        rows = self.place("vector_rows", [P, 5, P], at=self.lower)
        self.col, self.vectors_dma = {}, nc.alloc_semaphore("vectors_landed")
        plan = []
        r = 0
        def add(name, n, srcs):
            nonlocal r
            if r // P != (r + n - 1) // P:
                r = (r + P - 1) // P * P
            self.col[name] = r
            plan.append((r, n, srcs))
            r += n
        def rows_of(name, n):
            ap = d[name]
            letters = "abc"[:len(ap.shape)]
            flat = ap if len(ap.shape) == 1 else ap.rearrange(f"{' '.join(letters)} -> ({' '.join(letters)})")
            add(name, n, [(slice(0, P), flat.rearrange("(r p) -> r p", p=P))])
        rows_of("c", 8); rows_of("c_ctx", 8); rows_of("c_2", 8)
        rows_of("norm_g", 16); rows_of("b_mod", 48); rows_of("pool_scale", 4); rows_of("subln_g", 2)
        qk = d["qk_norm_g"].rearrange("l m k -> (l m) k")
        add("qk_norm_g", 4, [(slice(0, QK), qk), (slice(QK, P), qk)])
        rows_of("ret_norm_w_2", 8); rows_of("hgrn_norm_w_2", 8); rows_of("hgrn_lb_logits_2", 8)
        rows_of("norm1_w_2", 16); rows_of("norm2_w_2", 16); rows_of("final_norm_w_2", 8)
        rows_of("ada_b_2", 96); rows_of("conv_b_2", 44)
        add("conv_w0", 66, [(slice(0, P), d["conv_w_2"][0].rearrange("j (r p) -> (j r) p", p=P))])
        add("conv_w1", 66, [(slice(0, P), d["conv_w_2"][1].rearrange("j (r p) -> (j r) p", p=P))])
        assert r <= 5 * P, r
        zero = self.V.did(nc.vector.memset(rows[:, :, :], 0.0))
        nc.sync.wait_ge(*zero)
        n_dma = 0
        for at, n, srcs in plan:
            for where, src in srcs:
                nc.sync.dma_start(rows[at % P:at % P + n, at // P, where], src).then_inc(self.vectors_dma, 16)
                n_dma += 1
        self.T.wait((self.vectors_dma, 16 * n_dma), (self.consts_in, 16 * self.n_consts))
        for g in range(5):
            last = nc.tensor.transpose(self.banks(0, 5 * P)[:, g * P:(g + 1) * P], rows[:, g, :], self.ident)
        turned = self.T.did(last)
        self.A.wait(turned)
        self.cols_ready = self.A.did(nc.scalar.activation(self.colsf, self.banks(0, 5 * P), ACT.Identity))

    def column(self, name, k=0, n=1):
        return self.colsf[:, self.col[name] + k:self.col[name] + k + n]

    def load_constants(self):
        nc = self.nc
        self.lamv = self.place("lamv", [P, 2, 4, QK], at=self.lower + 8192)
        loads = [(self.squares, self.dram["squares"]), (self.rope, self.dram["rope_axial"])]
        for dst, src in loads:
            nc.sync.dma_start(dst[:, :, :], src).then_inc(self.consts_in, 16)
        lam = self.dram["lam_vecs"].rearrange("l a k -> (l a k)").rearrange("(o n) -> o n", o=1).broadcast_to([P, 512])
        nc.sync.dma_start(self.lamv[:, :, :, :].rearrange("p l a k -> p (l a k)"), lam).then_inc(self.consts_in, 16)
        self.n_consts = 3

    def grant_slots(self, evac):
        for j in (0, 1):
            self.T.e.sem_inc(self.used[j], 1)
            self.G.e.sem_inc(self.split[j], 1)
            evac.e.sem_inc(self.freed[j], 1)
        self.uses = 0

    def round_tile(self, j, use, k):
        self.A.wait((self.landed[j], use * 16), (self.used[j], use))
        self.A.e.activation(self.hi[j][:, 0:k * P], self.raw[j][:, 0:k * P], ACT.Copy).then_inc(self.rounded[j], 1)

    def prime(self, k):
        self.round_tile(0, self.uses + 1, k)

    def linear(self, n, k, source, moving, ready, act_evac, vec_evac=None, act_counts=0, vec_counts=0, then_k=None,
               mod=(), vec_frees=False, lead_source=None):
        nc, T, V, A, G = self.nc, self.T, self.V, self.A, self.G
        u, half = self.uses, n // 2
        with nc.Fori(0, half, engines=[ET.SP]) as i:
            for j in (0, 1):
                self.S.wait((self.split[j], i + (u + 1)))
                nc.sync.dma_start(self.raw[j][:, 0:k * P].rearrange("p (k n) -> p k n", k=k),
                                  source(i, j)).then_inc(self.landed[j], 16)
            for m in mod:
                self.mod_load(m, i)
        with nc.Fori(0, half, engines=[ET.Pool]) as i:
            for j in (0, 1):
                nc.gpsimd.wait_ge(self.rounded[j], i + (u + 1))
                nc.gpsimd.tensor_tensor(self.lo[j][:, 0:k * P], self.raw[j][:, 0:k * P],
                                        self.hi[j][:, 0:k * P].bitcast(F32), ALU.subtract).then_inc(self.split[j], 1)
        T.wait(*ready)
        with nc.Fori(0, half, engines=[ET.PE]) as i:
            for j in (0, 1):
                nc.tensor.wait_ge(self.split[j], i + (u + 2))
                nc.tensor.wait_ge(self.freed[j], i + (u + 1))
                for q in range(k):
                    w_hi = self.hi[j][:, q * P:(q + 1) * P]
                    w_lo = self.lo[j][:, q * P:(q + 1) * P]
                    terms = [(w_hi, 0), (w_hi, 1), (w_lo, 0)]
                    for t, (w, which) in enumerate(terms):
                        for bank, c, cols in moving:
                            x = (self.h_hi, self.h_lo)[which] if not self.act_pair else self.act_pair[which]
                            last = nc.tensor.matmul(self.ps[:, bank + j, 0:cols], w, x[:, q, c:c + cols],
                                                    start=(q == 0 and t == 0), stop=(q == k - 1 and t == 2))
                last.then_inc(self.used[j], 1)
            for m in mod:
                self.mod_turn(m, i)
        if mod or vec_evac:
            counts = {V: vec_counts + sum(self.mod_counts(m) for m in mod)}
            with passes(nc, half, counts) as i:
                for m in mod:
                    self.mod_sum(m, i)
                for j in (0, 1):
                    if vec_evac:
                        vec_evac(i, j, i + (u + 2))
                for m in mod:
                    self.mod_finish(m, i)
            self.mod_last = V.now()
            for m in mod:
                self.mod_uses[m["slot"]] += half
        if half > 1:
            with passes(nc, half - 1, {A: act_counts}) as i:
                self.round_tile(1, i + (u + 1), k)
                act_evac(i, 0, i + (u + 2))
                self.round_tile(0, i + (u + 2), k)
                act_evac(i, 1, i + (u + 2))
        self.round_tile(1, u + half, k)
        act_evac(half - 1, 0, u + half + 1)
        if then_k:
            self.round_tile(0, u + half + 1, then_k)
        act_evac(half - 1, 1, u + half + 1)
        self.uses = u + half
        self.product_done = (self.used[1], u + half + 1)
        self.banks_read = [(self.freed[j], u + half + 1) for j in (0, 1)]

    act_pair = None

    def mod_setup(self):
        self.mod_w = [self.place(f"mod_w{s}", [P, KT, CHUNK_COLS]) for s in (0, 1)]
        self.mod_acc = [[self.place(f"mod_acc{s}{v}", [P, CHUNK_COLS]) for v in (0, 1)] for s in (0, 1)]
        for s in (0, 1):
            self.V.e.sem_inc(self.mod_summed[s], 1)

    def mod_chunk(self, slot, source, outs):
        return {"slot": slot, "source": source, "outs": outs}

    def mod_counts(self, m):
        return (KT + 1) * len(m["outs"]) - 1

    def mod_use(self, m, i, add):
        return i + (self.mod_uses[m["slot"]] + add)

    def mod_load(self, m, i):
        s = m["slot"]
        self.S.wait((self.mod_summed[s], self.mod_use(m, i, 1)))
        self.S.e.dma_start(self.mod_w[s][:, :, :], m["source"](i)).then_inc(self.mod_landed[s], 16)

    def mod_sum(self, m, i):
        s, V = m["slot"], self.V
        V.wait((self.mod_landed[s], self.mod_use(m, i, 1) * 16))
        for v, (c, _, _) in enumerate(m["outs"]):
            acc, w = self.mod_acc[s][v][:, :], self.mod_w[s]
            t = V.did(V.e.tensor_scalar(acc, w[:, 0, :], self.act_c[:, c:c + 1], None, ALU.mult))
            for q in range(1, KT):
                V.wait(t)
                x = V.e.scalar_tensor_tensor(acc, w[:, q, :], self.act_c[:, c + q:c + q + 1], acc, ALU.mult, ALU.add)
                if q < KT - 1:
                    t = V.did(x)
                elif v == len(m["outs"]) - 1:
                    x.then_inc(self.mod_summed[s], 1)
                else:
                    V.did(x)

    def mod_turn(self, m, i):
        s = m["slot"]
        self.T.wait((self.mod_summed[s], self.mod_use(m, i, 2)))
        for v in range(len(m["outs"])):
            for q in range(2):
                k = v * 2 + q
                last = self.T.e.matmul(self.ps[:, 7 - s, k:k + 1], self.mod_acc[s][v][:, q * P:(q + 1) * P],
                                       self.ones[:, 0:1], start=True, stop=True)
        last.then_inc(self.mod_turned[s], 1)

    def mod_finish(self, m, i):
        s, V = m["slot"], self.V
        V.wait((self.mod_turned[s], self.mod_use(m, i, 1)))
        for v, (_, out, bias) in enumerate(m["outs"]):
            k = v * 2
            V.did(V.e.tensor_tensor(out(i), self.ps[:, 7 - s, k:k + 2], bias(i), ALU.add))

    def mod_alone(self, n, mods):
        nc = self.nc
        with nc.Fori(0, n, engines=[ET.SP]) as i:
            for m in mods:
                self.mod_load(m, i)
        with nc.Fori(0, n, engines=[ET.PE]) as i:
            for m in mods:
                self.mod_turn(m, i)
        with passes(nc, n, {self.V: sum(self.mod_counts(m) for m in mods)}) as i:
            for m in mods:
                self.mod_sum(m, i)
            for m in mods:
                self.mod_finish(m, i)
        self.mod_last = self.V.now()
        for m in mods:
            self.mod_uses[m["slot"]] += n

    def norm(self, tag, t, x_ready, segments, free):
        nc, T, V, A, G = self.nc, self.T, self.V, self.A, self.G
        sq, rstd, tmp, h = self.norm_buffers
        A.wait(*x_ready, *free)
        T.wait(*free)
        taken = []
        for k in range(KT):
            if k >= 2:
                A.wait(taken[k - 2])
            s = A.did(A.e.activation(sq[k % 2][:, 0:t], self.xT[:, k, 0:t], ACT.Square))
            T.wait(s)
            for b in range(0, t, 512):
                last = T.e.matmul(self.ps[:, 4 + b // 512, 0:min(512, t - b)], self.ones,
                                  sq[k % 2][:, b:min(t, b + 512)], start=(k == 0), stop=(k == KT - 1))
            taken.append(T.did(last))
        A.wait(taken[-1])
        r = A.did(A.e.activation(rstd[:, 0:t], self.banks(4, t), ACT.Sqrt, bias=self.eps[:, 0:1], scale=1.0 / D))
        V.wait(r)
        r = V.did(V.e.reciprocal(rstd[:, 0:t], rstd[:, 0:t]))
        hi_done, lo_done, last_lo = [], [], []
        for k in range(KT):
            b = k % 2
            V.wait(r, *x_ready)
            if k >= 2:
                V.wait(hi_done[k - 2], lo_done[k - 2])
            n = V.did(V.e.tensor_tensor(tmp[b][:, 0:t], self.xT[:, k, 0:t], rstd[:, 0:t], ALU.mult))
            V.wait(n)
            A.wait(n)
            for first, count, gain, shift in segments:
                cut = slice(first, first + count)
                hv = V.did(V.e.tensor_scalar(h[b][:, cut], tmp[b][:, cut], gain[:, k:k + 1], shift[:, k:k + 1],
                                             ALU.mult, ALU.add))
                hh = A.did(A.e.activation(self.h_hi[:, k, cut], tmp[b][:, cut], ACT.Identity,
                                          bias=shift[:, k:k + 1], scale=gain[:, k:k + 1]))
            hi_done.append(hh)
            G.wait(hv, hh)
            lo = G.did(G.e.tensor_tensor(self.h_lo[:, k, 0:t], h[b][:, 0:t], self.h_hi[:, k, 0:t].bitcast(F32),
                                         ALU.subtract))
            lo_done.append(lo)
        return [hi_done[-1], lo_done[-1]]

    def split_pair(self, k, cut, value, ready):
        self.A.wait(*ready)
        hh = self.A.did(self.A.e.activation(self.h_hi[:, k, cut], value, ACT.Copy))
        self.G.wait(*ready, hh)
        return self.G.did(self.G.e.tensor_tensor(self.h_lo[:, k, cut], value, self.h_hi[:, k, cut].bitcast(F32),
                                                 ALU.subtract))


X_, C_ = slice(0, TX), slice(TX, TA)
TILE_A, TILE_B, TILE_Q, TILE_K, TILE_V, TILE_G = 0, 2, 4, 8, 12, 16


def load_x(p):
    nc, T, A = p.nc, p.T, p.A
    rows = p.place("x_rows", [P, TA // P, D], at=p.lower + 24576)
    nc.sync.dma_start(rows[:, 0:4, :], p.dram["x"].rearrange("b (t p) d -> p (b t) d", p=P)).then_inc(p.x_in, 16)
    nc.sync.dma_start(rows[:, 4:6, :], p.dram["ctx"].rearrange("b (t p) d -> p (b t) d", p=P)).then_inc(p.x_in, 16)
    T.wait((p.x_in, 32), (p.consts_in, 16 * p.n_consts))
    copied = []
    for k in range(KT):
        b = 2 + 2 * (k % 2)
        if k >= 2:
            T.wait(copied[k - 2])
        for t in range(TA // P):
            last = T.e.transpose(p.banks(b, TA)[:, t * P:(t + 1) * P], rows[:, t, k * P:(k + 1) * P], p.ident)
        A.wait(T.did(last))
        copied.append(A.did(A.e.activation(p.xT[:, k, :], p.banks(b, TA), ACT.Copy)))
    return copied[-1]


def first_block(p):
    nc, T, V, A, G = p.nc, p.T, p.V, p.A, p.G
    p.load_constants()
    p.load_vectors()
    p.mod_setup()
    eps = V.did(nc.vector.memset(p.eps[:, :], EPS))
    x_there = load_x(p)

    A.wait(p.cols_ready)
    c_there = A.did(nc.scalar.activation(p.act_c[:, :], p.column("c", 0, 24), ACT.Silu))
    lam, dots = p.small[:, 0:2], p.small[:, 2:6]
    prod = p.place("lam_products", [P, 2, 2, QK], at=p.lower + 12288)
    V.wait((p.consts_in, 16 * p.n_consts))
    t = V.did(V.e.tensor_tensor(prod[:, :, :, :], p.lamv[:, :, 0:4:2, :], p.lamv[:, :, 1:4:2, :], ALU.mult))
    V.wait(t)
    t = V.did(V.e.tensor_reduce(dots, prod[:, :, :, :].rearrange("p l a k -> p (l a) k"), AX, ALU.add))
    A.wait(t)
    t = A.did(A.e.activation(dots, dots, ACT.Exp))
    V.wait(t)
    for l in range(2):
        init = 0.8 - 0.6 * math.exp(-0.3 * l)
        t = V.did(V.e.scalar_tensor_tensor(lam[:, l:l + 1], dots[:, 2 * l + 1:2 * l + 2], -init,
                                           dots[:, 2 * l:2 * l + 1], ALU.add, ALU.subtract))
    lam_ready = t
    qk_gain = p.place("qk_gain", [P, 2, 8])
    sub_gain = p.small[:, 8:10]
    V.wait(p.cols_ready)
    for l in range(2):
        for m in range(2):
            for r in range(4):
                t = V.did(V.e.tensor_copy(qk_gain[:, l, 4 * m + r:4 * m + r + 1], p.column("qk_norm_g", 2 * l + m)))
        init = 0.8 - 0.6 * math.exp(-0.3 * l)
        t = V.did(V.e.tensor_scalar(sub_gain[:, l:l + 1], p.column("subln_g", l), 1.0 - init, None, ALU.mult))
    gains_ready = t

    wblk = p.place("group_weights", [P, 2, 2, 2, P])
    t = V.did(V.e.memset(wblk[:, :, :, :, :].rearrange("p a b c d -> p (a b c d)"), 0.0))
    nc.sync.wait_ge(*t)
    groups_in = nc.alloc_semaphore("group_weights_landed")
    for which, name in ((0, "w_pool"), (1, "w_fourier")):
        for l in range(2):
            for g in range(4):
                half = slice(64 * (g % 2), 64 * (g % 2) + 64)
                nc.sync.dma_start(wblk[half, l, which, g // 2, half], p.dram[name][l, g]).then_inc(groups_in, 16)
    groups_ready = (groups_in, 16 * 16)

    w_mod, ada = p.dram["w_mod"], p.dram["ada_w_2"]

    def mod1(l, slot, chunk):
        def source(i):
            return w_mod[l].rearrange("(k p) n -> p k n", p=P)[:, :, bass.ds(chunk(i) * CHUNK_COLS, CHUNK_COLS)]
        outs = [(8 * v, lambda i, v=v: p.mod1[:, l, v, bass.ds(chunk(i) * 2, 2)],
                 lambda i: p.colsf[:, bass.ds(chunk(i) * 2 + (p.col["b_mod"] + 24 * l), 2)]) for v in (0, 1)]
        return p.mod_chunk(slot, source, outs)

    def mod2(l, slot, chunk):
        def source(i):
            return ada[l].rearrange("(k p) n -> p k n", p=P)[:, :, bass.ds(chunk(i) * CHUNK_COLS, CHUNK_COLS)]
        return p.mod_chunk(slot, source, [
            (16, lambda i: p.mod2[:, bass.ds(chunk(i) * 2 + 48 * l, 2)],
             lambda i: p.colsf[:, bass.ds(chunk(i) * 2 + (p.col["ada_b_2"] + 48 * l), 2)])])

    V.wait(c_there)
    T.wait(V.now())
    p.mod_alone(6, [mod1(0, 0, lambda i: i * 2), mod1(0, 1, lambda i: i * 2 + 1)])

    proj = p.place("proj", [P, 24, TA])
    at = p.top - (24 - TILE_G) * TA * 4
    sq = [p.place(f"nsq{b}", [P, TA], at=at + b * 3072) for b in (0, 1)]
    rstd = p.place("nrstd", [P, TA], at=at + 6144)
    tmp = [p.place(f"ntmp{b}", [P, TA], at=at + 9216 + b * 3072) for b in (0, 1)]
    hf = [p.place(f"nh{b}", [P, TA], at=at + 15360 + b * 3072) for b in (0, 1)]
    p.mix_scratch = at - (TILE_G - TILE_K) * TA * 4
    p.norm_buffers = (sq, rstd, tmp, hf)
    gain = p.place("norm_gain", [P, 2, 2, 8])

    p.grant_slots(A)
    x_ready, free = [x_there, eps], [x_there, p.mod_last, lam_ready]
    for l in range(2):
        update_ctx = l == 0
        V.wait(p.mod_last)
        for v in range(2):
            t = V.did(V.e.scalar_tensor_tensor(gain[:, l, v, :], p.mod1[:, l, v, 8:16], 1.0,
                                               p.column("norm_g", 8 * l, 8), ALU.add, ALU.mult))
        gain_ready = t
        if l == 0:
            p.prime(KT)
        V.wait(gain_ready); A.wait(gain_ready)
        segments = [(0, TX, gain[:, l, 0, :], p.mod1[:, l, 0, 0:8]), (TX, TC, gain[:, l, 1, :], p.mod1[:, l, 1, 0:8])]
        h_ready = p.norm(f"l{l}", TA, x_ready, segments, free)

        def w_in(first):
            return lambda i, j: p.dram["w_in"][l].rearrange("(k p) n -> p k n", p=P)[
                :, :, bass.ds(i * (2 * P) + (first + j) * P, P)]

        def to_proj(first, func, ctx):
            def evac(i, j, use):
                A.wait((p.used[j], use))
                x = A.e.activation(proj[:, bass.ds(i * 2 + (first + j), 1), X_].rearrange("p o t -> p (o t)"),
                                   p.ps[:, j, :], func)
                if ctx:
                    x = A.e.activation(proj[:, bass.ds(i * 2 + (first + j), 1), C_].rearrange("p o t -> p (o t)"),
                                       p.ps[:, 2 + j, 0:TC], func)
                x.then_inc(p.freed[j], 1)
            return evac

        both = [(0, 0, TX), (2, TX, TC)]
        only_x = [(0, 0, TX)]
        if l == 0:
            p.linear(16, KT, w_in(0), both, h_ready, to_proj(0, ACT.Identity, True), then_k=KT,
                     mod=[mod1(1, 0, lambda i: i), mod2(0, 1, lambda i: i)])
            p.linear(8, KT, w_in(16), both, [], to_proj(16, ACT.Silu, True),
                     mod=[mod1(1, 0, lambda i: i + 8), mod2(0, 1, lambda i: i + 8)])
        else:
            p.linear(8, KT, w_in(0), only_x, h_ready, to_proj(0, ACT.Identity, False), then_k=KT,
                     mod=[mod2(0, 0, lambda i: i + 12), mod2(1, 1, lambda i: i)])
            p.linear(8, KT, w_in(8), both, [], to_proj(8, ACT.Identity, True), then_k=KT,
                     mod=[mod2(0, 0, lambda i: i + 16), mod2(1, 1, lambda i: i + 4)])
            p.linear(8, KT, w_in(16), only_x, [], to_proj(16, ACT.Silu, False),
                     mod=[mod2(0, 0, lambda i: i + 20), mod2(1, 1, lambda i: i + 8)])
        projected = list(p.banks_read) + [p.mod_last, p.product_done]
        t = TA if update_ctx else TX
        load_tables(p, l, projected)
        qk_done = norm_rope(p, l, proj, qk_gain, projected, gains_ready)
        p.prime(KT)
        fourier_done = fourier(p, l, proj, wblk, t, qk_done, groups_ready)
        pool_done = pooling(p, l, proj, wblk, t, fourier_done)
        heads_done = attention(p, l, proj, lam, t, pool_done)
        mixed = mix(p, l, proj, sub_gain, t, heads_done)

        def w_out(i, j):
            return p.dram["w_out"][l].rearrange("(k p) n -> p k n", p=P)[:, :, bass.ds(i * (2 * P) + j * P, P)]

        def residual(i, j, use):
            V.wait((p.used[j], use))
            xk = p.xT[:, bass.ds(i * 2 + j, 1), X_].rearrange("p o t -> p (o t)")
            x = V.e.scalar_tensor_tensor(xk, p.ps[:, j, :], p.mod1[:, l, 0, bass.ds(i * 2 + (16 + j), 1)], xk,
                                         ALU.mult, ALU.add)
            if update_ctx:
                xk = p.xT[:, bass.ds(i * 2 + j, 1), C_].rearrange("p o t -> p (o t)")
                x = V.e.scalar_tensor_tensor(xk, p.ps[:, 2 + j, 0:TC], p.mod1[:, l, 1, bass.ds(i * 2 + (16 + j), 1)],
                                             xk, ALU.mult, ALU.add)
            x.then_inc(p.freed[j], 1)

        mods = ([mod2(1, 1, lambda i: i + 12)] if l == 0 else
                [mod2(1, 0, lambda i: i + 16), mod2(1, 1, lambda i: i + 20)])
        p.linear(8, KT, w_out, both if update_ctx else only_x, mixed, lambda i, j, use: None, residual,
                 then_k=KT if l == 0 else None, mod=mods)
        x_ready, free = [*p.banks_read], [*p.banks_read, p.mod_last, p.product_done, *mixed]
    return x_ready


def load_tables(p, l, ready):
    if l == 0:
        p.tables_in = p.nc.alloc_semaphore("tables_landed")
    p.dft_x = p.place(f"dft_x{l}", [P, 2, 4, TX], at=p.lower)
    p.dft_ctx = p.place(f"dft_ctx{l}", [P, 2, 2, TC], at=p.lower + 16384)
    p.inv_count = p.place(f"inv_count{l}", [P, 2, TA], at=p.lower + 20480)
    p.S.wait(*ready)
    p.S.e.dma_start(p.dft_x[:, :, :, :], p.dram["dft_x"]).then_inc(p.tables_in, 16)
    p.S.e.dma_start(p.dft_ctx[:, :, :, :], p.dram["dft_ctx"]).then_inc(p.tables_in, 16)
    p.S.e.dma_start(p.inv_count[:, :, :], p.dram["inv_count"]).then_inc(p.tables_in, 16)
    p.tables_ready = (p.tables_in, 48 * (l + 1))
    p.scratch = p.lower + 26624


def flat(ap):
    return ap.rearrange("p o t -> p (o t)")


def norm_rope(p, l, proj, qk_gain, ready, gains_ready):
    T, V, A, base = p.T, p.V, p.A, p.scratch
    sq = [p.place(f"qk_sq{l}{j}", [P, TA], at=base + j * 3072) for j in (0, 1)]
    rs = [p.place(f"qk_rs{l}{j}", [P, TA], at=base + 6144 + j * 3072) for j in (0, 1)]
    t1 = [p.place(f"qk_t1{l}{j}", [P, TX], at=base + 12288 + j * 2048) for j in (0, 1)]
    t2 = [p.place(f"qk_t2{l}{j}", [P, TX], at=base + 16384 + j * 2048) for j in (0, 1)]
    for e in (A, V, T):
        e.wait(*ready, gains_ready)
    with passes(p.nc, 4, {T: 4, V: 10, A: 4}) as i:
        start = [T.now(), V.now(), A.now()]
        for e in (A, V, T):
            e.wait(*start)
        tile = [flat(proj[:, bass.ds(i * 2 + (TILE_Q + j), 1), :]) for j in (0, 1)]
        tile_x = [flat(proj[:, bass.ds(i * 2 + (TILE_Q + j), 1), X_]) for j in (0, 1)]
        squared, summed, rooted, normed, turned = [], [], [], [], []
        for j in (0, 1):
            squared.append(A.did(A.e.activation(sq[j][:, :], tile[j], ACT.Square)))
        for j in (0, 1):
            T.wait(squared[j])
            T.e.matmul(p.ps[:, 3 * j, :], p.ones_half, sq[j][:, 0:TX], start=True, stop=True)
            summed.append(T.did(T.e.matmul(p.ps[:, 3 * j + 1, 0:TC], p.ones_half, sq[j][:, TX:TA],
                                           start=True, stop=True)))
        for j in (0, 1):
            A.wait(summed[j])
            rooted.append(A.did(A.e.activation(rs[j][:, :], p.banks(3 * j, TA), ACT.Sqrt, bias=p.eps[:, 0:1],
                                               scale=1.0 / QK)))
        for j in (0, 1):
            V.wait(rooted[j])
            r = V.did(V.e.reciprocal(rs[j][:, :], rs[j][:, :]))
            V.wait(r)
            normed.append(V.did(V.e.scalar_tensor_tensor(tile[j], tile[j], qk_gain[:, l, bass.ds(i * 2 + j, 1)],
                                                         rs[j][:, :], ALU.mult, ALU.mult)))
            T.wait(normed[j])
            turned.append(T.did(T.e.matmul(p.ps[:, 3 * j + 2, :], p.rot_axial, tile_x[j], start=True, stop=True)))
        for j in (0, 1):
            V.wait(normed[j])
            a = V.did(V.e.tensor_tensor(t1[j][:, :], tile_x[j], p.rope[:, 0, :], ALU.mult))
            V.wait(turned[j])
            b = V.did(V.e.tensor_tensor(t2[j][:, :], p.ps[:, 3 * j + 2, :], p.rope[:, 1, :], ALU.mult))
            V.wait(a, b)
            V.did(V.e.tensor_tensor(tile_x[j], t1[j][:, :], t2[j][:, :], ALU.add))
    return [V.now(), A.now(), T.now()]


def fourier(p, l, proj, wblk, t, ready, groups_ready):
    T, A, base = p.T, p.A, p.scratch
    tok = p.place(f"f_tok{l}", [P, TA // P, 2, P], at=base)
    bx = p.place(f"f_bx{l}", [P, 2, 2, TX], at=base + 6144)
    cw = p.place(f"f_cw{l}", [P, 2, 2, P], at=base + 14336)
    T.wait(groups_ready, *ready)
    A.wait(*ready)
    for g in range(2):
        for s, m in enumerate((p.dft_c, p.dft_ns)):
            last = T.e.matmul(p.ps[:, 6, (2 * g + s) * P:(2 * g + s + 1) * P], m, wblk[:, l, 1, g, :],
                              start=True, stop=True)
    A.wait(T.did(last))
    folded = A.did(A.e.activation(cw[:, :, :, :].rearrange("p g s n -> p (g s n)"), p.ps[:, 6, :], ACT.Copy))
    copied = []
    for g in range(2):
        for q in range(t // P):
            last = T.e.transpose(p.banks(2 * g, t)[:, q * P:(q + 1) * P],
                                 proj[:, TILE_A + g, q * P:(q + 1) * P], p.ident)
        A.wait(T.did(last))
        copied.append(A.did(A.e.activation(tok[:, 0:t // P, g, :],
                                           p.banks(2 * g, t).rearrange("p (q n) -> p q n", n=P), ACT.Copy)))
    T.wait(*copied, folded, p.tables_ready)
    for first, length, tab in ((0, TX, p.dft_x), (TX, TC, p.dft_ctx)):
        if first >= t:
            continue
        T.wait(A.now())
        moved = []
        for g in range(2):
            for s in range(2):
                for q in range(length // P):
                    last = T.e.matmul(p.ps[:, 2 * g + s, 0:length], tok[:, first // P + q, g, :], tab[:, s, q, :],
                                      start=(q == 0), stop=(q == length // P - 1))
                A.wait(T.did(last))
                moved.append(A.did(A.e.activation(bx[:, g, s, 0:length], p.ps[:, 2 * g + s, 0:length], ACT.Copy)))
        T.wait(*moved)
        for g in range(2):
            for s in range(2):
                last = T.e.matmul(p.ps[:, 4 + g, 0:length], cw[:, g, s, :], bx[:, g, s, 0:length],
                                  start=(s == 0), stop=(s == 1))
            A.wait(T.did(last))
            A.did(A.e.activation(proj[:, TILE_A + g, first:first + length], p.ps[:, 4 + g, 0:length], ACT.Copy))
    return [T.now(), A.now()]


def pooling(p, l, proj, wblk, t, ready):
    T, V, A, base = p.T, p.V, p.A, p.scratch
    edge, width = 16, TX + 32
    pad = p.place(f"pool_pad{l}", [P, 3, width], at=base)
    mean = p.place(f"pool_mean{l}", [P, TX], at=base + 12 * width)
    V.wait(*ready, p.tables_ready)
    free = [A.now()]
    low, high, whole = slice(0, 64), slice(64, P), slice(0, P)
    for first, length in ((0, TX), (TX, TC)):
        if first >= t:
            continue
        V.wait(*free)
        zero = V.did(V.e.memset(pad[:, :, :].rearrange("p a w -> p (a w)"), 0.0))
        for g in range(2):
            V.wait(zero, *free)
            c = V.did(V.e.tensor_copy(pad[:, 0, edge:edge + length], proj[:, TILE_B + g, first:first + length]))
            plan = [(1, 0, -1, 0, 7, whole), (2, 1, -1, 1, 6, high if g == 0 else whole)]
            if g == 1:
                plan += [(1, 2, -2, 2, 4, whole), (2, 1, -4, 4, 0, high)]
            for dst, src, d0, d1, reach, rows in plan:
                a, b = edge - reach, edge + length + reach
                V.wait(c)
                c = V.did(V.e.tensor_tensor(pad[rows, dst, a:b], pad[rows, src, a + d0:b + d0],
                                            pad[rows, src, a + d1:b + d1], ALU.add))
            done = []
            for rows, src in ((low, 1), (high, 2)):
                V.wait(c)
                k = V.did(V.e.tensor_tensor(mean[rows, 0:length], pad[rows, src, edge:edge + length],
                                            p.inv_count[rows, g, first:first + length], ALU.mult))
                V.wait(k)
                done.append(V.did(V.e.tensor_tensor(mean[rows, 0:length], mean[rows, 0:length],
                                                    pad[rows, 0, edge:edge + length], ALU.subtract)))
            T.wait(*done)
            mm = T.did(T.e.matmul(p.ps[:, 6 + g, 0:length], wblk[:, l, 0, g, :], mean[:, 0:length],
                                  start=True, stop=True))
            A.wait(mm, *done)
            A.did(A.e.activation(proj[:, TILE_B + g, first:first + length], p.ps[:, 6 + g, 0:length], ACT.Copy,
                                 scale=p.column("pool_scale", 2 * l + g)))
            free = [A.now(), *done]
    return [V.now(), A.now(), T.now()]


def attention(p, l, proj, neg_lam, t, ready):
    T, V, A, G, base = p.T, p.V, p.A, p.G, p.lower
    qs = p.place(f"a_q{l}", [P, TA], at=base)
    vt = p.place(f"a_vt{l}", [P, TA], at=base + 3072)
    v = p.place(f"a_v{l}", [P, TA // P, P], at=base + 6144)
    prob = [[p.place(f"a_p{l}{b}{m}", [P, TA], at=base + 9216 + (2 * b + m) * 3072) for m in (0, 1)] for b in (0, 1)]
    pt = p.place(f"a_pt{l}", [P, TA // P, TA], at=base + 21504)
    st = p.place(f"a_stat{l}", [P, 2, 8], at=base + 21504 + 18432)
    ks = p.place(f"a_k{l}", [P, TA], at=base + 21504 + 18432 + 64)
    queries = t // P
    for e in (T, V, A, G):
        e.wait(*ready)
    n = queries
    outs = 1 if t == TX else 2
    with passes(p.nc, HEADS, {T: 1 + 3 * n + outs, V: 7 * n, A: 2 + 3 * n + outs, G: 2}) as i:
        start = [T.now(), V.now(), A.now(), G.now()]
        for e in (T, V, A, G):
            e.wait(*start)
        q_in = A.did(A.e.activation(qs[:, 0:t], flat(proj[:, bass.ds(i + TILE_Q, 1), 0:t]), ACT.Copy))
        v_in = G.did(G.e.tensor_copy(vt[:, :], flat(proj[:, bass.ds(i + TILE_V, 1), :])))
        k_in = G.did(G.e.tensor_copy(ks[:, :], flat(proj[:, bass.ds(i + TILE_K, 1), :])))
        T.wait(v_in)
        for k in range(TA // P):
            last = T.e.transpose(p.banks(6, TA)[:, k * P:(k + 1) * P], vt[:, k * P:(k + 1) * P], p.ident)
        A.wait(T.did(last))
        v_ready = A.did(A.e.activation(v[:, :, :].rearrange("p k n -> p (k n)"), p.banks(6, TA), ACT.Copy))
        T.wait(q_in, k_in)
        soft, turned, exps, moved = {}, {}, {}, {}

        def keys(q):
            return (0, TA) if q < TX // P else (TX, TC)

        def scores(q):
            first, count = keys(q)
            for m in (0, 1):
                rows = slice(QK * m, QK * m + QK)
                if q:
                    T.wait(exps[q - 1][m])
                for b in range(0, count, 512):
                    w = min(512, count - b)
                    last = T.e.matmul(p.ps[:, 2 * m + b // 512, 0:w], qs[rows, q * P:(q + 1) * P],
                                      ks[rows, first + b:first + b + w], start=True, stop=True)
                soft[q, m] = T.did(last)

        def softmax(q):
            first, count = keys(q)
            s, b = st[:, q % 2, :], q % 2
            exps[q] = []
            if q >= 2:
                V.wait(turned[q - 2])
                A.wait(turned[q - 2])
            for m in (0, 1):
                V.wait(soft[q, m])
                mx = V.did(V.e.tensor_reduce(s[:, m:m + 1], p.banks(2 * m, count), AX, ALU.max))
                V.wait(mx)
                neg = V.did(V.e.tensor_scalar(s[:, 2 + m:3 + m], s[:, m:m + 1], -QK ** -0.5, None, ALU.mult))
                A.wait(neg)
                exps[q].append(A.did(A.e.activation(prob[b][m][:, 0:count], p.banks(2 * m, count), ACT.Exp,
                                                    bias=s[:, 2 + m:3 + m], scale=QK ** -0.5,
                                                    accum_out=s[:, 4 + m:5 + m])))
            V.wait(*exps[q])
            r = V.did(V.e.reciprocal(s[:, 6:8], s[:, 4:6]))
            V.wait(r)
            a = V.did(V.e.tensor_scalar(prob[b][1][:, 0:count], prob[b][1][:, 0:count], s[:, 7:8],
                                        neg_lam[:, l:l + 1], ALU.mult, ALU.mult))
            V.wait(a)
            c = V.did(V.e.scalar_tensor_tensor(prob[b][0][:, 0:count], prob[b][0][:, 0:count], s[:, 6:7],
                                               prob[b][1][:, 0:count], ALU.mult, ALU.add))
            return c

        def transposed(q, ready_p):
            first, count = keys(q)
            b = q % 2
            T.wait(ready_p)
            if q:
                T.wait(moved[q - 1])
            else:
                T.wait(v_ready)
            for k in range(count // P):
                last = T.e.transpose(p.banks(4, count)[:, k * P:(k + 1) * P], prob[b][0][:, k * P:(k + 1) * P], p.ident)
            turned[q] = T.did(last)
            A.wait(turned[q])
            k0 = first // P
            moved[q] = A.did(A.e.activation(pt[:, k0:k0 + count // P, q * P:(q + 1) * P],
                                            p.banks(4, count).rearrange("p (k n) -> p k n", n=P), ACT.Copy))

        scores(0)
        for q in range(queries):
            c = softmax(q)
            if q + 1 < queries:
                scores(q + 1)
            transposed(q, c)
        for out, (first, count, k0) in enumerate(((0, TX, 0), (TX, TC, TX // P))[:outs]):
            T.wait(moved[(first + count) // P - 1])
            for k in range(k0, TA // P):
                last = T.e.matmul(p.ps[:, 6 + out, 0:count], v[:, k, :], pt[:, k, first:first + count],
                                  start=(k == k0), stop=(k == TA // P - 1))
            A.wait(T.did(last))
            A.did(A.e.activation(flat(proj[:, bass.ds(i + TILE_Q, 1), first:first + count]),
                                 p.ps[:, 6 + out, 0:count], ACT.Copy))
    return [V.now(), A.now(), T.now(), G.now()]


def mix(p, l, proj, sub_gain, t, ready):
    T, V, A, G, base = p.T, p.V, p.A, p.G, p.mix_scratch
    sq = [p.place(f"m_sq{l}{b}", [P, TA], at=base + 3072 * b) for b in (0, 1)]
    rs = [p.place(f"m_rs{l}{b}", [P, TA], at=base + 6144 + 3072 * b) for b in (0, 1)]
    for e in (T, V, A, G):
        e.wait(*ready)
    rescaled = []
    for h in range(HEADS):
        b, o = h % 2, proj[:, TILE_Q + h, 0:t]
        if h >= 2:
            A.wait(rescaled[h - 2])
        a = A.did(A.e.activation(sq[b][:, 0:t], o, ACT.Square))
        T.wait(a)
        for c in range(0, t, 512):
            w = min(512, t - c)
            last = T.e.matmul(p.ps[:, 2 * b + c // 512, 0:w], p.ones, sq[b][:, c:c + w], start=True, stop=True)
        A.wait(T.did(last))
        r = A.did(A.e.activation(rs[b][:, 0:t], p.banks(2 * b, t), ACT.Sqrt, bias=p.eps[:, 0:1], scale=1.0 / P))
        V.wait(r)
        r = V.did(V.e.reciprocal(rs[b][:, 0:t], rs[b][:, 0:t]))
        V.wait(r)
        rescaled.append(V.did(V.e.scalar_tensor_tensor(o, o, sub_gain[:, l:l + 1], rs[b][:, 0:t], ALU.mult, ALU.mult)))
    for k, tile in enumerate([TILE_A, TILE_A + 1, TILE_B, TILE_B + 1] + [TILE_Q + h for h in range(HEADS)]):
        y = proj[:, tile, 0:t]
        V.wait(V.now())
        m = V.did(V.e.tensor_tensor(y, y, proj[:, TILE_G + k, 0:t], ALU.mult))
        last = p.split_pair(k, slice(0, t), y, [m])
    return [last, A.now(), V.now()]


RQ, RK, RV, RG, HQ, HF, HI, HG = range(0, 32, 4)
SH1, SC1, G1, SH2, SC2, G2 = range(0, 48, 8)


def second_block(p):
    nc, T, V, A, G, S = p.nc, p.T, p.V, p.A, p.G, p.S
    p.place_ring("second", SLOT)
    rope = p.place("rope_half", [P, 2, TX])
    decay = p.place("decay", [P, HEADS, TX])
    masks = p.place("level_masks", [P, 8, P], I32)
    vec = p.place("layer_vectors", [P, 176])
    bounds = p.place("lower_bounds", [P, 2, HEADS])
    proj = p.place("proj_second", [P, 32, TX])
    room = p.top - 32 * TX * 4
    p.norm_buffers = ([p.place(f"n2sq{b}", [P, TX], at=room + b * 2048) for b in (0, 1)],
                      p.place("n2rstd", [P, TX], at=room + 4096),
                      [p.place(f"n2tmp{b}", [P, TX], at=room + 6144 + b * 2048) for b in (0, 1)],
                      [p.place(f"n2h{b}", [P, TX], at=room + 10240 + b * 2048) for b in (0, 1)])
    act_hi = p.place("act_hi", [P, FFH, TX], F32R, at=room)
    act_lo = p.place("act_lo", [P, FFH, TX], F32R, at=room + FFH * 2048)
    conv = p.place("conv", [P, TX], at=room + 2 * FFH * 2048)
    actf = p.place("act_value", [P, TX], at=room + 2 * FFH * 2048 + 2048)
    conv_linear = nc.alloc_semaphore("conv_linear")
    conv_silu = nc.alloc_semaphore("conv_silu")
    tables_in = nc.alloc_semaphore("second_tables_landed")
    for dst, name in ((rope, "rope_half"), (decay, "decay"), (masks, "level_masks")):
        S.e.dma_start(dst[:, :, :], p.dram[name]).then_inc(tables_in, 16)

    lg, e = p.column("hgrn_lb_logits_2", 0, 8), p.small[:, 16:24]
    mx, tot = p.small[:, 24:28], p.small[:, 28:32]
    t = V.did(V.e.tensor_tensor(mx, lg[:, 0:4], lg[:, 4:8], ALU.max))
    for l in range(2):
        V.wait(t)
        V.did(V.e.tensor_tensor(e[:, 4 * l:4 * l + 4], lg[:, 4 * l:4 * l + 4], mx, ALU.subtract))
    A.wait(V.now())
    t = A.did(A.e.activation(e, e, ACT.Exp))
    V.wait(t)
    t = V.did(V.e.tensor_tensor(tot, e[:, 0:4], e[:, 4:8], ALU.add))
    V.wait(t)
    t = V.did(V.e.reciprocal(tot, tot))
    V.wait(t)
    for l in range(2):
        V.did(V.e.tensor_tensor(e[:, 4 * l:4 * l + 4], e[:, 4 * l:4 * l + 4], tot, ALU.mult))
    V.wait(V.now())
    t = V.did(V.e.tensor_tensor(mx, e[:, 0:4], e[:, 4:8], ALU.add))
    V.did(V.e.tensor_tensor(bounds[:, 0, :], e[:, 0:4], e[:, 0:4], ALU.subtract))
    V.wait(t)
    V.did(V.e.tensor_tensor(bounds[:, 1, :], mx, e[:, 0:4], ALU.subtract))
    for en in (V, A, T, G, S):
        en.wait(V.now(), (tables_in, 48))

    layer_sems = [x.sem for x in (T, V, A, G)] + [A.hold, S.hold, conv_linear, conv_silu,
                  *p.landed, *p.rounded, *p.split, *p.used, *p.freed]

    def new_layer():
        nc.all_engine_barrier()
        for s in layer_sems:
            G.e.sem_clear(s)
        nc.all_engine_barrier()

    new_layer()
    with nc.Fori(0, 2) as l:
        for en in (T, V, A, G):
            en.e.sem_inc(en.sem, 1)
            en.n = 1
        p.grant_slots(V)
        fields, at = {}, 0
        def take(name, src, n):
            nonlocal at
            fields[name] = vec[:, at:at + n]
            V.did(V.e.tensor_copy(vec[:, at:at + n], src))
            at += n
        c = p.col
        take("mod", p.mod2[:, bass.ds(l * 48, 48)], 48)
        take("norm1", p.colsf[:, bass.ds(l * 8 + c["norm1_w_2"], 8)], 8)
        take("norm2", p.colsf[:, bass.ds(l * 8 + c["norm2_w_2"], 8)], 8)
        take("head_gain_r", p.colsf[:, bass.ds(l * 4 + c["ret_norm_w_2"], 4)], 4)
        take("head_gain_h", p.colsf[:, bass.ds(l * 4 + c["hgrn_norm_w_2"], 4)], 4)
        take("conv_b", p.colsf[:, bass.ds(l * 22 + c["conv_b_2"], 22)], 22)
        take("conv_w", p.colsf[:, bass.ds(l * (c["conv_w1"] - c["conv_w0"]) + c["conv_w0"], 66)], 66)
        take("lb", bounds[:, bass.ds(l, 1), :].rearrange("p o h -> p (o h)"), 4)
        V.wait(V.now())
        gains = p.small[:, 32:48]
        keep = p.small[:, 48:52]
        mod = fields["mod"]
        V.did(V.e.scalar_tensor_tensor(gains[:, 0:8], mod[:, SC1:SC1 + 8], 1.0, fields["norm1"], ALU.add, ALU.mult))
        V.did(V.e.scalar_tensor_tensor(gains[:, 8:16], mod[:, SC2:SC2 + 8], 1.0, fields["norm2"], ALU.add, ALU.mult))
        vectors = V.did(V.e.tensor_scalar(keep, fields["lb"], -1.0, 1.0, ALU.mult, ALU.add))

        def columns_of(name, first):
            def source(i, j):
                return p.dram[name].rearrange("l (k p) n -> p l k n", p=P)[
                    :, bass.ds(l, 1), :, bass.ds(i * (2 * P) + (first + j) * P, P)].rearrange("p o k n -> p (o k) n")
            return source

        p.prime(KT)
        V.wait(vectors); A.wait(vectors)
        h_ready = p.norm("m", TX, [vectors], [(0, TX, gains[:, 0:8], mod[:, SH1:SH1 + 8])], [])
        only_x = [(0, 0, TX)]

        def to_proj(first, func):
            def evac(i, j, use):
                A.wait((p.used[j], use))
                A.e.activation(flat(proj[:, bass.ds(i * 2 + (first + j), 1), :]), p.ps[:, j, :],
                               func).then_inc(p.freed[j], 1)
            return evac

        for first, n, func in ((0, 12, ACT.Identity), (12, 8, ACT.Silu), (20, 8, ACT.Identity), (28, 4, ACT.Silu)):
            p.linear(n, KT, columns_of("w_in_2", first), only_x, h_ready if first == 0 else [],
                     to_proj(first, func), then_k=KT)
        projected = [*p.banks_read, p.product_done]
        retention_done = retention(p, proj, rope, decay, projected)
        hgrn_done = hgrn(p, proj, masks, fields["lb"], keep, retention_done)
        mixed = mix_heads(p, proj, fields, hgrn_done)

        def residual(gate):
            def evac(i, j, use):
                V.wait((p.used[j], use))
                xk = flat(p.xT[:, bass.ds(i * 2 + j, 1), X_])
                V.e.scalar_tensor_tensor(xk, p.ps[:, j, :], vec[:, bass.ds(i * 2 + (gate + j), 1)], xk,
                                         ALU.mult, ALU.add).then_inc(p.freed[j], 1)
            return evac

        p.linear(8, KT, columns_of("w_out_2", 0), only_x, mixed, lambda i, j, use: None, residual(G1), then_k=KT)

        h_ready = p.norm("f", TX, [*p.banks_read], [(0, TX, gains[:, 8:16], mod[:, SH2:SH2 + 8])],
                         [*p.banks_read, p.product_done, *mixed])
        for half in range(2):
            u, done0 = p.uses, half * FFH
            act_free = [p.product_done]

            def gate_val(i, j, half=half):
                name = ("w_gate_2", "w_val_2")[j]
                return p.dram[name].rearrange("l (k p) n -> p l k n", p=P)[
                    :, bass.ds(l, 1), :, bass.ds(i * P + half * FFH * P, P)].rearrange("p o k n -> p (o k) n")

            def conv_col(i, k, half=half):
                at_ = k * 22 + half * FFH
                base = 48 + 8 + 8 + 4 + 4 + 22
                return vec[:, bass.ds(i + (base + at_), 1)]

            def bias_col(i, half=half):
                return vec[:, bass.ds(i + (48 + 8 + 8 + 4 + 4 + half * FFH), 1)]

            def act_side(i, j, use, u=u):
                if j == 0:
                    A.wait((p.used[0], use), (p.freed[1], use - 1))
                    A.e.activation(conv[:, :], p.ps[:, 0, :], ACT.Identity, bias=bias_col(i),
                                   scale=conv_col(i, 2)).then_inc(conv_linear, 1)
                else:
                    A.wait((p.freed[0], use))
                    A.e.activation(conv[:, :], conv[:, :], ACT.Silu).then_inc(conv_silu, 1)

            def vec_side(i, j, use, done0=done0):
                if j == 0:
                    V.wait((conv_linear, i + (done0 + 1)))
                    t = V.did(V.e.scalar_tensor_tensor(conv[:, 1:TX], p.ps[:, 0, 0:TX - 1], conv_col(i, 1),
                                                       conv[:, 1:TX], ALU.mult, ALU.add))
                    V.wait(t)
                    V.e.scalar_tensor_tensor(conv[:, 2:TX], p.ps[:, 0, 0:TX - 2], conv_col(i, 0), conv[:, 2:TX],
                                             ALU.mult, ALU.add).then_inc(p.freed[0], 1)
                else:
                    V.wait((conv_silu, i + (done0 + 1)), (p.used[1], use))
                    V.e.tensor_tensor(actf[:, :], conv[:, :], p.ps[:, 1, :], ALU.mult).then_inc(p.freed[1], 1)
                    V.wait((p.freed[1], use))
                    hi_t, lo_t = (flat(x[:, bass.ds(i, 1), :]) for x in (act_hi, act_lo))
                    t = V.did(V.e.tensor_copy(hi_t, actf[:, :]))
                    V.wait(t)
                    V.wait(V.did(V.e.tensor_tensor(lo_t, actf[:, :], hi_t.bitcast(F32), ALU.subtract)))

            V.wait(*act_free, *(h_ready if half == 0 else []))
            A.wait(*(h_ready if half == 0 else []))
            p.linear(2 * FFH, KT, gate_val, only_x, h_ready, act_side, vec_side, vec_counts=3, then_k=FFH)
            act_ready = [V.now()]

            def down(i, j, half=half):
                return p.dram["w_down_2"].rearrange("l (k p) n -> p l k n", p=P)[
                    :, bass.ds(l, 1), half * FFH:(half + 1) * FFH, bass.ds(i * (2 * P) + j * P, P)].rearrange(
                    "p o k n -> p (o k) n")

            p.act_pair = (act_hi, act_lo)
            p.linear(8, FFH, down, only_x, act_ready, lambda i, j, use: None, residual(G2),
                     then_k=KT if half == 0 else None)
            p.act_pair = None
        for en in (T, V, A, G, S):
            en.wait(*p.banks_read, p.product_done)
        new_layer()
    for en in (T, V, A, G):
        en.e.sem_inc(en.sem, 1)
        en.n = 1
    final_norm(p, proj)


def retention(p, proj, rope, decay, ready):
    T, V, A, G, base = p.T, p.V, p.A, p.G, p.lower
    q = [p.place(f"r_{n}", [P, TX], at=base + 2048 * k) for k, n in enumerate(("q", "k"))]
    t2 = [p.place(f"r_t{k}", [P, TX], at=base + 4096 + 2048 * k) for k in range(2)]
    vt = p.place("r_vt", [P, TX], at=base + 8192)
    v = p.place("r_v", [P, 4, P], at=base + 10240)
    st = p.place("r_st", [P, 4, TX], at=base + 12288)
    for e in (T, V, A, G):
        e.wait(*ready)
    with passes(p.nc, HEADS, {T: 8, V: 10, A: 2, G: 1}) as i:
        start = [T.now(), V.now(), A.now(), G.now()]
        for e in (T, V, A, G):
            e.wait(*start)
        v_in = G.did(G.e.tensor_copy(vt[:, :], flat(proj[:, bass.ds(i + RV, 1), :])))
        rotated = []
        for k, tile in enumerate((RQ, RK)):
            x = flat(proj[:, bass.ds(i + tile, 1), :])
            turned = T.did(T.e.matmul(p.ps[:, 5 + k, :], p.rot_half, x, start=True, stop=True))
            a = V.did(V.e.tensor_tensor(q[k][:, :], x, rope[:, 0, :], ALU.mult))
            V.wait(turned)
            b = V.did(V.e.tensor_tensor(t2[k][:, :], p.ps[:, 5 + k, :], rope[:, 1, :], ALU.mult))
            V.wait(a, b)
            rotated.append(V.did(V.e.tensor_tensor(q[k][:, :], q[k][:, :], t2[k][:, :], ALU.add)))
        T.wait(v_in)
        for k in range(4):
            last = T.e.transpose(p.ps[:, 7, k * P:(k + 1) * P], vt[:, k * P:(k + 1) * P], p.ident)
        A.wait(T.did(last))
        v_ready = A.did(A.e.activation(v[:, :, :].rearrange("p k n -> p (k n)"), p.ps[:, 7, :], ACT.Copy))
        T.wait(*rotated)
        decayed = []
        for j in range(4):
            w = TX - j * P
            s = T.did(T.e.matmul(p.ps[:, j, 0:w], q[1][:, j * P:(j + 1) * P], q[0][:, j * P:TX], start=True, stop=True))
            V.wait(s)
            decayed.append(V.did(V.e.tensor_tensor(st[:, j, 0:w], p.ps[:, j, 0:w],
                                                   decay[:, bass.ds(i, 1), 0:w].rearrange("p o t -> p (o t)"),
                                                   ALU.mult)))
        T.wait(v_ready)
        for j in range(4):
            T.wait(decayed[j])
            last = T.e.matmul(p.ps[:, 4, j * P:TX], v[:, j, :], st[:, j, 0:TX - j * P], start=(j == 0), stop=(j == 3))
        A.wait(T.did(last))
        A.did(A.e.activation(flat(proj[:, bass.ds(i + RQ, 1), :]), p.ps[:, 4, :], ACT.Copy))
    return [T.now(), V.now(), A.now(), G.now()]


def hgrn(p, proj, masks, lb, keep, ready):
    T, V, A, G, base = p.T, p.V, p.A, p.G, p.lower
    N = HEADS * TX
    names = ("fwd", "bwd", "key", "q_level", "k_level")
    fwd, bwd, key, ql, kl = (p.place(f"h_{n}", [P, N], at=base + 8192 * k) for k, n in enumerate(names))
    diag = p.place("h_diag", [P, N], at=base + 8192 * 5)
    z = proj[:, HF:HF + 4, :].rearrange("p h t -> p (h t)")
    q = proj[:, HQ:HQ + 4, :].rearrange("p h t -> p (h t)")
    room = proj[:, RK:RK + 8, :].rearrange("p h t -> p (h t)")
    v = room[:, 0:N].rearrange("p (h k n) -> p h k n", h=4, k=4)
    near = room[:, N:2 * N]
    far = z
    for e in (T, V, A, G):
        e.wait(*ready)
    copied = []
    for h in range(HEADS):
        for k in range(4):
            last = T.e.transpose(p.ps[:, 4 + h, k * P:(k + 1) * P], proj[:, HI + h, k * P:(k + 1) * P], p.ident)
        t_ = T.did(last)
        A.wait(t_)
        copied.append(A.did(A.e.activation(v[:, h, :, :].rearrange("p k n -> p (k n)"), p.ps[:, 4 + h, :], ACT.Copy)))
    sp = A.did(A.e.activation(fwd[:, :], z, ACT.Sigmoid))
    sn = A.did(A.e.activation(kl[:, :], z, ACT.Sigmoid, scale=-1.0))
    V.wait(sp, sn)
    ones = V.did(V.e.memset(bwd[:, :], 1.0))
    for h in range(HEADS):
        cut = slice(h * TX, (h + 1) * TX)
        V.did(V.e.scalar_tensor_tensor(fwd[:, cut], kl[:, cut], lb[:, h:h + 1], fwd[:, cut], ALU.mult, ALU.add))
        last_key = V.did(V.e.tensor_scalar(key[:, cut], kl[:, cut], keep[:, h:h + 1], None, ALU.mult))
    zero = V.did(V.e.memset(diag[:, :], 0.0))
    read, scored = [last_key], []
    T.wait(*copied, last_key)
    taken = {}
    for level in range(len(LEVELS) + 1):
        set_ = 4 * (level % 2)
        if level == 0:
            rhs, lhs = q, key[:, :]
        else:
            V.wait(V.now(), *scored)
            a = V.did(V.e.tensor_tensor(ql[:, :], q, fwd[:, :], ALU.mult))
            G.wait(V.now(), *scored)
            b = G.did(G.e.tensor_tensor(kl[:, :], key[:, :], bwd[:, :], ALU.mult))
            T.wait(a, b)
            rhs, lhs = ql[:, :], kl[:, :]
            half = LEVELS[level - 1]
            fb, bb = (x[:, :].rearrange("p (b t) -> p b t", t=2 * half) for x in (fwd, bwd))
            shape = [P, N // (2 * half), half]
            V.wait(a, b)
            w = V.did(V.e.tensor_tensor(bb[:, :, 0:half], bb[:, :, 0:half],
                                        fb[:, :, 2 * half - 1:2 * half].broadcast_to(shape), ALU.mult))
            V.wait(w)
            V.did(V.e.tensor_tensor(fb[:, :, half:2 * half], fb[:, :, half:2 * half],
                                    fb[:, :, half - 1:half].broadcast_to(shape), ALU.mult))
        if level >= 2:
            T.wait(taken[level - 2])
        for c in range(16):
            last = T.e.matmul(p.ps[:, set_ + c // 4, (c % 4) * P:(c % 4 + 1) * P], lhs[:, c * P:(c + 1) * P],
                              rhs[:, c * P:(c + 1) * P], start=True, stop=True)
        scored = [T.did(last)]
        V.wait(*scored, zero, V.now())
        taken[level] = V.did(V.e.copy_predicated(
            diag[:, :].rearrange("p (c n) -> p c n", n=P),
            masks[:, level:level + 1, :].broadcast_to([P, 16, P]),
            p.banks(set_, N).rearrange("p (c n) -> p c n", n=P)))
    V.wait(V.now(), *scored)
    a = V.did(V.e.tensor_tensor(ql[:, :], q, fwd[:, :], ALU.mult))
    G.wait(V.now(), *scored)
    b = G.did(G.e.tensor_tensor(kl[:, :], key[:, :], bwd[:, :], ALU.mult))
    T.wait(a, b, taken[6])
    for h in range(HEADS):
        for c in range(2):
            at = (4 * h + 2 * c) * P
            last = T.e.matmul(p.ps[:, h // 2, ((h % 2) * 2 + c) * P:((h % 2) * 2 + c + 1) * P], kl[:, at:at + P],
                              ql[:, at + P:at + 2 * P], start=True, stop=True)
    near_scored = T.did(last)
    A.wait(near_scored)
    near_in = A.did(A.e.activation(near[:, 0:1024], p.banks(0, 1024), ACT.Copy))
    V.wait(a, b)
    fb, bb = (x[:, :].rearrange("p (b t) -> p b t", t=2 * P) for x in (fwd, bwd))
    shape = [P, N // (2 * P), P]
    w = V.did(V.e.tensor_tensor(bb[:, :, 0:P], bb[:, :, 0:P], fb[:, :, 2 * P - 1:2 * P].broadcast_to(shape), ALU.mult))
    V.wait(w)
    w = V.did(V.e.tensor_tensor(fb[:, :, P:2 * P], fb[:, :, P:2 * P], fb[:, :, P - 1:P].broadcast_to(shape), ALU.mult))
    V.wait(w, near_scored)
    a = V.did(V.e.tensor_tensor(ql[:, :], q, fwd[:, :], ALU.mult))
    G.wait(w, near_scored)
    b = G.did(G.e.tensor_tensor(kl[:, :], key[:, :], bwd[:, :], ALU.mult))
    T.wait(a, b, taken[7], near_in)
    for h in range(HEADS):
        for c in range(2):
            at = 4 * h * P
            last = T.e.matmul(p.ps[:, 4 + h, c * 256:(c + 1) * 256], kl[:, at + c * P:at + (c + 1) * P],
                              ql[:, at + 2 * P:at + 4 * P], start=True, stop=True)
    A.wait(T.did(last))
    far_in = A.did(A.e.activation(far, p.banks(4, N), ACT.Copy))
    T.wait(near_in, far_in, taken[7])
    sources = lambda h, tq: (
        [(k, far[:, h * TX + k * 256 + (tq - 2) * P:][:, 0:P]) for k in (0, 1)] if tq >= 2 else []) + (
        [(tq - 1, near[:, (2 * h + tq // 2) * P:][:, 0:P])] if tq % 2 else []) + [
        (tq, diag[:, (4 * h + tq) * P:][:, 0:P])]
    for h in range(HEADS):
        for tq in range(4):
            terms = sources(h, tq)
            for n, (k, s) in enumerate(terms):
                last = T.e.matmul(p.ps[:, h, tq * P:(tq + 1) * P], v[:, h, k, :], s, start=(n == 0),
                                  stop=(n == len(terms) - 1))
        A.wait(T.did(last))
        A.did(A.e.activation(proj[:, HQ + h, :], p.ps[:, h, :], ACT.Copy))
    return [T.now(), V.now(), A.now(), G.now()]


def mix_heads(p, proj, fields, ready):
    T, V, A, G = p.T, p.V, p.A, p.G
    sq = [proj[:, RK + b, :] for b in (0, 1)]
    rs = [proj[:, RK + 2 + b, :] for b in (0, 1)]
    for e in (T, V, A, G):
        e.wait(*ready)
    tiles = [(RQ + h, RG + h, fields["head_gain_r"][:, h:h + 1]) for h in range(HEADS)] + \
            [(HQ + h, HG + h, fields["head_gain_h"][:, h:h + 1]) for h in range(HEADS)]
    scaled = []
    for k, (o_t, g_t, gain) in enumerate(tiles):
        b, o = k % 2, proj[:, o_t, :]
        if k >= 2:
            A.wait(scaled[k - 2])
        T.wait(A.did(A.e.activation(sq[b], o, ACT.Square)))
        A.wait(T.did(T.e.matmul(p.ps[:, b, :], p.ones, sq[b], start=True, stop=True)))
        V.wait(A.did(A.e.activation(rs[b], p.ps[:, b, :], ACT.Sqrt, bias=p.eps[:, 0:1], scale=1.0 / P)))
        V.wait(V.did(V.e.reciprocal(rs[b], rs[b])))
        V.wait(V.did(V.e.scalar_tensor_tensor(o, o, gain, rs[b], ALU.mult, ALU.mult)))
        m = V.did(V.e.tensor_tensor(o, o, proj[:, g_t, :], ALU.mult))
        scaled.append(m)
        last = p.split_pair(k, X_, o, [m])
    return [last, A.now(), V.now()]


def final_norm(p, proj):
    T, V, A, S = p.T, p.V, p.A, p.S
    sq, rs = [proj[:, b, :] for b in (0, 1)], proj[:, 2, :]
    y = [proj[:, 3 + b, :] for b in (0, 1)]
    rows = proj[:, 8:16, :].rearrange("p a t -> p (a t)").rearrange("p (t d) -> p t d", d=D)
    done = []
    for k in range(KT):
        if k >= 2:
            A.wait(done[k - 2])
        T.wait(A.did(A.e.activation(sq[k % 2], p.xT[:, k, X_], ACT.Square)))
        done.append(T.did(T.e.matmul(p.ps[:, 0, :], p.ones, sq[k % 2], start=(k == 0), stop=(k == KT - 1))))
    A.wait(done[-1])
    V.wait(A.did(A.e.activation(rs, p.ps[:, 0, :], ACT.Sqrt, bias=p.eps[:, 0:1], scale=1.0 / D)))
    V.wait(V.did(V.e.reciprocal(rs, rs)))
    turned, copied = [], []
    for k in range(KT):
        b = k % 2
        if k >= 2:
            V.wait(turned[k - 2])
            T.wait(copied[k - 2])
        T.wait(V.did(V.e.scalar_tensor_tensor(y[b], p.xT[:, k, X_], p.column("final_norm_w_2", k), rs,
                                              ALU.mult, ALU.mult)))
        for t in range(4):
            last = T.e.transpose(p.ps[:, 2 + b, t * P:(t + 1) * P], y[b][:, t * P:(t + 1) * P], p.ident)
        turned.append(T.did(last))
        A.wait(turned[-1])
        copied.append(A.did(A.e.activation(rows[:, :, k * P:(k + 1) * P],
                                           p.ps[:, 2 + b, :].rearrange("p (t n) -> p t n", n=P), ACT.Copy)))
    S.wait(A.now())
    S.e.dma_start(p.dram["out"].rearrange("b (t p) d -> p (b t) d", p=P), rows).then_inc(p.out_stored, 16)
    S.wait((p.out_stored, 16))


def kernel(**inputs):
    import concourse.bacc as bacc
    from concourse.bass_utils import run_bass_kernel_spmd as run

    nc = bacc.Bacc("TRN2", target_bir_lowering=False, num_devices=1)
    arrays = {k: np.ascontiguousarray(v) for k, v in inputs.items()}
    arrays.update(tables())
    dram = {k: nc.dram_tensor(f"in_{k}", v.shape, mybir.dt.from_np(v.dtype), kind="ExternalInput").ap()
            for k, v in arrays.items()}
    dram["out"] = nc.dram_tensor("out", (1, TX, D), F32, kind="ExternalOutput").ap()
    p = Program(nc, dram)
    x_ready = first_block(p)
    for e in (p.T, p.V, p.A, p.G, p.S):
        e.wait(*x_ready, p.mod_last)
    second_block(p)
    r = run(nc, [{f"in_{k}": v for k, v in arrays.items()}], core_ids=[0])
    return r.results[0]["out"]
```

```python
import math
from contextlib import contextmanager

import numpy as np
import concourse.bass as bass
from concourse import mybir

F32 = mybir.dt.float32
F32R = mybir.dt.float32r
I32 = mybir.dt.int32
ALU = mybir.AluOpType
ACT = mybir.ActivationFunctionType
AX = mybir.AxisListType.X
ET = mybir.EngineType

P = 128
D = 1024
KT = D // P
TX = 512
TC = 256
TA = TX + TC
EPS = 1e-6
GRID_W = 64
QK = 64
HEADS = 4
FF = 2816
FFH = FF // P // 2
CHUNK_COLS = 256
LEVELS = (1, 2, 4, 8, 16, 32, 64)
SLOT = FFH * P


def tables():
    t = {}
    eye = np.eye(P, dtype=np.float32)
    t["ident"] = eye
    t["ones"] = np.ones((P, P), np.float32)
    half = np.kron(np.eye(2), np.ones((QK, QK)))
    t["ones_half"] = half.astype(np.float32)
    rot = np.zeros((P, P), np.float32)
    for base in range(0, P, 32):
        for i in range(16):
            rot[base + 16 + i, base + i] = -1.0
            rot[base + i, base + 16 + i] = 1.0
    t["rot_axial"] = rot
    rot = np.zeros((P, P), np.float32)
    for i in range(64):
        rot[64 + i, i] = -1.0
        rot[i, 64 + i] = 1.0
    t["rot_half"] = rot
    n = np.arange(64)
    ang = 2 * np.pi * np.outer(n, n) / 64
    t["dft_c"] = np.kron(np.eye(2), np.cos(ang) / 8).astype(np.float32)
    t["dft_ns"] = np.kron(np.eye(2), -np.sin(ang) / 8).astype(np.float32)
    square = ["ident", "ones", "ones_half", "rot_axial", "rot_half", "dft_c", "dft_ns"]
    out = {"squares": np.stack([t[k] for k in square], 1)}

    f4 = np.float32
    rows = TX // GRID_W
    row = np.repeat(np.arange(rows), GRID_W).astype(f4)
    col = np.tile(np.arange(GRID_W), rows).astype(f4)
    inv = (f4(10000.0) ** (-np.arange(0, 32, 2, dtype=f4) / f4(32))).astype(f4)
    ar, ac = row[:, None] * inv[None], col[:, None] * inv[None]
    ang = np.concatenate([ar, ar, ac, ac], -1).astype(f4)
    cs = np.stack([np.cos(ang).T, np.sin(ang).T], 1)
    out["rope_axial"] = np.concatenate([cs, cs], 0).astype(f4)

    def dft(length):
        k = np.arange(length)
        a = 2 * np.pi * (np.outer(k, k) % length) / length
        c = np.stack([np.cos(a), np.sin(a)]) / math.sqrt(length)
        return c.reshape(2, length // P, P, length).transpose(2, 0, 1, 3).astype(f4)
    out["dft_x"] = dft(TX)
    out["dft_ctx"] = dft(TC)

    def inv_counts(length):
        t_ = np.arange(length)
        r = []
        for w in (2, 4, 8, 16):
            lo, hi = w // 2, w - w // 2 - 1
            a, b = np.clip(t_ - lo, 0, length - 1), np.clip(t_ + hi, 0, length - 1)
            r.append(1.0 / (b - a + 1))
        r = np.array(r)
        return np.repeat(r.reshape(2, 2, 1, length), 64, 2).reshape(2, P, length).transpose(1, 0, 2)
    inv = (f4(10000.0) ** (-np.arange(0, P, 2, dtype=f4) / f4(P))).astype(f4)
    ang = (np.arange(TX, dtype=f4)[:, None] * inv[None]).astype(f4).T
    cs = np.stack([np.cos(ang), np.sin(ang)], 1)
    out["rope_half"] = np.concatenate([cs, cs], 0).astype(f4)
    gamma = 1.0 - 2.0 ** (-5.0 - np.arange(HEADS))
    dist = np.arange(TX)[None, :] - np.arange(P)[:, None]
    decay = np.where(dist[:, None] >= 0, gamma[None, :, None] ** np.maximum(dist[:, None], 0), 0.0)
    out["decay"] = (decay * P ** -0.5).astype(f4)
    k_, q_ = np.arange(P)[:, None], np.arange(P)[None, :]
    masks = [k_ == q_]
    for half in LEVELS:
        masks.append((k_ // (2 * half) == q_ // (2 * half)) & (k_ // half % 2 == 0) & (q_ // half % 2 == 1))
    out["level_masks"] = np.stack(masks, 1).astype(np.int32)
    out["inv_count"] = np.concatenate([inv_counts(TX), inv_counts(TC)], -1).astype(f4)
    return out


class Engine:

    def __init__(self, nc, e, kind, name, hold=False):
        self.e, self.kind, self.sem, self.n, self.pass_ = e, kind, nc.alloc_semaphore(name), 0, None
        self.hold = nc.alloc_semaphore(name + "_holds") if hold else None

    def wait(self, *tokens):
        for sem, value in tokens:
            self.e.wait_ge(sem, value)
        if self.hold and any(not isinstance(value, int) for _, value in tokens):
            self.e.sem_inc(self.hold, 1)
        return self.e

    def now(self):
        if self.pass_ is None:
            return (self.sem, self.n)
        i, per, base = self.pass_
        return (self.sem, i * per + (base + self.n))

    def did(self, instruction):
        instruction.then_inc(self.sem, 1)
        self.n += 1
        return self.now()


@contextmanager
def passes(nc, n, counts):
    with nc.Fori(0, n, engines=[e.kind for e in counts]) as i:
        for e, per in counts.items():
            e.pass_, e.n = (i, per, e.n), 0
        yield i
        for e, per in counts.items():
            assert e.n == per, (e.kind, "marks in a pass:", e.n, "declared", per)
            e.n, e.pass_ = e.pass_[2] + n * per, None


def pipeline(n, *steps):
    for turn in range(n + len(steps) - 1):
        for s in range(len(steps) - 1, -1, -1):
            if 0 <= turn - s < n:
                steps[s](turn - s)


class Program:

    def __init__(self, nc, dram):
        self.nc, self.dram = nc, dram
        self.T = Engine(nc, nc.tensor, ET.PE, "tensor_progress")
        self.V = Engine(nc, nc.vector, ET.DVE, "vector_progress")
        self.A = Engine(nc, nc.scalar, ET.Activation, "scalar_progress", hold=True)
        self.G = Engine(nc, nc.gpsimd, ET.Pool, "gpsimd_progress")
        self.S = Engine(nc, nc.sync, ET.SP, "sync_progress", hold=True)
        self.top = 16640
        sem = nc.alloc_semaphore
        self.consts_in = sem("consts_landed")
        self.x_in = sem("x_landed")
        self.out_stored = sem("out_stored")
        self.landed = [sem(f"weight_landed{j}") for j in (0, 1)]
        self.rounded = [sem(f"weight_rounded{j}") for j in (0, 1)]
        self.split = [sem(f"weight_split{j}") for j in (0, 1)]
        self.used = [sem(f"weight_used{j}") for j in (0, 1)]
        self.freed = [sem(f"bank_freed{j}") for j in (0, 1)]
        self.uses = 0
        self.mod_landed = [sem(f"mod_landed{j}") for j in (0, 1)]
        self.mod_summed = [sem(f"mod_summed{j}") for j in (0, 1)]
        self.mod_turned = [sem(f"mod_turned{j}") for j in (0, 1)]
        self.mod_uses = [0, 0]
        self.layer_sems = [*self.landed, *self.rounded, *self.split, *self.used, *self.freed]

        self.xT = self.place("xT", [P, KT, TA])
        self.lower = self.top
        self.h_hi = self.place("h_hi", [P, KT, TA], F32R)
        self.h_lo = self.place("h_lo", [P, KT, TA], F32R)
        self.squares = self.place("squares", [P, 7, P])
        (self.ident, self.ones, self.ones_half, self.rot_axial, self.rot_half,
         self.dft_c, self.dft_ns) = (self.squares[:, k, :] for k in range(7))
        self.cols = self.place("cols", [P, 5, P])
        self.colsf = self.cols[:, :, :].rearrange("p a b -> p (a b)")
        self.mod1 = self.place("mod1", [P, 2, 2, 24])
        self.mod2 = self.place("mod2", [P, 96])
        self.act_c = self.place("act_c", [P, 24])
        self.eps = self.place("eps", [P, 1])
        self.small = self.place("small", [P, 64])
        self.roots = self.place("inverse_roots", [P, 48])
        self.rope = self.place("rope", [P, 2, TX])
        self.ssq = self.place("summed_squares", [P, TA])
        self.ring_base = self.top
        self.place_ring("first", D)
        self.ps = nc.alloc_psum_tensor("ps", [P, 8, 512], F32)

    def place_ring(self, tag, floats):
        self.top = self.ring_base
        self.raw = [self.place(f"w_raw_{tag}{j}", [P, floats]) for j in (0, 1)]
        self.hi = [self.place(f"w_hi_{tag}{j}", [P, floats], F32R) for j in (0, 1)]
        self.lo = [self.place(f"w_lo_{tag}{j}", [P, floats], F32R) for j in (0, 1)]

    def place(self, name, shape, dt=F32, at=None):
        size = 4
        for s in shape[1:]:
            size *= s
        t = self.nc.alloc_sbuf_tensor_at(name, shape, dt, offset=self.top if at is None else at)
        if at is None:
            self.top += (size + 31) // 32 * 32
        return t

    def banks(self, b, n):
        return self.ps[:, :, :].rearrange("p b n -> p (b n)")[:, b * 512:b * 512 + n]

    def load_vectors(self):
        nc, d = self.nc, self.dram
        rows = self.place("vector_rows", [P, 5, P], at=self.lower)
        self.col, self.vectors_dma = {}, nc.alloc_semaphore("vectors_landed")
        plan = []
        r = 0
        def add(name, n, srcs):
            nonlocal r
            if r // P != (r + n - 1) // P:
                r = (r + P - 1) // P * P
            self.col[name] = r
            plan.append((r, n, srcs))
            r += n
        def rows_of(name, n):
            ap = d[name]
            letters = "abc"[:len(ap.shape)]
            flat = ap if len(ap.shape) == 1 else ap.rearrange(f"{' '.join(letters)} -> ({' '.join(letters)})")
            add(name, n, [(slice(0, P), flat.rearrange("(r p) -> r p", p=P))])
        rows_of("c", 8); rows_of("c_ctx", 8); rows_of("c_2", 8)
        rows_of("norm_g", 16); rows_of("b_mod", 48); rows_of("pool_scale", 4); rows_of("subln_g", 2)
        qk = d["qk_norm_g"].rearrange("l m k -> (l m) k")
        add("qk_norm_g", 4, [(slice(0, QK), qk), (slice(QK, P), qk)])
        rows_of("ret_norm_w_2", 8); rows_of("hgrn_norm_w_2", 8); rows_of("hgrn_lb_logits_2", 8)
        rows_of("norm1_w_2", 16); rows_of("norm2_w_2", 16); rows_of("final_norm_w_2", 8)
        rows_of("ada_b_2", 96); rows_of("conv_b_2", 44)
        add("conv_w0", 66, [(slice(0, P), d["conv_w_2"][0].rearrange("j (r p) -> (j r) p", p=P))])
        add("conv_w1", 66, [(slice(0, P), d["conv_w_2"][1].rearrange("j (r p) -> (j r) p", p=P))])
        assert r <= 5 * P, r
        zero = self.V.did(nc.vector.memset(rows[:, :, :], 0.0))
        nc.sync.wait_ge(*zero)
        n_dma = 0
        for at, n, srcs in plan:
            for where, src in srcs:
                nc.sync.dma_start(rows[at % P:at % P + n, at // P, where], src).then_inc(self.vectors_dma, 16)
                n_dma += 1
        self.T.wait((self.vectors_dma, 16 * n_dma), (self.consts_in, 16 * self.n_consts))
        for g in range(5):
            last = nc.tensor.transpose(self.banks(0, 5 * P)[:, g * P:(g + 1) * P], rows[:, g, :], self.ident)
        turned = self.T.did(last)
        self.A.wait(turned)
        self.cols_ready = self.A.did(nc.scalar.activation(self.colsf, self.banks(0, 5 * P), ACT.Identity))

    def column(self, name, k=0, n=1):
        return self.colsf[:, self.col[name] + k:self.col[name] + k + n]

    def load_constants(self):
        nc = self.nc
        self.lamv = self.place("lamv", [P, 2, 4, QK], at=self.lower + 8192)
        loads = [(self.squares, self.dram["squares"]), (self.rope, self.dram["rope_axial"])]
        for dst, src in loads:
            nc.sync.dma_start(dst[:, :, :], src).then_inc(self.consts_in, 16)
        lam = self.dram["lam_vecs"].rearrange("l a k -> (l a k)").rearrange("(o n) -> o n", o=1).broadcast_to([P, 512])
        nc.sync.dma_start(self.lamv[:, :, :, :].rearrange("p l a k -> p (l a k)"), lam).then_inc(self.consts_in, 16)
        self.n_consts = 3

    def grant_slots(self, evac):
        for j in (0, 1):
            self.T.e.sem_inc(self.used[j], 1)
            self.G.e.sem_inc(self.split[j], 1)
            evac.e.sem_inc(self.freed[j], 1)
        self.uses = 0

    def round_tile(self, j, use, k):
        self.A.wait((self.landed[j], use * 16), (self.used[j], use))
        self.A.e.activation(self.hi[j][:, 0:k * P], self.raw[j][:, 0:k * P], ACT.Copy).then_inc(self.rounded[j], 1)

    def split_tile(self, j, use, k):
        self.G.wait((self.rounded[j], use))
        self.G.e.tensor_tensor(self.lo[j][:, 0:k * P], self.raw[j][:, 0:k * P], self.hi[j][:, 0:k * P].bitcast(F32),
                               ALU.subtract).then_inc(self.split[j], 1)

    def prime(self, k):
        self.round_tile(0, self.uses + 1, k)
        self.split_tile(0, self.uses + 1, k)

    def linear(self, n, k, source, moving, ready, act_evac, vec_evac=None, act_counts=0, vec_counts=0, then_k=None,
               mod=(), ready_tiles=None):
        nc, T, V, A, G = self.nc, self.T, self.V, self.A, self.G
        u, half = self.uses, n // 2
        with nc.Fori(0, half, engines=[ET.SP]) as i:
            for j in (0, 1):
                self.S.wait((self.split[j], i + (u + 1)))
                nc.sync.dma_start(self.raw[j][:, 0:k * P].rearrange("p (k n) -> p k n", k=k),
                                  source(i, j)).then_inc(self.landed[j], 16)
            for m in mod:
                self.mod_load(m, i)
        if half > 1:
            with nc.Fori(0, half - 1, engines=[ET.Pool]) as i:
                self.split_tile(1, i + (u + 1), k)
                self.split_tile(0, i + (u + 2), k)
        self.split_tile(1, u + half, k)
        if then_k:
            self.split_tile(0, u + half + 1, then_k)
        T.wait(*ready)
        with nc.Fori(0, half, engines=[ET.PE]) as i:
            for j in (0, 1):
                nc.tensor.wait_ge(self.split[j], i + (u + 2))
                nc.tensor.wait_ge(self.freed[j], i + (u + 1))
                for q in range(k):
                    if ready_tiles:
                        T.wait(*ready_tiles[q])
                    w_hi = self.hi[j][:, q * P:(q + 1) * P]
                    w_lo = self.lo[j][:, q * P:(q + 1) * P]
                    terms = [(w_hi, 0), (w_hi, 1), (w_lo, 0)]
                    for t, (w, which) in enumerate(terms):
                        for bank, c, cols in moving:
                            x = (self.h_hi, self.h_lo)[which] if not self.act_pair else self.act_pair[which]
                            last = nc.tensor.matmul(self.ps[:, bank + j, 0:cols], w, x[:, q, c:c + cols],
                                                    start=(q == 0 and t == 0), stop=(q == k - 1 and t == 2))
                last.then_inc(self.used[j], 1)
            for m in mod:
                self.mod_turn(m, i)
        if mod or vec_evac:
            counts = {V: vec_counts + sum(self.mod_counts(m) for m in mod)}
            with passes(nc, half, counts) as i:
                for m in mod:
                    self.mod_sum(m, i)
                for j in (0, 1):
                    if vec_evac:
                        vec_evac(i, j, i + (u + 2))
                for m in mod:
                    self.mod_finish(m, i)
            self.mod_last = V.now()
            for m in mod:
                self.mod_uses[m["slot"]] += half
        if half > 1:
            with passes(nc, half - 1, {A: act_counts}) as i:
                self.round_tile(1, i + (u + 1), k)
                act_evac(i, 0, i + (u + 2))
                self.round_tile(0, i + (u + 2), k)
                act_evac(i, 1, i + (u + 2))
        self.round_tile(1, u + half, k)
        act_evac(half - 1, 0, u + half + 1)
        if then_k:
            self.round_tile(0, u + half + 1, then_k)
        act_evac(half - 1, 1, u + half + 1)
        self.uses = u + half
        self.product_done = (self.used[1], u + half + 1)
        self.banks_read = [(self.freed[j], u + half + 1) for j in (0, 1)]

    act_pair = None

    def mod_setup(self):
        self.pool_scratch = self.top
        self.mod_w = [self.place(f"mod_w{s}", [P, KT, CHUNK_COLS]) for s in (0, 1)]
        self.mod_acc = [[self.place(f"mod_acc{s}{v}", [P, CHUNK_COLS]) for v in (0, 1)] for s in (0, 1)]
        for s in (0, 1):
            self.V.e.sem_inc(self.mod_summed[s], 1)

    def mod_chunk(self, slot, source, outs):
        return {"slot": slot, "source": source, "outs": outs}

    def mod_counts(self, m):
        return (KT + 1) * len(m["outs"]) - 1

    def mod_use(self, m, i, add):
        return i + (self.mod_uses[m["slot"]] + add)

    def mod_load(self, m, i):
        s = m["slot"]
        self.S.wait((self.mod_summed[s], self.mod_use(m, i, 1)))
        self.S.e.dma_start(self.mod_w[s][:, :, :], m["source"](i)).then_inc(self.mod_landed[s], 16)

    def mod_sum(self, m, i):
        s, V = m["slot"], self.V
        V.wait((self.mod_landed[s], self.mod_use(m, i, 1) * 16))
        for v, (c, _, _) in enumerate(m["outs"]):
            acc, w = self.mod_acc[s][v][:, :], self.mod_w[s]
            t = V.did(V.e.tensor_scalar(acc, w[:, 0, :], self.act_c[:, c:c + 1], None, ALU.mult))
            for q in range(1, KT):
                V.wait(t)
                x = V.e.scalar_tensor_tensor(acc, w[:, q, :], self.act_c[:, c + q:c + q + 1], acc, ALU.mult, ALU.add)
                if q < KT - 1:
                    t = V.did(x)
                elif v == len(m["outs"]) - 1:
                    x.then_inc(self.mod_summed[s], 1)
                else:
                    V.did(x)

    def mod_turn(self, m, i):
        s = m["slot"]
        self.T.wait((self.mod_summed[s], self.mod_use(m, i, 2)))
        for v in range(len(m["outs"])):
            for q in range(2):
                k = v * 2 + q
                last = self.T.e.matmul(self.ps[:, 7 - s, k:k + 1], self.mod_acc[s][v][:, q * P:(q + 1) * P],
                                       self.ones[:, 0:1], start=True, stop=True)
        last.then_inc(self.mod_turned[s], 1)

    def mod_finish(self, m, i):
        s, V = m["slot"], self.V
        V.wait((self.mod_turned[s], self.mod_use(m, i, 1)))
        for v, (_, out, bias) in enumerate(m["outs"]):
            k = v * 2
            V.did(V.e.tensor_tensor(out(i), self.ps[:, 7 - s, k:k + 2], bias(i), ALU.add))

    def mod_alone(self, n, mods):
        nc = self.nc
        with nc.Fori(0, n, engines=[ET.SP]) as i:
            for m in mods:
                self.mod_load(m, i)
        with nc.Fori(0, n, engines=[ET.PE]) as i:
            for m in mods:
                self.mod_turn(m, i)
        with passes(nc, n, {self.V: sum(self.mod_counts(m) for m in mods)}) as i:
            for m in mods:
                self.mod_sum(m, i)
            for m in mods:
                self.mod_finish(m, i)
        self.mod_last = self.V.now()
        for m in mods:
            self.mod_uses[m["slot"]] += n

    def add_squares(self, x, cut, square):
        V = self.V
        V.wait(V.did(V.e.tensor_tensor(square, x, x, ALU.mult)))
        V.wait(V.did(V.e.tensor_tensor(self.ssq[:, cut], self.ssq[:, cut], square, ALU.add)))

    def token_sums(self, bank, first, x, t, ones):
        n = ones.shape[1]
        for q in range(t // P):
            at = first + q * n
            last = self.T.e.matmul(self.ps[:, bank, at:at + n], x[:, q * P:(q + 1) * P], ones, start=True, stop=True)
        return self.T.did(last)

    def inverse_roots(self, out, sums, n, ready):
        self.A.wait(*ready)
        self.V.wait(self.A.did(self.A.e.activation(out, sums, ACT.Sqrt, bias=self.eps[:, 0:1], scale=1.0 / n)))
        return self.V.did(self.V.e.reciprocal(out, out))

    def spread(self, bank, roots, first, t):
        for q in range(t // P):
            over = roots[:, first + q:first + q + 1].broadcast_to([P, P])
            last = self.T.e.matmul(self.banks(bank, t)[:, q * P:(q + 1) * P], over, self.ident, start=True, stop=True)
        return self.T.did(last)

    def norm(self, t, ready, segments, free):
        T, V, A, G = self.T, self.V, self.A, self.G
        tmp, h = self.norm_buffers
        for e in (T, V, A):
            e.wait(*ready, *free)
        sums = self.token_sums(6, 0, self.ssq, t, self.ones[:, 0:1])
        T.wait(self.inverse_roots(self.roots[:, 0:t // P], self.ps[:, 6, 0:t // P], D, [sums]))
        V.wait(self.spread(4, self.roots, 0, t))
        rstd = self.banks(4, t)
        normed, value, hi_done, lo_done = {}, {}, {}, {}

        def scale(k):
            if k >= 3:
                V.wait(hi_done[k - 3], value[k - 3])
            normed[k] = V.did(V.e.tensor_tensor(tmp[k % 3][:, 0:t], self.xT[:, k, 0:t], rstd, ALU.mult))

        def modulate(k):
            V.wait(normed[k])
            A.wait(normed[k])
            if k >= 3:
                V.wait(lo_done[k - 3])
            for first, count, gain, shift in segments:
                cut = slice(first, first + count)
                value[k] = V.did(V.e.tensor_scalar(h[k % 3][:, cut], tmp[k % 3][:, cut], gain[:, k:k + 1],
                                                   shift[:, k:k + 1], ALU.mult, ALU.add))
                hi_done[k] = A.did(A.e.activation(self.h_hi[:, k, cut], tmp[k % 3][:, cut], ACT.Identity,
                                                  bias=shift[:, k:k + 1], scale=gain[:, k:k + 1]))

        def rest(k):
            e = G if k % 3 else V
            e.wait(value[k], hi_done[k])
            lo_done[k] = e.did(e.e.tensor_tensor(self.h_lo[:, k, 0:t], h[k % 3][:, 0:t],
                                                 self.h_hi[:, k, 0:t].bitcast(F32), ALU.subtract))

        pipeline(KT, scale, modulate, rest)
        return [[hi_done[k], lo_done[k]] for k in range(KT)]

    def split_pair(self, k, cut, value, ready):
        self.A.wait(*ready)
        hh = self.A.did(self.A.e.activation(self.h_hi[:, k, cut], value, ACT.Copy))
        self.G.wait(*ready, hh)
        return self.G.did(self.G.e.tensor_tensor(self.h_lo[:, k, cut], value, self.h_hi[:, k, cut].bitcast(F32),
                                                 ALU.subtract))


X_, C_ = slice(0, TX), slice(TX, TA)
TILE_A, TILE_B, TILE_Q, TILE_K, TILE_V, TILE_G = 0, 2, 4, 8, 12, 16


def load_x(p):
    nc, T, A = p.nc, p.T, p.A
    rows = p.place("x_rows", [P, TA // P, D], at=p.lower + 24576)
    nc.sync.dma_start(rows[:, 0:4, :], p.dram["x"].rearrange("b (t p) d -> p (b t) d", p=P)).then_inc(p.x_in, 16)
    nc.sync.dma_start(rows[:, 4:6, :], p.dram["ctx"].rearrange("b (t p) d -> p (b t) d", p=P)).then_inc(p.x_in, 16)
    T.wait((p.x_in, 32), (p.consts_in, 16 * p.n_consts))
    copied = []
    for k in range(KT):
        b = 2 + 2 * (k % 2)
        if k >= 2:
            T.wait(copied[k - 2])
        for t in range(TA // P):
            last = T.e.transpose(p.banks(b, TA)[:, t * P:(t + 1) * P], rows[:, t, k * P:(k + 1) * P], p.ident)
        A.wait(T.did(last))
        copied.append(A.did(A.e.activation(p.xT[:, k, :], p.banks(b, TA), ACT.Copy)))
    return copied[-1]


def first_block(p):
    nc, T, V, A, G = p.nc, p.T, p.V, p.A, p.G
    p.load_constants()
    p.load_vectors()
    p.mod_setup()
    eps = V.did(nc.vector.memset(p.eps[:, :], EPS))
    x_there = load_x(p)

    A.wait(p.cols_ready)
    c_there = A.did(nc.scalar.activation(p.act_c[:, :], p.column("c", 0, 24), ACT.Silu))
    lam, dots = p.small[:, 0:2], p.small[:, 2:6]
    prod = p.place("lam_products", [P, 2, 2, QK], at=p.lower + 12288)
    V.wait((p.consts_in, 16 * p.n_consts))
    t = V.did(V.e.tensor_tensor(prod[:, :, :, :], p.lamv[:, :, 0:4:2, :], p.lamv[:, :, 1:4:2, :], ALU.mult))
    V.wait(t)
    t = V.did(V.e.tensor_reduce(dots, prod[:, :, :, :].rearrange("p l a k -> p (l a) k"), AX, ALU.add))
    A.wait(t)
    t = A.did(A.e.activation(dots, dots, ACT.Exp))
    V.wait(t)
    for l in range(2):
        init = 0.8 - 0.6 * math.exp(-0.3 * l)
        t = V.did(V.e.scalar_tensor_tensor(lam[:, l:l + 1], dots[:, 2 * l + 1:2 * l + 2], -init,
                                           dots[:, 2 * l:2 * l + 1], ALU.add, ALU.subtract))
    lam_ready = t
    qk_gain = p.place("qk_gain", [P, 2, 8])
    sub_gain = p.small[:, 8:10]
    V.wait(p.cols_ready)
    for l in range(2):
        for m in range(2):
            for r in range(4):
                t = V.did(V.e.tensor_copy(qk_gain[:, l, 4 * m + r:4 * m + r + 1], p.column("qk_norm_g", 2 * l + m)))
        init = 0.8 - 0.6 * math.exp(-0.3 * l)
        t = V.did(V.e.tensor_scalar(sub_gain[:, l:l + 1], p.column("subln_g", l), 1.0 - init, None, ALU.mult))
    gains_ready = t

    wblk = p.place("group_weights", [P, 2, 2, 2, P])
    t = V.did(V.e.memset(wblk[:, :, :, :, :].rearrange("p a b c d -> p (a b c d)"), 0.0))
    nc.sync.wait_ge(*t)
    groups_in = nc.alloc_semaphore("group_weights_landed")
    for which, name in ((0, "w_pool"), (1, "w_fourier")):
        for l in range(2):
            for g in range(4):
                half = slice(64 * (g % 2), 64 * (g % 2) + 64)
                nc.sync.dma_start(wblk[half, l, which, g // 2, half], p.dram[name][l, g]).then_inc(groups_in, 16)
    groups_ready = (groups_in, 16 * 16)

    w_mod, ada = p.dram["w_mod"], p.dram["ada_w_2"]

    def mod1(l, slot, chunk):
        def source(i):
            return w_mod[l].rearrange("(k p) n -> p k n", p=P)[:, :, bass.ds(chunk(i) * CHUNK_COLS, CHUNK_COLS)]
        outs = [(8 * v, lambda i, v=v: p.mod1[:, l, v, bass.ds(chunk(i) * 2, 2)],
                 lambda i: p.colsf[:, bass.ds(chunk(i) * 2 + (p.col["b_mod"] + 24 * l), 2)]) for v in (0, 1)]
        return p.mod_chunk(slot, source, outs)

    def mod2(l, slot, chunk):
        def source(i):
            return ada[l].rearrange("(k p) n -> p k n", p=P)[:, :, bass.ds(chunk(i) * CHUNK_COLS, CHUNK_COLS)]
        return p.mod_chunk(slot, source, [
            (16, lambda i: p.mod2[:, bass.ds(chunk(i) * 2 + 48 * l, 2)],
             lambda i: p.colsf[:, bass.ds(chunk(i) * 2 + (p.col["ada_b_2"] + 48 * l), 2)])])

    V.wait(c_there)
    T.wait(V.now())
    p.mod_alone(6, [mod1(0, 0, lambda i: i * 2), mod1(0, 1, lambda i: i * 2 + 1)])

    proj = p.place("proj", [P, 24, TA])
    at = p.top - (24 - TILE_G) * TA * 4
    p.mix_scratch = at - (TILE_G - TILE_K) * TA * 4
    buffers = [p.place(f"norm{b}", [P, TA], at=at + b * 3072) for b in range(7)]
    p.norm_buffers = (buffers[1:4], buffers[4:7])
    square = p.place("square", [P, TA], at=at + 7 * 3072)
    gain = p.place("norm_gain", [P, 2, 2, 8])

    V.wait(x_there)
    V.wait(V.did(V.e.memset(p.ssq[:, :], 0.0)))
    for k in range(KT):
        p.add_squares(p.xT[:, k, :], slice(0, TA), square[:, :])
    p.grant_slots(A)
    x_ready, free = [x_there, eps], [x_there, p.mod_last, lam_ready]
    for l in range(2):
        update_ctx = l == 0
        V.wait(p.mod_last)
        for v in range(2):
            t = V.did(V.e.scalar_tensor_tensor(gain[:, l, v, :], p.mod1[:, l, v, 8:16], 1.0,
                                               p.column("norm_g", 8 * l, 8), ALU.add, ALU.mult))
        gain_ready = t
        if l == 0:
            p.prime(KT)
        V.wait(gain_ready); A.wait(gain_ready)
        segments = [(0, TX, gain[:, l, 0, :], p.mod1[:, l, 0, 0:8]), (TX, TC, gain[:, l, 1, :], p.mod1[:, l, 1, 0:8])]
        h_tiles = p.norm(TA, [*x_ready, V.now()], segments, free)

        def w_in(first):
            return lambda i, j: p.dram["w_in"][l].rearrange("(k p) n -> p k n", p=P)[
                :, :, bass.ds(i * (2 * P) + (first + j) * P, P)]

        def to_proj(first, func, ctx):
            def evac(i, j, use):
                A.wait((p.used[j], use))
                x = A.e.activation(proj[:, bass.ds(i * 2 + (first + j), 1), X_].rearrange("p o t -> p (o t)"),
                                   p.ps[:, j, :], func)
                if ctx:
                    x = A.e.activation(proj[:, bass.ds(i * 2 + (first + j), 1), C_].rearrange("p o t -> p (o t)"),
                                       p.ps[:, 2 + j, 0:TC], func)
                x.then_inc(p.freed[j], 1)
            return evac

        both = [(0, 0, TX), (2, TX, TC)]
        only_x = [(0, 0, TX)]
        if l == 0:
            p.linear(16, KT, w_in(0), both, [], to_proj(0, ACT.Identity, True), then_k=KT, ready_tiles=h_tiles,
                     mod=[mod1(1, 0, lambda i: i), mod2(0, 1, lambda i: i)])
            p.linear(8, KT, w_in(16), both, [], to_proj(16, ACT.Silu, True),
                     mod=[mod1(1, 0, lambda i: i + 8), mod2(0, 1, lambda i: i + 8)])
        else:
            p.linear(8, KT, w_in(0), only_x, [], to_proj(0, ACT.Identity, False), then_k=KT, ready_tiles=h_tiles,
                     mod=[mod2(0, 0, lambda i: i + 12), mod2(1, 1, lambda i: i)])
            p.linear(8, KT, w_in(8), both, [], to_proj(8, ACT.Identity, True), then_k=KT,
                     mod=[mod2(0, 0, lambda i: i + 16), mod2(1, 1, lambda i: i + 4)])
            p.linear(8, KT, w_in(16), only_x, [], to_proj(16, ACT.Silu, False),
                     mod=[mod2(0, 0, lambda i: i + 20), mod2(1, 1, lambda i: i + 8)])
        projected = list(p.banks_read) + [p.mod_last, p.product_done]
        t = TA if update_ctx else TX
        load_tables(p, l, projected)
        qk_done = norm_rope(p, l, proj, qk_gain, projected, gains_ready)
        fourier(p, l, proj, wblk, t, qk_done, groups_ready)
        pool_done = pooling(p, l, proj, wblk, t, qk_done)
        p.S.wait(*pool_done)
        heads_done = attention(p, l, proj, lam, t, pool_done)
        p.prime(KT)
        h_tiles, mixed = mix(p, l, proj, sub_gain, t, heads_done)

        def w_out(i, j):
            return p.dram["w_out"][l].rearrange("(k p) n -> p k n", p=P)[:, :, bass.ds(i * (2 * P) + j * P, P)]

        def residual(i, j, use):
            V.wait((p.used[j], use))
            xk = p.xT[:, bass.ds(i * 2 + j, 1), X_].rearrange("p o t -> p (o t)")
            x = V.e.scalar_tensor_tensor(xk, p.ps[:, j, :], p.mod1[:, l, 0, bass.ds(i * 2 + (16 + j), 1)], xk,
                                         ALU.mult, ALU.add)
            if update_ctx:
                xk = p.xT[:, bass.ds(i * 2 + j, 1), C_].rearrange("p o t -> p (o t)")
                x = V.e.scalar_tensor_tensor(xk, p.ps[:, 2 + j, 0:TC], p.mod1[:, l, 1, bass.ds(i * 2 + (16 + j), 1)],
                                             xk, ALU.mult, ALU.add)
            x.then_inc(p.freed[j], 1)
            V.wait((p.freed[j], use))
            whole = slice(0, TA if update_ctx else TX)
            p.add_squares(flat(p.xT[:, bass.ds(i * 2 + j, 1), whole]), whole, square[:, whole])

        V.wait(*mixed)
        V.wait(V.did(V.e.memset(p.ssq[:, 0:t], 0.0)))
        mods = ([mod2(1, 1, lambda i: i + 12)] if l == 0 else
                [mod2(1, 0, lambda i: i + 16), mod2(1, 1, lambda i: i + 20)])
        p.linear(8, KT, w_out, both if update_ctx else only_x, [], lambda i, j, use: None, residual, vec_counts=4,
                 ready_tiles=h_tiles,
                 then_k=KT if l == 0 else None, mod=mods)
        x_ready, free = [*p.banks_read, V.now()], [*p.banks_read, p.mod_last, p.product_done, *mixed]
    return x_ready


def load_tables(p, l, ready):
    if l == 0:
        p.tables_in = p.nc.alloc_semaphore("tables_landed")
    p.dft_x = p.place(f"dft_x{l}", [P, 2, 4, TX], at=p.lower)
    p.dft_ctx = p.place(f"dft_ctx{l}", [P, 2, 2, TC], at=p.lower + 16384)
    p.inv_count = p.place(f"inv_count{l}", [P, 2, TA], at=p.lower + 20480)
    p.S.wait(*ready)
    p.S.e.dma_start(p.dft_x[:, :, :, :], p.dram["dft_x"]).then_inc(p.tables_in, 16)
    p.S.e.dma_start(p.dft_ctx[:, :, :, :], p.dram["dft_ctx"]).then_inc(p.tables_in, 16)
    p.S.e.dma_start(p.inv_count[:, :, :], p.dram["inv_count"]).then_inc(p.tables_in, 16)
    p.tables_ready = (p.tables_in, 48 * (l + 1))
    p.scratch = p.lower + 26624


def flat(ap):
    return ap.rearrange("p o t -> p (o t)")


def norm_rope(p, l, proj, qk_gain, ready, gains_ready):
    T, V, A, G, base = p.T, p.V, p.A, p.G, p.scratch
    sq = [p.place(f"qk_sq{l}{j}", [P, TA], at=base + j * 3072) for j in range(3)]
    cs = [p.place(f"qk_cos{l}{j}", [P, TX], at=base + 9216 + j * 2048) for j in range(3)]
    sn = [p.place(f"qk_sin{l}{j}", [P, TX], at=base + 15360 + j * 2048) for j in range(3)]
    wide = sq[0:2]
    per = 2 * TA // P
    for e in (A, V, T, G):
        e.wait(*ready, gains_ready)
    with passes(p.nc, 2, {T: 12, V: 13, A: 9, G: 4}) as i:
        start = [e.now() for e in (T, V, A, G)]
        for e in (T, V, A, G):
            e.wait(*start)
        tile = [flat(proj[:, bass.ds(i * 4 + (TILE_Q + k), 1), :]) for k in range(4)]
        tile_x = [flat(proj[:, bass.ds(i * 4 + (TILE_Q + k), 1), X_]) for k in range(4)]
        squared, summed, over, normed, turned, cosine, done = ({} for _ in range(7))
        for k in range(4):
            if k >= 3:
                A.wait(summed[k - 3])
            squared[k] = A.did(A.e.activation(sq[k % 3][:, :], tile[k], ACT.Square))
            T.wait(squared[k])
            summed[k] = p.token_sums(6, k * per, sq[k % 3], TA, p.ones_half[:, 0:P:QK])
        roots = p.inverse_roots(p.roots[:, 0:4 * per], p.ps[:, 6, 0:4 * per], QK, [summed[3]])

        def norm(k):
            b = 3 * (k % 2)
            A.wait(roots)
            if k >= 2:
                A.wait(over[k - 2])
                T.wait(normed[k - 2])
            T.wait(A.did(A.e.activation(
                wide[k % 2][:, :].rearrange("p (a o) -> p a o", o=QK),
                p.roots[:, k * per:(k + 1) * per].rearrange("p (a o) -> p a o", o=1).broadcast_to([P, per, QK]),
                ACT.Copy)))
            for c in range(TA // P):
                last = T.e.transpose(p.banks(b, TA)[:, c * P:(c + 1) * P], wide[k % 2][:, c * P:(c + 1) * P], p.ident)
            over[k] = T.did(last)
            V.wait(over[k])
            normed[k] = V.did(V.e.scalar_tensor_tensor(tile[k], tile[k], qk_gain[:, l, bass.ds(i * 4 + k, 1)],
                                                       p.banks(b, TA), ALU.mult, ALU.mult))

        def turn(k):
            T.wait(normed[k])
            if k >= 2:
                T.wait(done[k - 2])
            turned[k] = T.did(T.e.matmul(p.ps[:, 3 * (k % 2) + 2, :], p.rot_axial, tile_x[k], start=True, stop=True))
            G.wait(normed[k])
            if k >= 3:
                G.wait(done[k - 3])
            cosine[k] = G.did(G.e.tensor_tensor(cs[k % 3][:, :], tile_x[k], p.rope[:, 0, :], ALU.mult))

        def combine(k):
            V.wait(turned[k], normed[k])
            s = V.did(V.e.tensor_tensor(sn[k % 3][:, :], p.ps[:, 3 * (k % 2) + 2, :], p.rope[:, 1, :], ALU.mult))
            V.wait(s, cosine[k])
            done[k] = V.did(V.e.tensor_tensor(tile_x[k], cs[k % 3][:, :], sn[k % 3][:, :], ALU.add))

        pipeline(4, norm, turn, combine)
    return [e.now() for e in (T, V, A, G)]


def fourier(p, l, proj, wblk, t, ready, groups_ready):
    T, A, base = p.T, p.A, p.scratch
    tok = p.place(f"f_tok{l}", [P, TA // P, 2, P], at=base)
    bx = p.place(f"f_bx{l}", [P, 2, 2, TX], at=base + 6144)
    cw = p.place(f"f_cw{l}", [P, 2, 2, P], at=base + 14336)
    T.wait(groups_ready, *ready)
    A.wait(*ready)
    for g in range(2):
        for s, m in enumerate((p.dft_c, p.dft_ns)):
            last = T.e.matmul(p.ps[:, 6, (2 * g + s) * P:(2 * g + s + 1) * P], m, wblk[:, l, 1, g, :],
                              start=True, stop=True)
    A.wait(T.did(last))
    folded = A.did(A.e.activation(cw[:, :, :, :].rearrange("p g s n -> p (g s n)"), p.ps[:, 6, :], ACT.Copy))
    copied = []
    for g in range(2):
        for q in range(t // P):
            last = T.e.transpose(p.banks(2 * g, t)[:, q * P:(q + 1) * P],
                                 proj[:, TILE_A + g, q * P:(q + 1) * P], p.ident)
        A.wait(T.did(last))
        copied.append(A.did(A.e.activation(tok[:, 0:t // P, g, :],
                                           p.banks(2 * g, t).rearrange("p (q n) -> p q n", n=P), ACT.Copy)))
    T.wait(*copied, folded, p.tables_ready)
    for first, length, tab in ((0, TX, p.dft_x), (TX, TC, p.dft_ctx)):
        if first >= t:
            continue
        T.wait(A.now())
        moved = []
        for g in range(2):
            for s in range(2):
                for q in range(length // P):
                    last = T.e.matmul(p.ps[:, 2 * g + s, 0:length], tok[:, first // P + q, g, :], tab[:, s, q, :],
                                      start=(q == 0), stop=(q == length // P - 1))
                A.wait(T.did(last))
                moved.append(A.did(A.e.activation(bx[:, g, s, 0:length], p.ps[:, 2 * g + s, 0:length], ACT.Copy)))
        T.wait(*moved)
        for g in range(2):
            for s in range(2):
                last = T.e.matmul(p.ps[:, 4 + g, 0:length], cw[:, g, s, :], bx[:, g, s, 0:length],
                                  start=(s == 0), stop=(s == 1))
            A.wait(T.did(last))
            A.did(A.e.activation(proj[:, TILE_A + g, first:first + length], p.ps[:, 4 + g, 0:length], ACT.Copy))
    return [T.now(), A.now()]


def pooling(p, l, proj, wblk, t, ready):
    T, V, A, base = p.T, p.V, p.A, p.pool_scratch
    edge, width = 16, TX + 32
    pad = p.place(f"pool_pad{l}", [P, 3, width], at=base)
    mean = p.place(f"pool_mean{l}", [P, 2, TA], at=base + 12 * width)
    V.wait(*ready, p.tables_ready)
    low, high, whole = slice(0, 64), slice(64, P), slice(0, P)
    parts = [(first, length, g) for first, length in ((0, TX), (TX, TC)) if first < t for g in range(2)]
    done, free = {}, []
    for first, length, g in parts:
        cut = slice(first, first + length)
        if g == 0:
            V.wait(*free)
            V.wait(V.did(V.e.memset(pad[:, :, :].rearrange("p a w -> p (a w)"), 0.0)))
        V.wait(*free)
        c = V.did(V.e.tensor_copy(pad[:, 0, edge:edge + length], proj[:, TILE_B + g, cut]))
        plan = [(1, 0, -1, 0, 7, whole), (2, 1, -1, 1, 6, high if g == 0 else whole)]
        if g == 1:
            plan += [(1, 2, -2, 2, 4, whole), (2, 1, -4, 4, 0, high)]
        for dst, src, d0, d1, reach, rows in plan:
            a, b = edge - reach, edge + length + reach
            V.wait(c)
            c = V.did(V.e.tensor_tensor(pad[rows, dst, a:b], pad[rows, src, a + d0:b + d0],
                                        pad[rows, src, a + d1:b + d1], ALU.add))
        free = []
        for rows, src in ((low, 1), (high, 2)):
            V.wait(c)
            V.wait(V.did(V.e.tensor_tensor(mean[rows, g, cut], pad[rows, src, edge:edge + length],
                                           p.inv_count[rows, g, cut], ALU.mult)))
            free.append(V.did(V.e.tensor_tensor(mean[rows, g, cut], mean[rows, g, cut],
                                                pad[rows, 0, edge:edge + length], ALU.subtract)))
        done[first, g] = free
    for first, length, g in parts:
        cut = slice(first, first + length)
        T.wait(*done[first, g], A.now())
        A.wait(T.did(T.e.matmul(p.ps[:, 6 + g, 0:length], wblk[:, l, 0, g, :], mean[:, g, cut], start=True, stop=True)))
        A.did(A.e.activation(proj[:, TILE_B + g, cut], p.ps[:, 6 + g, 0:length], ACT.Copy,
                             scale=p.column("pool_scale", 2 * l + g)))
    return [V.now(), A.now(), T.now()]


def attention(p, l, proj, neg_lam, t, ready):
    T, V, A, G, base = p.T, p.V, p.A, p.G, p.lower
    qs = p.place(f"a_q{l}", [P, TA], at=base)
    vt = p.place(f"a_vt{l}", [P, TA], at=base + 3072)
    v = p.place(f"a_v{l}", [P, TA // P, P], at=base + 6144)
    prob = [[p.place(f"a_p{l}{b}{m}", [P, TA], at=base + 9216 + (2 * b + m) * 3072) for m in (0, 1)] for b in (0, 1)]
    pt = p.place(f"a_pt{l}", [P, TA // P, TA], at=base + 21504)
    st = p.place(f"a_stat{l}", [P, 2, 8], at=base + 21504 + 18432)
    ks = p.place(f"a_k{l}", [P, TA], at=base + 21504 + 18432 + 64)
    queries = t // P
    for e in (T, V, A, G):
        e.wait(*ready)
    n = queries
    outs = 1 if t == TX else 2
    with passes(p.nc, HEADS, {T: 1 + 3 * n + outs, V: 2 + 7 * n, A: 2 + 3 * n + outs}) as i:
        start = [e.now() for e in (T, V, A)]
        for e in (T, V, A):
            e.wait(*start)
        q_in = A.did(A.e.activation(qs[:, 0:t], flat(proj[:, bass.ds(i + TILE_Q, 1), 0:t]), ACT.Copy))
        k_in = V.did(V.e.tensor_copy(ks[:, :], flat(proj[:, bass.ds(i + TILE_K, 1), :])))
        v_in = V.did(V.e.tensor_copy(vt[:, :], flat(proj[:, bass.ds(i + TILE_V, 1), :])))
        soft, turned, exps, moved = {}, {}, {}, {}
        ring = lambda q, m: 2 * ((2 * q + m) % 3)

        def keys(q):
            return (0, TA) if q < TX // P else (TX, TC)

        def scores(q):
            first, count = keys(q)
            for m in (0, 1):
                rows = slice(QK * m, QK * m + QK)
                if 2 * q + m >= 3:
                    T.wait(exps[2 * q + m - 3])
                for b in range(0, count, 512):
                    w = min(512, count - b)
                    last = T.e.matmul(p.ps[:, ring(q, m) + b // 512, 0:w], qs[rows, q * P:(q + 1) * P],
                                      ks[rows, first + b:first + b + w], start=True, stop=True)
                soft[q, m] = T.did(last)

        def softmax(q):
            first, count = keys(q)
            s, b = st[:, q % 2, :], q % 2
            if q >= 2:
                V.wait(turned[q - 2])
                A.wait(turned[q - 2])
            for m in (0, 1):
                V.wait(soft[q, m])
                mx = V.did(V.e.tensor_reduce(s[:, m:m + 1], p.banks(ring(q, m), count), AX, ALU.max))
                V.wait(mx)
                neg = V.did(V.e.tensor_scalar(s[:, 2 + m:3 + m], s[:, m:m + 1], -QK ** -0.5, None, ALU.mult))
                A.wait(neg)
                exps[2 * q + m] = A.did(A.e.activation(prob[b][m][:, 0:count], p.banks(ring(q, m), count), ACT.Exp,
                                                       bias=s[:, 2 + m:3 + m], scale=QK ** -0.5,
                                                       accum_out=s[:, 4 + m:5 + m]))

        combined = {}

        def combine(q):
            count, s, b = keys(q)[1], st[:, q % 2, :], q % 2
            V.wait(exps[2 * q], exps[2 * q + 1])
            V.wait(V.did(V.e.reciprocal(s[:, 6:8], s[:, 4:6])))
            V.wait(V.did(V.e.tensor_scalar(prob[b][1][:, 0:count], prob[b][1][:, 0:count], s[:, 7:8],
                                           neg_lam[:, l:l + 1], ALU.mult, ALU.mult)))
            combined[q] = V.did(V.e.scalar_tensor_tensor(prob[b][0][:, 0:count], prob[b][0][:, 0:count], s[:, 6:7],
                                                         prob[b][1][:, 0:count], ALU.mult, ALU.add))

        def transpose(q):
            first, count = keys(q)
            b, k0 = q % 2, first // P
            T.wait(combined[q], moved[q - 1] if q else v_ready)
            for k in range(count // P):
                last = T.e.transpose(p.banks(6, count)[:, k * P:(k + 1) * P], prob[b][0][:, k * P:(k + 1) * P], p.ident)
            turned[q] = T.did(last)
            A.wait(turned[q])
            moved[q] = A.did(A.e.activation(pt[:, k0:k0 + count // P, q * P:(q + 1) * P],
                                            p.banks(6, count).rearrange("p (k n) -> p k n", n=P), ACT.Copy))

        T.wait(q_in, k_in)
        scores(0)
        T.wait(v_in)
        for k in range(TA // P):
            last = T.e.transpose(p.banks(6, TA)[:, k * P:(k + 1) * P], vt[:, k * P:(k + 1) * P], p.ident)
        A.wait(T.did(last))
        v_ready = A.did(A.e.activation(v[:, :, :].rearrange("p k n -> p (k n)"), p.banks(6, TA), ACT.Copy))
        softmax(0)
        for q in range(1, queries + 1):
            if q < queries:
                scores(q)
            combine(q - 1)
            if q < queries:
                softmax(q)
            transpose(q - 1)
        for out, (first, count, k0) in enumerate(((0, TX, 0), (TX, TC, TX // P))[:outs]):
            T.wait(moved[queries - 1])
            for k in range(k0, TA // P):
                last = T.e.matmul(p.ps[:, 6 + out, 0:count], v[:, k, :], pt[:, k, first:first + count],
                                  start=(k == k0), stop=(k == TA // P - 1))
            A.wait(T.did(last))
            A.did(A.e.activation(flat(proj[:, bass.ds(i + TILE_Q, 1), first:first + count]),
                                 p.ps[:, 6 + out, 0:count], ACT.Copy))
    return [e.now() for e in (T, V, A)]


def mix(p, l, proj, sub_gain, t, ready):
    T, V, A, G, base = p.T, p.V, p.A, p.G, p.mix_scratch
    sq = [p.place(f"m_sq{l}{b}", [P, TA], at=base + 3072 * b) for b in range(3)]
    for e in (T, V, A, G):
        e.wait(*ready)
    heads = [(proj[:, TILE_Q + h, 0:t], sub_gain[:, l:l + 1], proj[:, TILE_G + 4 + h, 0:t]) for h in range(HEADS)]
    plain = [(proj[:, tile, 0:t], None, proj[:, TILE_G + k, 0:t])
             for k, tile in enumerate((TILE_A, TILE_A + 1, TILE_B, TILE_B + 1))]
    return norm_gate_split(p, plain + heads, t, [s[:, 0:t] for s in sq])


def norm_gate_split(p, items, t, sq):
    T, V, A, G = p.T, p.V, p.A, p.G
    heads = [k for k, (_, gain, _) in enumerate(items) if gain is not None]
    squared, summed, over, scaled, gated, hi, lo = ({} for _ in range(7))
    per = t // P
    for n, k in enumerate(heads):
        if n >= 3:
            A.wait(summed[heads[n - 3]])
        squared[k] = A.did(A.e.activation(sq[n % 3], items[k][0], ACT.Square))
        T.wait(squared[k])
        summed[k] = p.token_sums(4, n * per, sq[n % 3], t, p.ones[:, 0:1])
    roots = p.inverse_roots(p.roots[:, 0:len(heads) * per], p.ps[:, 4, 0:len(heads) * per], P, [summed[heads[-1]]])

    def scale(k):
        o, gain, _ = items[k]
        if k in squared:
            n = heads.index(k)
            b = 6 - 2 * (n % 2)
            T.wait(roots)
            if n >= 2:
                T.wait(scaled[k - 2])
            V.wait(p.spread(b, p.roots, n * per, t))
            scaled[k] = V.did(V.e.scalar_tensor_tensor(o, o, gain, p.banks(b, t), ALU.mult, ALU.mult))

    def gate(k):
        o, _, g = items[k]
        if k in scaled:
            V.wait(scaled[k])
        gated[k] = V.did(V.e.tensor_tensor(o, o, g, ALU.mult))

    def high(k):
        A.wait(gated[k])
        hi[k] = A.did(A.e.activation(p.h_hi[:, k, 0:t], items[k][0], ACT.Copy))

    def low(k):
        e = V if k % 3 == 0 else G
        e.wait(gated[k], hi[k])
        lo[k] = e.did(e.e.tensor_tensor(p.h_lo[:, k, 0:t], items[k][0], p.h_hi[:, k, 0:t].bitcast(F32),
                                        ALU.subtract))

    pipeline(len(items), scale, gate, high, low)
    return [[hi[k], lo[k]] for k in range(len(items))], [V.now(), A.now(), G.now()]


RQ, RK, RV, RG, HQ, HF, HI, HG = range(0, 32, 4)
SH1, SC1, G1, SH2, SC2, G2 = range(0, 48, 8)


def second_block(p):
    nc, T, V, A, G, S = p.nc, p.T, p.V, p.A, p.G, p.S
    p.place_ring("second", SLOT)
    rope = p.place("rope_half", [P, 2, TX])
    decay = p.place("decay", [P, HEADS, TX])
    masks = p.place("level_masks", [P, 8, P], I32)
    vec = p.place("layer_vectors", [P, 176])
    bounds = p.place("lower_bounds", [P, 2, HEADS])
    proj = p.place("proj_second", [P, 32, TX])
    room = p.top - 32 * TX * 4
    buffers = [p.place(f"norm_second{b}", [P, TX], at=room + b * 2048) for b in range(7)]
    p.norm_buffers = (buffers[1:4], buffers[4:7])
    square = p.place("square_second", [P, TX], at=room + 50 * 1024)
    act_hi = p.place("act_hi", [P, FFH, TX], F32R, at=room)
    act_lo = p.place("act_lo", [P, FFH, TX], F32R, at=room + FFH * 2048)
    conv = p.place("conv", [P, TX], at=room + 2 * FFH * 2048)
    actf = p.place("act_value", [P, TX], at=room + 2 * FFH * 2048 + 2048)
    conv_linear = nc.alloc_semaphore("conv_linear")
    conv_silu = nc.alloc_semaphore("conv_silu")
    tables_in = nc.alloc_semaphore("second_tables_landed")
    for dst, name in ((rope, "rope_half"), (decay, "decay"), (masks, "level_masks")):
        S.e.dma_start(dst[:, :, :], p.dram[name]).then_inc(tables_in, 16)

    lg, e = p.column("hgrn_lb_logits_2", 0, 8), p.small[:, 16:24]
    mx, tot = p.small[:, 24:28], p.small[:, 28:32]
    t = V.did(V.e.tensor_tensor(mx, lg[:, 0:4], lg[:, 4:8], ALU.max))
    for l in range(2):
        V.wait(t)
        V.did(V.e.tensor_tensor(e[:, 4 * l:4 * l + 4], lg[:, 4 * l:4 * l + 4], mx, ALU.subtract))
    A.wait(V.now())
    t = A.did(A.e.activation(e, e, ACT.Exp))
    V.wait(t)
    t = V.did(V.e.tensor_tensor(tot, e[:, 0:4], e[:, 4:8], ALU.add))
    V.wait(t)
    t = V.did(V.e.reciprocal(tot, tot))
    V.wait(t)
    for l in range(2):
        V.did(V.e.tensor_tensor(e[:, 4 * l:4 * l + 4], e[:, 4 * l:4 * l + 4], tot, ALU.mult))
    V.wait(V.now())
    t = V.did(V.e.tensor_tensor(mx, e[:, 0:4], e[:, 4:8], ALU.add))
    V.did(V.e.tensor_tensor(bounds[:, 0, :], e[:, 0:4], e[:, 0:4], ALU.subtract))
    V.wait(t)
    V.did(V.e.tensor_tensor(bounds[:, 1, :], mx, e[:, 0:4], ALU.subtract))
    for en in (V, A, T, G, S):
        en.wait(V.now(), (tables_in, 48))

    layer_sems = [x.sem for x in (T, V, A, G)] + [A.hold, S.hold, conv_linear, conv_silu,
                  *p.landed, *p.rounded, *p.split, *p.used, *p.freed]

    def new_layer():
        nc.all_engine_barrier()
        for s in layer_sems:
            G.e.sem_clear(s)
        nc.all_engine_barrier()

    new_layer()
    with nc.Fori(0, 2) as l:
        for en in (T, V, A, G):
            en.e.sem_inc(en.sem, 1)
            en.n = 1
        p.grant_slots(V)
        fields, at = {}, 0
        def take(name, src, n):
            nonlocal at
            fields[name] = vec[:, at:at + n]
            V.did(V.e.tensor_copy(vec[:, at:at + n], src))
            at += n
        c = p.col
        take("mod", p.mod2[:, bass.ds(l * 48, 48)], 48)
        take("norm1", p.colsf[:, bass.ds(l * 8 + c["norm1_w_2"], 8)], 8)
        take("norm2", p.colsf[:, bass.ds(l * 8 + c["norm2_w_2"], 8)], 8)
        take("head_gain_r", p.colsf[:, bass.ds(l * 4 + c["ret_norm_w_2"], 4)], 4)
        take("head_gain_h", p.colsf[:, bass.ds(l * 4 + c["hgrn_norm_w_2"], 4)], 4)
        take("conv_b", p.colsf[:, bass.ds(l * 22 + c["conv_b_2"], 22)], 22)
        take("conv_w", p.colsf[:, bass.ds(l * (c["conv_w1"] - c["conv_w0"]) + c["conv_w0"], 66)], 66)
        take("lb", bounds[:, bass.ds(l, 1), :].rearrange("p o h -> p (o h)"), 4)
        V.wait(V.now())
        gains = p.small[:, 32:48]
        keep = p.small[:, 48:52]
        mod = fields["mod"]
        V.did(V.e.scalar_tensor_tensor(gains[:, 0:8], mod[:, SC1:SC1 + 8], 1.0, fields["norm1"], ALU.add, ALU.mult))
        V.did(V.e.scalar_tensor_tensor(gains[:, 8:16], mod[:, SC2:SC2 + 8], 1.0, fields["norm2"], ALU.add, ALU.mult))
        vectors = V.did(V.e.tensor_scalar(keep, fields["lb"], -1.0, 1.0, ALU.mult, ALU.add))

        def columns_of(name, first):
            def source(i, j):
                return p.dram[name].rearrange("l (k p) n -> p l k n", p=P)[
                    :, bass.ds(l, 1), :, bass.ds(i * (2 * P) + (first + j) * P, P)].rearrange("p o k n -> p (o k) n")
            return source

        p.prime(KT)
        V.wait(vectors); A.wait(vectors)
        h_tiles = p.norm(TX, [vectors], [(0, TX, gains[:, 0:8], mod[:, SH1:SH1 + 8])], [])
        only_x = [(0, 0, TX)]

        def to_proj(first, func):
            def evac(i, j, use):
                A.wait((p.used[j], use))
                A.e.activation(flat(proj[:, bass.ds(i * 2 + (first + j), 1), :]), p.ps[:, j, :],
                               func).then_inc(p.freed[j], 1)
            return evac

        for first, n, func in ((0, 12, ACT.Identity), (12, 8, ACT.Silu), (20, 8, ACT.Identity), (28, 4, ACT.Silu)):
            p.linear(n, KT, columns_of("w_in_2", first), only_x, [],
                     to_proj(first, func), then_k=KT, ready_tiles=h_tiles if first == 0 else None)
        projected = [*p.banks_read, p.product_done]
        retention_done = retention(p, proj, rope, decay, projected)
        hgrn_done = hgrn(p, proj, masks, fields["lb"], keep, retention_done)
        h_tiles, mixed = mix_heads(p, proj, fields, hgrn_done)

        def residual(gate, squares):
            def evac(i, j, use):
                V.wait((p.used[j], use))
                xk = flat(p.xT[:, bass.ds(i * 2 + j, 1), X_])
                V.e.scalar_tensor_tensor(xk, p.ps[:, j, :], vec[:, bass.ds(i * 2 + (gate + j), 1)], xk,
                                         ALU.mult, ALU.add).then_inc(p.freed[j], 1)
                V.wait((p.freed[j], use))
                if squares:
                    p.add_squares(xk, X_, square[:, :])
            return evac

        V.wait(*mixed)
        V.wait(V.did(V.e.memset(p.ssq[:, X_], 0.0)))
        p.linear(8, KT, columns_of("w_out_2", 0), only_x, [], lambda i, j, use: None, residual(G1, True),
                 vec_counts=4, then_k=KT, ready_tiles=h_tiles)

        h_tiles = p.norm(TX, [*p.banks_read, V.now()], [(0, TX, gains[:, 8:16], mod[:, SH2:SH2 + 8])],
                         [*p.banks_read, p.product_done, *mixed])
        for half in range(2):
            u, done0 = p.uses, half * FFH
            act_free = [p.product_done]

            def gate_val(i, j, half=half):
                name = ("w_gate_2", "w_val_2")[j]
                return p.dram[name].rearrange("l (k p) n -> p l k n", p=P)[
                    :, bass.ds(l, 1), :, bass.ds(i * P + half * FFH * P, P)].rearrange("p o k n -> p (o k) n")

            def conv_col(i, k, half=half):
                at_ = k * 22 + half * FFH
                base = 48 + 8 + 8 + 4 + 4 + 22
                return vec[:, bass.ds(i + (base + at_), 1)]

            def bias_col(i, half=half):
                return vec[:, bass.ds(i + (48 + 8 + 8 + 4 + 4 + half * FFH), 1)]

            def act_side(i, j, use, u=u):
                if j == 0:
                    A.wait((p.used[0], use), (p.freed[1], use - 1))
                    A.e.activation(conv[:, :], p.ps[:, 0, :], ACT.Identity, bias=bias_col(i),
                                   scale=conv_col(i, 2)).then_inc(conv_linear, 1)
                else:
                    A.wait((p.freed[0], use))
                    A.e.activation(conv[:, :], conv[:, :], ACT.Silu).then_inc(conv_silu, 1)

            def vec_side(i, j, use, done0=done0):
                if j == 0:
                    V.wait((conv_linear, i + (done0 + 1)))
                    t = V.did(V.e.scalar_tensor_tensor(conv[:, 1:TX], p.ps[:, 0, 0:TX - 1], conv_col(i, 1),
                                                       conv[:, 1:TX], ALU.mult, ALU.add))
                    V.wait(t)
                    V.e.scalar_tensor_tensor(conv[:, 2:TX], p.ps[:, 0, 0:TX - 2], conv_col(i, 0), conv[:, 2:TX],
                                             ALU.mult, ALU.add).then_inc(p.freed[0], 1)
                else:
                    V.wait((conv_silu, i + (done0 + 1)), (p.used[1], use))
                    V.e.tensor_tensor(actf[:, :], conv[:, :], p.ps[:, 1, :], ALU.mult).then_inc(p.freed[1], 1)
                    V.wait((p.freed[1], use))
                    hi_t, lo_t = (flat(x[:, bass.ds(i, 1), :]) for x in (act_hi, act_lo))
                    t = V.did(V.e.tensor_copy(hi_t, actf[:, :]))
                    V.wait(t)
                    V.wait(V.did(V.e.tensor_tensor(lo_t, actf[:, :], hi_t.bitcast(F32), ALU.subtract)))

            V.wait(*act_free)
            p.linear(2 * FFH, KT, gate_val, only_x, [], act_side, vec_side, vec_counts=3, then_k=FFH,
                     ready_tiles=h_tiles if half == 0 else None)
            act_ready = [V.now()]

            def down(i, j, half=half):
                return p.dram["w_down_2"].rearrange("l (k p) n -> p l k n", p=P)[
                    :, bass.ds(l, 1), half * FFH:(half + 1) * FFH, bass.ds(i * (2 * P) + j * P, P)].rearrange(
                    "p o k n -> p (o k) n")

            p.act_pair = (act_hi, act_lo)
            if half == 1:
                V.wait(V.did(V.e.memset(p.ssq[:, X_], 0.0)))
            p.linear(8, FFH, down, only_x, act_ready, lambda i, j, use: None, residual(G2, half == 1),
                     vec_counts=4 if half == 1 else 0,
                     then_k=KT if half == 0 else None)
            p.act_pair = None
        for en in (T, V, A, G, S):
            en.wait(*p.banks_read, p.product_done)
        new_layer()
    for en in (T, V, A, G):
        en.e.sem_inc(en.sem, 1)
        en.n = 1
    final_norm(p, proj)


def retention(p, proj, rope, decay, ready):
    T, V, A, G, base = p.T, p.V, p.A, p.G, p.lower
    q = [p.place(f"r_{n}", [P, TX], at=base + 2048 * k) for k, n in enumerate(("q", "k"))]
    t2 = [p.place(f"r_t{k}", [P, TX], at=base + 4096 + 2048 * k) for k in range(2)]
    vt = p.place("r_vt", [P, TX], at=base + 8192)
    v = p.place("r_v", [P, 4, P], at=base + 10240)
    st = p.place("r_st", [P, 4, TX], at=base + 12288)
    for e in (T, V, A, G):
        e.wait(*ready)
    with passes(p.nc, HEADS, {T: 8, V: 10, A: 2, G: 1}) as i:
        start = [T.now(), V.now(), A.now(), G.now()]
        for e in (T, V, A, G):
            e.wait(*start)
        v_in = G.did(G.e.tensor_copy(vt[:, :], flat(proj[:, bass.ds(i + RV, 1), :])))
        rotated = []
        for k, tile in enumerate((RQ, RK)):
            x = flat(proj[:, bass.ds(i + tile, 1), :])
            turned = T.did(T.e.matmul(p.ps[:, 5 + k, :], p.rot_half, x, start=True, stop=True))
            a = V.did(V.e.tensor_tensor(q[k][:, :], x, rope[:, 0, :], ALU.mult))
            V.wait(turned)
            b = V.did(V.e.tensor_tensor(t2[k][:, :], p.ps[:, 5 + k, :], rope[:, 1, :], ALU.mult))
            V.wait(a, b)
            rotated.append(V.did(V.e.tensor_tensor(q[k][:, :], q[k][:, :], t2[k][:, :], ALU.add)))
        T.wait(v_in)
        for k in range(4):
            last = T.e.transpose(p.ps[:, 7, k * P:(k + 1) * P], vt[:, k * P:(k + 1) * P], p.ident)
        A.wait(T.did(last))
        v_ready = A.did(A.e.activation(v[:, :, :].rearrange("p k n -> p (k n)"), p.ps[:, 7, :], ACT.Copy))
        T.wait(*rotated)
        decayed = []
        for j in range(4):
            w = TX - j * P
            s = T.did(T.e.matmul(p.ps[:, j, 0:w], q[1][:, j * P:(j + 1) * P], q[0][:, j * P:TX], start=True, stop=True))
            V.wait(s)
            decayed.append(V.did(V.e.tensor_tensor(st[:, j, 0:w], p.ps[:, j, 0:w],
                                                   decay[:, bass.ds(i, 1), 0:w].rearrange("p o t -> p (o t)"),
                                                   ALU.mult)))
        T.wait(v_ready)
        for j in range(4):
            T.wait(decayed[j])
            last = T.e.matmul(p.ps[:, 4, j * P:TX], v[:, j, :], st[:, j, 0:TX - j * P], start=(j == 0), stop=(j == 3))
        A.wait(T.did(last))
        A.did(A.e.activation(flat(proj[:, bass.ds(i + RQ, 1), :]), p.ps[:, 4, :], ACT.Copy))
    return [T.now(), V.now(), A.now(), G.now()]


def hgrn(p, proj, masks, lb, keep, ready):
    T, V, A, G, base = p.T, p.V, p.A, p.G, p.lower
    N = HEADS * TX
    names = ("fwd", "bwd", "key", "q_level", "k_level")
    fwd, bwd, key, ql, kl = (p.place(f"h_{n}", [P, N], at=base + 8192 * k) for k, n in enumerate(names))
    diag = p.place("h_diag", [P, N], at=base + 8192 * 5)
    z = proj[:, HF:HF + 4, :].rearrange("p h t -> p (h t)")
    q = proj[:, HQ:HQ + 4, :].rearrange("p h t -> p (h t)")
    room = proj[:, RK:RK + 8, :].rearrange("p h t -> p (h t)")
    v = room[:, 0:N].rearrange("p (h k n) -> p h k n", h=4, k=4)
    near = room[:, N:2 * N]
    far = z
    for e in (T, V, A, G):
        e.wait(*ready)
    copied = []
    for h in range(HEADS):
        for k in range(4):
            last = T.e.transpose(p.ps[:, 4 + h, k * P:(k + 1) * P], proj[:, HI + h, k * P:(k + 1) * P], p.ident)
        t_ = T.did(last)
        A.wait(t_)
        copied.append(A.did(A.e.activation(v[:, h, :, :].rearrange("p k n -> p (k n)"), p.ps[:, 4 + h, :], ACT.Copy)))
    sp = A.did(A.e.activation(fwd[:, :], z, ACT.Sigmoid))
    sn = A.did(A.e.activation(kl[:, :], z, ACT.Sigmoid, scale=-1.0))
    V.wait(sp, sn)
    ones = V.did(V.e.memset(bwd[:, :], 1.0))
    for h in range(HEADS):
        cut = slice(h * TX, (h + 1) * TX)
        V.did(V.e.scalar_tensor_tensor(fwd[:, cut], kl[:, cut], lb[:, h:h + 1], fwd[:, cut], ALU.mult, ALU.add))
        last_key = V.did(V.e.tensor_scalar(key[:, cut], kl[:, cut], keep[:, h:h + 1], None, ALU.mult))
    zero = V.did(V.e.memset(diag[:, :], 0.0))
    scored, grown = {}, last_key
    ql_, kl_ = [ql[:, :], z], [kl[:, :], near]
    T.wait(*copied, last_key)
    taken = {}
    for level in range(len(LEVELS) + 1):
        set_ = 4 * (level % 2)
        ql, kl = ql_[level % 2], kl_[level % 2]
        if level == 0:
            rhs, lhs = q, key[:, :]
        else:
            if level >= 2:
                V.wait(scored[level - 2])
                G.wait(scored[level - 2])
            V.wait(grown)
            a = V.did(V.e.tensor_tensor(ql, q, fwd[:, :], ALU.mult))
            G.wait(grown, last_key)
            b = G.did(G.e.tensor_tensor(kl, key[:, :], bwd[:, :], ALU.mult))
            T.wait(a, b)
            rhs, lhs = ql, kl
            half = LEVELS[level - 1]
            fb, bb = (x[:, :].rearrange("p (b t) -> p b t", t=2 * half) for x in (fwd, bwd))
            shape = [P, N // (2 * half), half]
            G.wait(b)
            w = G.did(G.e.tensor_tensor(bb[:, :, 0:half], bb[:, :, 0:half],
                                        fb[:, :, 2 * half - 1:2 * half].broadcast_to(shape), ALU.mult))
            V.wait(a, w)
            grown = V.did(V.e.tensor_tensor(fb[:, :, half:2 * half], fb[:, :, half:2 * half],
                                            fb[:, :, half - 1:half].broadcast_to(shape), ALU.mult))
        if level >= 2:
            T.wait(taken[level - 2])
        for c in range(16):
            last = T.e.matmul(p.ps[:, set_ + c // 4, (c % 4) * P:(c % 4 + 1) * P], lhs[:, c * P:(c + 1) * P],
                              rhs[:, c * P:(c + 1) * P], start=True, stop=True)
        scored[level] = T.did(last)
        V.wait(scored[level], zero, *([taken[level - 1]] if level else []))
        taken[level] = V.did(V.e.copy_predicated(
            diag[:, :].rearrange("p (c n) -> p c n", n=P),
            masks[:, level:level + 1, :].broadcast_to([P, 16, P]),
            p.banks(set_, N).rearrange("p (c n) -> p c n", n=P)))
    ql, kl = ql_[0], kl_[0]
    V.wait(grown, scored[6])
    a = V.did(V.e.tensor_tensor(ql, q, fwd[:, :], ALU.mult))
    G.wait(grown, scored[6])
    b = G.did(G.e.tensor_tensor(kl, key[:, :], bwd[:, :], ALU.mult))
    T.wait(a, b, taken[6])
    for h in range(HEADS):
        for c in range(2):
            at = (4 * h + 2 * c) * P
            last = T.e.matmul(p.ps[:, h // 2, ((h % 2) * 2 + c) * P:((h % 2) * 2 + c + 1) * P], kl[:, at:at + P],
                              ql[:, at + P:at + 2 * P], start=True, stop=True)
    near_scored = T.did(last)
    A.wait(near_scored, scored[7])
    near_in = A.did(A.e.activation(near[:, 0:1024], p.banks(0, 1024), ACT.Copy))
    V.wait(a, b)
    fb, bb = (x[:, :].rearrange("p (b t) -> p b t", t=2 * P) for x in (fwd, bwd))
    shape = [P, N // (2 * P), P]
    w = V.did(V.e.tensor_tensor(bb[:, :, 0:P], bb[:, :, 0:P], fb[:, :, 2 * P - 1:2 * P].broadcast_to(shape), ALU.mult))
    V.wait(w)
    w = V.did(V.e.tensor_tensor(fb[:, :, P:2 * P], fb[:, :, P:2 * P], fb[:, :, P - 1:P].broadcast_to(shape), ALU.mult))
    V.wait(w, near_scored)
    a = V.did(V.e.tensor_tensor(ql[:, :], q, fwd[:, :], ALU.mult))
    G.wait(w, near_scored)
    b = G.did(G.e.tensor_tensor(kl[:, :], key[:, :], bwd[:, :], ALU.mult))
    T.wait(a, b, taken[7], near_in)
    for h in range(HEADS):
        for c in range(2):
            at = 4 * h * P
            last = T.e.matmul(p.ps[:, 4 + h, c * 256:(c + 1) * 256], kl[:, at + c * P:at + (c + 1) * P],
                              ql[:, at + 2 * P:at + 4 * P], start=True, stop=True)
    A.wait(T.did(last), scored[7])
    far_in = A.did(A.e.activation(far, p.banks(4, N), ACT.Copy))
    T.wait(near_in, far_in, taken[7])
    sources = lambda h, tq: (
        [(k, far[:, h * TX + k * 256 + (tq - 2) * P:][:, 0:P]) for k in (0, 1)] if tq >= 2 else []) + (
        [(tq - 1, near[:, (2 * h + tq // 2) * P:][:, 0:P])] if tq % 2 else []) + [
        (tq, diag[:, (4 * h + tq) * P:][:, 0:P])]
    for h in range(HEADS):
        for tq in range(4):
            terms = sources(h, tq)
            for n, (k, s) in enumerate(terms):
                last = T.e.matmul(p.ps[:, h, tq * P:(tq + 1) * P], v[:, h, k, :], s, start=(n == 0),
                                  stop=(n == len(terms) - 1))
        A.wait(T.did(last))
        A.did(A.e.activation(proj[:, HQ + h, :], p.ps[:, h, :], ACT.Copy))
    return [T.now(), V.now(), A.now(), G.now()]


def mix_heads(p, proj, fields, ready):
    T, V, A, G = p.T, p.V, p.A, p.G
    for e in (T, V, A, G):
        e.wait(*ready)
    items = [(proj[:, RQ + h, :], fields["head_gain_r"][:, h:h + 1], proj[:, RG + h, :]) for h in range(HEADS)] + \
            [(proj[:, HQ + h, :], fields["head_gain_h"][:, h:h + 1], proj[:, HG + h, :]) for h in range(HEADS)]
    return norm_gate_split(p, items, TX, [proj[:, RK + b, :] for b in range(3)])


def final_norm(p, proj):
    T, V, A, S = p.T, p.V, p.A, p.S
    y = [proj[:, 3 + b, :] for b in (0, 1)]
    rows = proj[:, 8:16, :].rearrange("p a t -> p (a t)").rearrange("p (t d) -> p t d", d=D)
    sums = p.token_sums(0, 0, p.ssq, TX, p.ones[:, 0:1])
    T.wait(p.inverse_roots(p.roots[:, 0:TX // P], p.ps[:, 0, 0:TX // P], D, [sums]))
    V.wait(p.spread(1, p.roots, 0, TX))
    turned, copied = [], []
    for k in range(KT):
        b = k % 2
        if k >= 2:
            V.wait(turned[k - 2])
            T.wait(copied[k - 2])
        T.wait(V.did(V.e.scalar_tensor_tensor(y[b], p.xT[:, k, X_], p.column("final_norm_w_2", k), p.ps[:, 1, :],
                                              ALU.mult, ALU.mult)))
        for t in range(4):
            last = T.e.transpose(p.ps[:, 2 + b, t * P:(t + 1) * P], y[b][:, t * P:(t + 1) * P], p.ident)
        turned.append(T.did(last))
        A.wait(turned[-1])
        copied.append(A.did(A.e.activation(rows[:, :, k * P:(k + 1) * P],
                                           p.ps[:, 2 + b, :].rearrange("p (t n) -> p t n", n=P), ACT.Copy)))
    S.wait(A.now())
    S.e.dma_start(p.dram["out"].rearrange("b (t p) d -> p (b t) d", p=P), rows).then_inc(p.out_stored, 16)
    S.wait((p.out_stored, 16))


def kernel(**inputs):
    import concourse.bacc as bacc
    from concourse.bass_utils import run_bass_kernel_spmd as run

    nc = bacc.Bacc("TRN2", target_bir_lowering=False, num_devices=1)
    arrays = {k: np.ascontiguousarray(v) for k, v in inputs.items()}
    arrays.update(tables())
    dram = {k: nc.dram_tensor(f"in_{k}", v.shape, mybir.dt.from_np(v.dtype), kind="ExternalInput").ap()
            for k, v in arrays.items()}
    dram["out"] = nc.dram_tensor("out", (1, TX, D), F32, kind="ExternalOutput").ap()
    p = Program(nc, dram)
    x_ready = first_block(p)
    for e in (p.T, p.V, p.A, p.G, p.S):
        e.wait(*x_ready, p.mod_last)
    second_block(p)
    r = run(nc, [{f"in_{k}": v for k, v in arrays.items()}], core_ids=[0])
    return r.results[0]["out"]
```

```python
import math
from contextlib import contextmanager

import numpy as np
import concourse.bass as bass
from concourse import mybir

F32 = mybir.dt.float32
F32R = mybir.dt.float32r
I32 = mybir.dt.int32
ALU = mybir.AluOpType
ACT = mybir.ActivationFunctionType
AX = mybir.AxisListType.X
ET = mybir.EngineType

P = 128
D = 1024
KT = D // P
TX = 512
TC = 256
TA = TX + TC
EPS = 1e-6
GRID_W = 64
QK = 64
HEADS = 4
FF = 2816
FFH = FF // P // 2
CHUNK_COLS = 256
LEVELS = (1, 2, 4, 8, 16, 32, 64)
SLOT = FFH * P


def tables():
    t = {}
    eye = np.eye(P, dtype=np.float32)
    t["ident"] = eye
    t["ones"] = np.ones((P, P), np.float32)
    half = np.kron(np.eye(2), np.ones((QK, QK)))
    t["ones_half"] = half.astype(np.float32)
    rot = np.zeros((P, P), np.float32)
    for base in range(0, P, 32):
        for i in range(16):
            rot[base + 16 + i, base + i] = -1.0
            rot[base + i, base + 16 + i] = 1.0
    t["rot_axial"] = rot
    rot = np.zeros((P, P), np.float32)
    for i in range(64):
        rot[64 + i, i] = -1.0
        rot[i, 64 + i] = 1.0
    t["rot_half"] = rot
    n = np.arange(64)
    ang = 2 * np.pi * np.outer(n, n) / 64
    t["dft_c"] = np.kron(np.eye(2), np.cos(ang) / 8).astype(np.float32)
    t["dft_ns"] = np.kron(np.eye(2), -np.sin(ang) / 8).astype(np.float32)
    square = ["ident", "ones", "ones_half", "rot_axial", "rot_half", "dft_c", "dft_ns"]
    out = {"squares": np.stack([t[k] for k in square], 1)}

    f4 = np.float32
    rows = TX // GRID_W
    row = np.repeat(np.arange(rows), GRID_W).astype(f4)
    col = np.tile(np.arange(GRID_W), rows).astype(f4)
    inv = (f4(10000.0) ** (-np.arange(0, 32, 2, dtype=f4) / f4(32))).astype(f4)
    ar, ac = row[:, None] * inv[None], col[:, None] * inv[None]
    ang = np.concatenate([ar, ar, ac, ac], -1).astype(f4)
    cs = np.stack([np.cos(ang).T, np.sin(ang).T], 1)
    out["rope_axial"] = np.concatenate([cs, cs], 0).astype(f4)

    def dft(length):
        k = np.arange(length)
        a = 2 * np.pi * (np.outer(k, k) % length) / length
        c = np.stack([np.cos(a), np.sin(a)]) / math.sqrt(length)
        return c.reshape(2, length // P, P, length).transpose(2, 0, 1, 3).astype(f4)
    out["dft_x"] = dft(TX)
    out["dft_ctx"] = dft(TC)

    def inv_counts(length):
        t_ = np.arange(length)
        r = []
        for w in (2, 4, 8, 16):
            lo, hi = w // 2, w - w // 2 - 1
            a, b = np.clip(t_ - lo, 0, length - 1), np.clip(t_ + hi, 0, length - 1)
            r.append(1.0 / (b - a + 1))
        r = np.array(r)
        return np.repeat(r.reshape(2, 2, 1, length), 64, 2).reshape(2, P, length).transpose(1, 0, 2)
    inv = (f4(10000.0) ** (-np.arange(0, P, 2, dtype=f4) / f4(P))).astype(f4)
    ang = (np.arange(TX, dtype=f4)[:, None] * inv[None]).astype(f4).T
    cs = np.stack([np.cos(ang), np.sin(ang)], 1)
    out["rope_half"] = np.concatenate([cs, cs], 0).astype(f4)
    gamma = 1.0 - 2.0 ** (-5.0 - np.arange(HEADS))
    dist = np.arange(TX)[None, :] - np.arange(P)[:, None]
    decay = np.where(dist[:, None] >= 0, gamma[None, :, None] ** np.maximum(dist[:, None], 0), 0.0)
    out["decay"] = (decay * P ** -0.5).astype(f4)
    k_, q_ = np.arange(P)[:, None], np.arange(P)[None, :]
    masks = [k_ == q_]
    for half in LEVELS:
        masks.append((k_ // (2 * half) == q_ // (2 * half)) & (k_ // half % 2 == 0) & (q_ // half % 2 == 1))
    out["level_masks"] = np.stack(masks, 1).astype(np.int32)
    out["inv_count"] = np.concatenate([inv_counts(TX), inv_counts(TC)], -1).astype(f4)
    return out


class Engine:

    def __init__(self, nc, e, kind, name, hold=False):
        self.e, self.kind, self.sem, self.n, self.pass_ = e, kind, nc.alloc_semaphore(name), 0, None
        self.hold = nc.alloc_semaphore(name + "_holds") if hold else None

    def wait(self, *tokens):
        for sem, value in tokens:
            self.e.wait_ge(sem, value)
        if self.hold and any(not isinstance(value, int) for _, value in tokens):
            self.e.sem_inc(self.hold, 1)
        return self.e

    def now(self):
        if self.pass_ is None:
            return (self.sem, self.n)
        i, per, base = self.pass_
        return (self.sem, i * per + (base + self.n))

    def did(self, instruction):
        instruction.then_inc(self.sem, 1)
        self.n += 1
        return self.now()


@contextmanager
def passes(nc, n, counts):
    with nc.Fori(0, n, engines=[e.kind for e in counts]) as i:
        for e, per in counts.items():
            e.pass_, e.n = (i, per, e.n), 0
        yield i
        for e, per in counts.items():
            assert e.n == per, (e.kind, "marks in a pass:", e.n, "declared", per)
            e.n, e.pass_ = e.pass_[2] + n * per, None


def pipeline(n, *steps):
    for turn in range(n + len(steps) - 1):
        for s in range(len(steps) - 1, -1, -1):
            if 0 <= turn - s < n:
                steps[s](turn - s)


class Program:

    def __init__(self, nc, dram):
        self.nc, self.dram = nc, dram
        self.T = Engine(nc, nc.tensor, ET.PE, "tensor_progress")
        self.V = Engine(nc, nc.vector, ET.DVE, "vector_progress")
        self.A = Engine(nc, nc.scalar, ET.Activation, "scalar_progress", hold=True)
        self.G = Engine(nc, nc.gpsimd, ET.Pool, "gpsimd_progress")
        self.S = Engine(nc, nc.sync, ET.SP, "sync_progress", hold=True)
        self.top = 16640
        sem = nc.alloc_semaphore
        self.consts_in = sem("consts_landed")
        self.x_in = sem("x_landed")
        self.out_stored = sem("out_stored")
        self.landed = [sem(f"weight_landed{j}") for j in (0, 1)]
        self.rounded = [sem(f"weight_rounded{j}") for j in (0, 1)]
        self.split = [sem(f"weight_split{j}") for j in (0, 1)]
        self.used = [sem(f"weight_used{j}") for j in (0, 1)]
        self.freed = [sem(f"bank_freed{j}") for j in (0, 1)]
        self.uses = 0
        self.mod_landed = [sem(f"mod_landed{j}") for j in (0, 1)]
        self.mod_summed = [sem(f"mod_summed{j}") for j in (0, 1)]
        self.mod_turned = [sem(f"mod_turned{j}") for j in (0, 1)]
        self.mod_uses = [0, 0]
        self.layer_sems = [*self.landed, *self.rounded, *self.split, *self.used, *self.freed]

        self.xT = self.place("xT", [P, KT, TA])
        self.lower = self.top
        self.h_hi = self.place("h_hi", [P, KT, TA], F32R)
        self.h_lo = self.place("h_lo", [P, KT, TA], F32R)
        self.squares = self.place("squares", [P, 7, P])
        (self.ident, self.ones, self.ones_half, self.rot_axial, self.rot_half,
         self.dft_c, self.dft_ns) = (self.squares[:, k, :] for k in range(7))
        self.cols = self.place("cols", [P, 5, P])
        self.colsf = self.cols[:, :, :].rearrange("p a b -> p (a b)")
        self.mod1 = self.place("mod1", [P, 2, 2, 24])
        self.mod2 = self.place("mod2", [P, 96])
        self.act_c = self.place("act_c", [P, 24])
        self.eps = self.place("eps", [P, 1])
        self.small = self.place("small", [P, 64])
        self.roots = self.place("inverse_roots", [P, 48])
        self.rope = self.place("rope", [P, 2, TX])
        self.ssq = self.place("summed_squares", [P, TA])
        self.ring_base = self.top
        self.place_ring("first", D)
        self.ps = nc.alloc_psum_tensor("ps", [P, 8, 512], F32)

    def place_ring(self, tag, floats):
        self.top = self.ring_base
        self.raw = [self.place(f"w_raw_{tag}{j}", [P, floats]) for j in (0, 1)]
        self.hi = [self.place(f"w_hi_{tag}{j}", [P, floats], F32R) for j in (0, 1)]
        self.lo = [self.place(f"w_lo_{tag}{j}", [P, floats], F32R) for j in (0, 1)]

    def place(self, name, shape, dt=F32, at=None):
        size = 4
        for s in shape[1:]:
            size *= s
        t = self.nc.alloc_sbuf_tensor_at(name, shape, dt, offset=self.top if at is None else at)
        if at is None:
            self.top += (size + 31) // 32 * 32
        return t

    def banks(self, b, n):
        return self.ps[:, :, :].rearrange("p b n -> p (b n)")[:, b * 512:b * 512 + n]

    def load_vectors(self):
        nc, d = self.nc, self.dram
        rows = self.place("vector_rows", [P, 5, P], at=self.lower)
        self.col, self.vectors_dma = {}, nc.alloc_semaphore("vectors_landed")
        plan = []
        r = 0
        def add(name, n, srcs):
            nonlocal r
            if r // P != (r + n - 1) // P:
                r = (r + P - 1) // P * P
            self.col[name] = r
            plan.append((r, n, srcs))
            r += n
        def rows_of(name, n):
            ap = d[name]
            letters = "abc"[:len(ap.shape)]
            flat = ap if len(ap.shape) == 1 else ap.rearrange(f"{' '.join(letters)} -> ({' '.join(letters)})")
            add(name, n, [(slice(0, P), flat.rearrange("(r p) -> r p", p=P))])
        rows_of("c", 8); rows_of("c_ctx", 8); rows_of("c_2", 8)
        rows_of("norm_g", 16); rows_of("b_mod", 48); rows_of("pool_scale", 4); rows_of("subln_g", 2)
        qk = d["qk_norm_g"].rearrange("l m k -> (l m) k")
        add("qk_norm_g", 4, [(slice(0, QK), qk), (slice(QK, P), qk)])
        rows_of("ret_norm_w_2", 8); rows_of("hgrn_norm_w_2", 8); rows_of("hgrn_lb_logits_2", 8)
        rows_of("norm1_w_2", 16); rows_of("norm2_w_2", 16); rows_of("final_norm_w_2", 8)
        rows_of("ada_b_2", 96); rows_of("conv_b_2", 44)
        add("conv_w0", 66, [(slice(0, P), d["conv_w_2"][0].rearrange("j (r p) -> (j r) p", p=P))])
        add("conv_w1", 66, [(slice(0, P), d["conv_w_2"][1].rearrange("j (r p) -> (j r) p", p=P))])
        assert r <= 5 * P, r
        zero = self.V.did(nc.vector.memset(rows[:, :, :], 0.0))
        nc.sync.wait_ge(*zero)
        n_dma = 0
        for at, n, srcs in plan:
            for where, src in srcs:
                nc.sync.dma_start(rows[at % P:at % P + n, at // P, where], src).then_inc(self.vectors_dma, 16)
                n_dma += 1
        self.T.wait((self.vectors_dma, 16 * n_dma), (self.consts_in, 16 * self.n_consts))
        for g in range(5):
            last = nc.tensor.transpose(self.banks(0, 5 * P)[:, g * P:(g + 1) * P], rows[:, g, :], self.ident)
        turned = self.T.did(last)
        self.A.wait(turned)
        self.cols_ready = self.A.did(nc.scalar.activation(self.colsf, self.banks(0, 5 * P), ACT.Identity))

    def column(self, name, k=0, n=1):
        return self.colsf[:, self.col[name] + k:self.col[name] + k + n]

    def load_constants(self):
        nc = self.nc
        self.lamv = self.place("lamv", [P, 2, 4, QK], at=self.lower + 8192)
        loads = [(self.squares, self.dram["squares"]), (self.rope, self.dram["rope_axial"])]
        for dst, src in loads:
            nc.sync.dma_start(dst[:, :, :], src).then_inc(self.consts_in, 16)
        lam = self.dram["lam_vecs"].rearrange("l a k -> (l a k)").rearrange("(o n) -> o n", o=1).broadcast_to([P, 512])
        nc.sync.dma_start(self.lamv[:, :, :, :].rearrange("p l a k -> p (l a k)"), lam).then_inc(self.consts_in, 16)
        self.n_consts = 3

    def grant_slots(self, evac):
        for j in (0, 1):
            self.T.e.sem_inc(self.used[j], 1)
            self.G.e.sem_inc(self.split[j], 1)
            evac.e.sem_inc(self.freed[j], 1)
        self.uses = 0

    def round_tile(self, j, use, k):
        self.A.wait((self.landed[j], use * 16), (self.used[j], use))
        self.A.e.activation(self.hi[j][:, 0:k * P], self.raw[j][:, 0:k * P], ACT.Copy).then_inc(self.rounded[j], 1)

    def split_tile(self, j, use, k):
        self.G.wait((self.rounded[j], use))
        self.G.e.tensor_tensor(self.lo[j][:, 0:k * P], self.raw[j][:, 0:k * P], self.hi[j][:, 0:k * P].bitcast(F32),
                               ALU.subtract).then_inc(self.split[j], 1)

    def prime(self, k):
        self.round_tile(0, self.uses + 1, k)
        self.split_tile(0, self.uses + 1, k)

    def linear(self, n, k, source, moving, ready, act_evac, vec_evac=None, vec_counts=0, then_k=None,
               mod=(), ready_tiles=None):
        nc, T, V, A = self.nc, self.T, self.V, self.A
        u, half = self.uses, n // 2
        with nc.Fori(0, half, engines=[ET.SP]) as i:
            for j in (0, 1):
                self.S.wait((self.split[j], i + (u + 1)))
                nc.sync.dma_start(self.raw[j][:, 0:k * P].rearrange("p (k n) -> p k n", k=k),
                                  source(i, j)).then_inc(self.landed[j], 16)
            for m in mod:
                self.mod_load(m, i)
        if half > 1:
            with nc.Fori(0, half - 1, engines=[ET.Pool]) as i:
                self.split_tile(1, i + (u + 1), k)
                self.split_tile(0, i + (u + 2), k)
        self.split_tile(1, u + half, k)
        if then_k:
            self.split_tile(0, u + half + 1, then_k)
        T.wait(*ready)
        with nc.Fori(0, half, engines=[ET.PE]) as i:
            for j in (0, 1):
                self.multiply(j, i + (u + 1), k, moving, ready_tiles)
            for m in mod:
                self.mod_turn(m, i)
        if mod or vec_evac:
            counts = {V: vec_counts + sum(self.mod_counts(m) for m in mod)}
            with passes(nc, half, counts) as i:
                for m in mod:
                    self.mod_sum(m, i)
                for j in (0, 1):
                    if vec_evac:
                        vec_evac(i, j, i + (u + 2))
                for m in mod:
                    self.mod_finish(m, i)
            self.mod_last = V.now()
            for m in mod:
                self.mod_uses[m["slot"]] += half
        if half > 1:
            with passes(nc, half - 1, {A: 0}) as i:
                self.round_tile(1, i + (u + 1), k)
                act_evac(i, 0, i + (u + 2))
                self.round_tile(0, i + (u + 2), k)
                act_evac(i, 1, i + (u + 2))
        self.round_tile(1, u + half, k)
        act_evac(half - 1, 0, u + half + 1)
        if then_k:
            self.round_tile(0, u + half + 1, then_k)
        act_evac(half - 1, 1, u + half + 1)
        self.finish(u + half)

    act_pair = None

    def multiply(self, j, use, k, moving, ready_tiles=None):
        self.T.wait((self.split[j], use + 1), (self.freed[j], use))
        h = self.act_pair or (self.h_hi, self.h_lo)
        for q in range(k):
            if ready_tiles:
                self.T.wait(*ready_tiles[q])
            w_hi, w_lo = self.hi[j][:, q * P:(q + 1) * P], self.lo[j][:, q * P:(q + 1) * P]
            for t, (w, which) in enumerate([(w_hi, 0), (w_hi, 1), (w_lo, 0)]):
                for bank, c, cols in moving:
                    last = self.T.e.matmul(self.ps[:, bank + j, 0:cols], w, h[which][:, q, c:c + cols],
                                           start=(q == 0 and t == 0), stop=(q == k - 1 and t == 2))
        last.then_inc(self.used[j], 1)

    def linear_beside(self, n, k, source, moving, act_evac, counts, steps):
        nc = self.nc
        u, half = self.uses, n // 2
        with nc.Fori(0, half, engines=[ET.SP]) as i:
            for j in (0, 1):
                self.S.wait((self.split[j], i + (u + 1)))
                nc.sync.dma_start(self.raw[j][:, 0:k * P].rearrange("p (k n) -> p k n", k=k),
                                  source(i, j)).then_inc(self.landed[j], 16)
        with passes(nc, half, counts) as i:
            before, between, after = steps(i)
            before()
            self.round_tile(1, i + (u + 1), k)
            self.split_tile(1, i + (u + 1), k)
            self.multiply(0, i + (u + 1), k, moving)
            act_evac(i, 0, i + (u + 2))
            between()
            self.round_tile(0, i + (u + 2), k)
            self.split_tile(0, i + (u + 2), k)
            self.multiply(1, i + (u + 1), k, moving)
            act_evac(i, 1, i + (u + 2))
            after()
        self.finish(u + half)

    def finish(self, uses):
        self.uses = uses
        self.product_done = (self.used[1], uses + 1)
        self.banks_read = [(self.freed[j], uses + 1) for j in (0, 1)]

    def mod_setup(self):
        self.pool_scratch = self.top
        self.mod_w = [self.place(f"mod_w{s}", [P, KT, CHUNK_COLS]) for s in (0, 1)]
        self.mod_acc = [[self.place(f"mod_acc{s}{v}", [P, CHUNK_COLS]) for v in (0, 1)] for s in (0, 1)]
        for s in (0, 1):
            self.V.e.sem_inc(self.mod_summed[s], 1)

    def mod_chunk(self, slot, source, outs):
        return {"slot": slot, "source": source, "outs": outs}

    def mod_counts(self, m):
        return (KT + 1) * len(m["outs"]) - 1

    def mod_use(self, m, i, add):
        return i + (self.mod_uses[m["slot"]] + add)

    def mod_load(self, m, i):
        s = m["slot"]
        self.S.wait((self.mod_summed[s], self.mod_use(m, i, 1)))
        self.S.e.dma_start(self.mod_w[s][:, :, :], m["source"](i)).then_inc(self.mod_landed[s], 16)

    def mod_sum(self, m, i):
        s, V = m["slot"], self.V
        V.wait((self.mod_landed[s], self.mod_use(m, i, 1) * 16))
        for v, (c, _, _) in enumerate(m["outs"]):
            acc, w = self.mod_acc[s][v][:, :], self.mod_w[s]
            t = V.did(V.e.tensor_scalar(acc, w[:, 0, :], self.act_c[:, c:c + 1], None, ALU.mult))
            for q in range(1, KT):
                V.wait(t)
                x = V.e.scalar_tensor_tensor(acc, w[:, q, :], self.act_c[:, c + q:c + q + 1], acc, ALU.mult, ALU.add)
                if q < KT - 1:
                    t = V.did(x)
                elif v == len(m["outs"]) - 1:
                    x.then_inc(self.mod_summed[s], 1)
                else:
                    V.did(x)

    def mod_turn(self, m, i):
        s = m["slot"]
        self.T.wait((self.mod_summed[s], self.mod_use(m, i, 2)))
        for v in range(len(m["outs"])):
            for q in range(2):
                k = v * 2 + q
                last = self.T.e.matmul(self.ps[:, 7 - s, k:k + 1], self.mod_acc[s][v][:, q * P:(q + 1) * P],
                                       self.ones[:, 0:1], start=True, stop=True)
        last.then_inc(self.mod_turned[s], 1)

    def mod_finish(self, m, i):
        s, V = m["slot"], self.V
        V.wait((self.mod_turned[s], self.mod_use(m, i, 1)))
        for v, (_, out, bias) in enumerate(m["outs"]):
            k = v * 2
            V.did(V.e.tensor_tensor(out(i), self.ps[:, 7 - s, k:k + 2], bias(i), ALU.add))

    def add_squares(self, x, cut, square):
        V = self.V
        V.wait(V.did(V.e.tensor_tensor(square, x, x, ALU.mult)))
        V.wait(V.did(V.e.tensor_tensor(self.ssq[:, cut], self.ssq[:, cut], square, ALU.add)))

    def token_sums(self, bank, first, x, t, ones):
        n = ones.shape[1]
        for q in range(t // P):
            at = first + q * n
            last = self.T.e.matmul(self.ps[:, bank, at:at + n], x[:, q * P:(q + 1) * P], ones, start=True, stop=True)
        return self.T.did(last)

    def inverse_roots(self, out, sums, n, ready):
        self.A.wait(*ready)
        self.V.wait(self.A.did(self.A.e.activation(out, sums, ACT.Sqrt, bias=self.eps[:, 0:1], scale=1.0 / n)))
        return self.V.did(self.V.e.reciprocal(out, out))

    def spread(self, bank, roots, first, t):
        for q in range(t // P):
            over = roots[:, first + q:first + q + 1].broadcast_to([P, P])
            last = self.T.e.matmul(self.banks(bank, t)[:, q * P:(q + 1) * P], over, self.ident, start=True, stop=True)
        return self.T.did(last)

    def norm(self, t, ready, segments, free):
        T, V, A, G = self.T, self.V, self.A, self.G
        tmp, h = self.norm_buffers
        for e in (T, V, A):
            e.wait(*ready, *free)
        sums = self.token_sums(6, 0, self.ssq, t, self.ones[:, 0:1])
        T.wait(self.inverse_roots(self.roots[:, 0:t // P], self.ps[:, 6, 0:t // P], D, [sums]))
        V.wait(self.spread(4, self.roots, 0, t))
        rstd = self.banks(4, t)
        normed, value, hi_done, lo_done = {}, {}, {}, {}

        def scale(k):
            if k >= 3:
                V.wait(hi_done[k - 3], value[k - 3])
            normed[k] = V.did(V.e.tensor_tensor(tmp[k % 3][:, 0:t], self.xT[:, k, 0:t], rstd, ALU.mult))

        def modulate(k):
            V.wait(normed[k])
            A.wait(normed[k])
            if k >= 3:
                V.wait(lo_done[k - 3])
            for first, count, gain, shift in segments:
                cut = slice(first, first + count)
                value[k] = V.did(V.e.tensor_scalar(h[k % 3][:, cut], tmp[k % 3][:, cut], gain[:, k:k + 1],
                                                   shift[:, k:k + 1], ALU.mult, ALU.add))
                hi_done[k] = A.did(A.e.activation(self.h_hi[:, k, cut], tmp[k % 3][:, cut], ACT.Identity,
                                                  bias=shift[:, k:k + 1], scale=gain[:, k:k + 1]))

        def rest(k):
            e = G if k % 3 else V
            e.wait(value[k], hi_done[k])
            lo_done[k] = e.did(e.e.tensor_tensor(self.h_lo[:, k, 0:t], h[k % 3][:, 0:t],
                                                 self.h_hi[:, k, 0:t].bitcast(F32), ALU.subtract))

        pipeline(KT, scale, modulate, rest)
        return [[hi_done[k], lo_done[k]] for k in range(KT)]


X_, C_ = slice(0, TX), slice(TX, TA)
TILE_A, TILE_B, TILE_Q, TILE_K, TILE_V, TILE_G = 0, 2, 4, 8, 12, 16


def load_x(p):
    nc, T, A = p.nc, p.T, p.A
    rows = p.place("x_rows", [P, TA // P, D], at=p.lower + 24576)
    nc.sync.dma_start(rows[:, 0:4, :], p.dram["x"].rearrange("b (t p) d -> p (b t) d", p=P)).then_inc(p.x_in, 16)
    nc.sync.dma_start(rows[:, 4:6, :], p.dram["ctx"].rearrange("b (t p) d -> p (b t) d", p=P)).then_inc(p.x_in, 16)
    T.wait((p.x_in, 32), (p.consts_in, 16 * p.n_consts))
    copied = []
    for k in range(KT):
        b = 2 + 2 * (k % 2)
        if k >= 2:
            T.wait(copied[k - 2])
        for t in range(TA // P):
            last = T.e.transpose(p.banks(b, TA)[:, t * P:(t + 1) * P], rows[:, t, k * P:(k + 1) * P], p.ident)
        A.wait(T.did(last))
        copied.append(A.did(A.e.activation(p.xT[:, k, :], p.banks(b, TA), ACT.Copy)))
    return copied[-1]


MOD_COLS = 512
MOD_CHUNKS = 3 * D // MOD_COLS
MOD_SLOTS = 4


def load_first_modulation(p, room):
    p.mod_chunk_in = [p.nc.alloc_semaphore(f"first_mod_landed{c}") for c in range(MOD_CHUNKS)]
    p.mod_chunks = [p.place(f"first_mod{c}", [P, KT, MOD_COLS], at=room + c * 4 * KT * MOD_COLS)
                    for c in range(MOD_SLOTS)] + [p.place("first_mod4", [P, KT, MOD_COLS], at=p.pool_scratch)]
    p.mod_chunks.append(p.mod_chunks[0])
    for c in range(MOD_SLOTS + 1):
        load_mod_chunk(p, c)


def load_mod_chunk(p, c):
    source = p.dram["w_mod"][0].rearrange("(k p) n -> p k n", p=P)[:, :, c * MOD_COLS:(c + 1) * MOD_COLS]
    p.S.e.dma_start(p.mod_chunks[c][:, :, :], source).then_inc(p.mod_chunk_in[c], 16)


def first_modulation(p):
    T, V, A, S = p.T, p.V, p.A, p.S
    rows = [p.place(f"first_mod_rows{b}", [P, MOD_COLS], at=p.lower + 14336 + 2048 * b) for b in (0, 1)]
    per = MOD_COLS // P
    product, copied, turned = {}, {}, {}

    def multiply(c):
        T.wait((p.mod_chunk_in[c], 16))
        if c >= 2:
            T.wait(copied[c - 2])
        for k in range(KT):
            last = T.e.matmul(p.ps[0:2, 6 + c % 2, :], p.act_c[:, k:2 * KT:KT], p.mod_chunks[c][:, k, :],
                              start=(k == 0), stop=(k == KT - 1))
        product[c] = T.did(last)

    def copy(c):
        A.wait(product[c])
        if c >= 2:
            A.wait(turned[c - 2])
        copied[c] = A.did(A.e.activation(rows[c % 2][0:2, :], p.ps[0:2, 6 + c % 2, :], ACT.Copy))

    def turn(c):
        T.wait(copied[c])
        for q in range(per):
            at = 2 * (c * per + q)
            last = T.e.matmul(p.ps[:, 0, at:at + 2], rows[c % 2][0:2, q * P:(q + 1) * P], p.ident[0:2, 0:2],
                              start=True, stop=True)
        turned[c] = T.did(last)

    pipeline(MOD_CHUNKS - 1, multiply, copy, turn)
    S.wait(product[0])
    load_mod_chunk(p, MOD_CHUNKS - 1)
    S.wait(product[MOD_SLOTS])
    for step in (multiply, copy, turn):
        step(MOD_CHUNKS - 1)
    V.wait(turned[MOD_CHUNKS - 1])
    for v in (0, 1):
        p.mod_last = V.did(V.e.tensor_tensor(p.mod1[:, 0, v, :], p.ps[:, 0, v:6 * KT:2], p.column("b_mod", 0, 24),
                                             ALU.add))


def first_block(p):
    nc, T, V, A = p.nc, p.T, p.V, p.A
    p.load_constants()
    p.load_vectors()
    p.mod_setup()
    eps = V.did(nc.vector.memset(p.eps[:, :], EPS))
    x_there = load_x(p)
    qk_gain = p.place("qk_gain", [P, 2, 8])
    wblk = p.place("group_weights", [P, 2, 2, 2, P])
    proj = p.place("proj", [P, 24, TA])
    load_first_modulation(p, p.top - 24 * TA * 4)

    A.wait(p.cols_ready)
    c_there = A.did(nc.scalar.activation(p.act_c[:, :], p.column("c", 0, 24), ACT.Silu))
    lam, dots = p.small[:, 0:2], p.small[:, 2:6]
    prod = p.place("lam_products", [P, 2, 2, QK], at=p.lower + 12288)
    V.wait((p.consts_in, 16 * p.n_consts))
    t = V.did(V.e.tensor_tensor(prod[:, :, :, :], p.lamv[:, :, 0:4:2, :], p.lamv[:, :, 1:4:2, :], ALU.mult))
    V.wait(t)
    t = V.did(V.e.tensor_reduce(dots, prod[:, :, :, :].rearrange("p l a k -> p (l a) k"), AX, ALU.add))
    A.wait(t)
    t = A.did(A.e.activation(dots, dots, ACT.Exp))
    V.wait(t)
    for l in range(2):
        init = 0.8 - 0.6 * math.exp(-0.3 * l)
        t = V.did(V.e.scalar_tensor_tensor(lam[:, l:l + 1], dots[:, 2 * l + 1:2 * l + 2], -init,
                                           dots[:, 2 * l:2 * l + 1], ALU.add, ALU.subtract))
    lam_ready = t
    sub_gain = p.small[:, 8:10]
    V.wait(p.cols_ready)
    for l in range(2):
        for m in range(2):
            for r in range(4):
                t = V.did(V.e.tensor_copy(qk_gain[:, l, 4 * m + r:4 * m + r + 1], p.column("qk_norm_g", 2 * l + m)))
        init = 0.8 - 0.6 * math.exp(-0.3 * l)
        t = V.did(V.e.tensor_scalar(sub_gain[:, l:l + 1], p.column("subln_g", l), 1.0 - init, None, ALU.mult))
    gains_ready = t

    t = V.did(V.e.memset(wblk[:, :, :, :, :].rearrange("p a b c d -> p (a b c d)"), 0.0))
    nc.sync.wait_ge(*t)
    groups_in = nc.alloc_semaphore("group_weights_landed")
    for which, name in ((0, "w_pool"), (1, "w_fourier")):
        for l in range(2):
            for g in range(4):
                half = slice(64 * (g % 2), 64 * (g % 2) + 64)
                nc.sync.dma_start(wblk[half, l, which, g // 2, half], p.dram[name][l, g]).then_inc(groups_in, 16)
    groups_ready = (groups_in, 16 * 16)

    w_mod, ada = p.dram["w_mod"], p.dram["ada_w_2"]

    def mod1(l, slot, chunk):
        def source(i):
            return w_mod[l].rearrange("(k p) n -> p k n", p=P)[:, :, bass.ds(chunk(i) * CHUNK_COLS, CHUNK_COLS)]
        outs = [(8 * v, lambda i, v=v: p.mod1[:, l, v, bass.ds(chunk(i) * 2, 2)],
                 lambda i: p.colsf[:, bass.ds(chunk(i) * 2 + (p.col["b_mod"] + 24 * l), 2)]) for v in (0, 1)]
        return p.mod_chunk(slot, source, outs)

    def mod2(l, slot, chunk):
        def source(i):
            return ada[l].rearrange("(k p) n -> p k n", p=P)[:, :, bass.ds(chunk(i) * CHUNK_COLS, CHUNK_COLS)]
        return p.mod_chunk(slot, source, [
            (16, lambda i: p.mod2[:, bass.ds(chunk(i) * 2 + 48 * l, 2)],
             lambda i: p.colsf[:, bass.ds(chunk(i) * 2 + (p.col["ada_b_2"] + 48 * l), 2)])])

    V.wait(c_there)
    T.wait(c_there)
    square = p.place("square", [P, TA], at=p.top - (24 - TILE_G) * TA * 4 + 7 * 3072)
    V.wait(x_there)
    V.wait(V.did(V.e.memset(p.ssq[:, :], 0.0)))
    for k in range(KT):
        p.add_squares(p.xT[:, k, :], slice(0, TA), square[:, :])
    first_modulation(p)

    at = p.top - (24 - TILE_G) * TA * 4
    p.mix_scratch = at - (TILE_G - TILE_K) * TA * 4
    buffers = [p.place(f"norm{b}", [P, TA], at=at + b * 3072) for b in range(1, 7)]
    p.norm_buffers = (buffers[0:3], buffers[3:6])
    gain = p.place("norm_gain", [P, 2, 2, 8])

    p.grant_slots(A)
    x_ready, free = [x_there, eps], [x_there, p.mod_last, lam_ready]
    for l in range(2):
        update_ctx = l == 0
        V.wait(p.mod_last)
        for v in range(2):
            t = V.did(V.e.scalar_tensor_tensor(gain[:, l, v, :], p.mod1[:, l, v, 8:16], 1.0,
                                               p.column("norm_g", 8 * l, 8), ALU.add, ALU.mult))
        gain_ready = t
        if l == 0:
            p.prime(KT)
        V.wait(gain_ready); A.wait(gain_ready)
        segments = [(0, TX, gain[:, l, 0, :], p.mod1[:, l, 0, 0:8]), (TX, TC, gain[:, l, 1, :], p.mod1[:, l, 1, 0:8])]
        h_tiles = p.norm(TA, [*x_ready, V.now()], segments, free)

        def w_in(first):
            return lambda i, j: p.dram["w_in"][l].rearrange("(k p) n -> p k n", p=P)[
                :, :, bass.ds(i * (2 * P) + (first + j) * P, P)]

        def to_proj(first, func, ctx):
            def evac(i, j, use):
                A.wait((p.used[j], use))
                x = A.e.activation(proj[:, bass.ds(i * 2 + (first + j), 1), X_].rearrange("p o t -> p (o t)"),
                                   p.ps[:, j, :], func)
                if ctx:
                    x = A.e.activation(proj[:, bass.ds(i * 2 + (first + j), 1), C_].rearrange("p o t -> p (o t)"),
                                       p.ps[:, 2 + j, 0:TC], func)
                x.then_inc(p.freed[j], 1)
            return evac

        both = [(0, 0, TX), (2, TX, TC)]
        only_x = [(0, 0, TX)]
        if l == 0:
            p.linear(16, KT, w_in(0), both, [], to_proj(0, ACT.Identity, True), then_k=KT, ready_tiles=h_tiles,
                     mod=[mod1(1, 0, lambda i: i), mod2(0, 1, lambda i: i)])
            p.linear(8, KT, w_in(16), both, [], to_proj(16, ACT.Silu, True),
                     mod=[mod1(1, 0, lambda i: i + 8), mod2(0, 1, lambda i: i + 8)])
        else:
            p.linear(8, KT, w_in(0), only_x, [], to_proj(0, ACT.Identity, False), then_k=KT, ready_tiles=h_tiles,
                     mod=[mod2(0, 0, lambda i: i + 12), mod2(1, 1, lambda i: i)])
            p.linear(8, KT, w_in(8), both, [], to_proj(8, ACT.Identity, True), then_k=KT,
                     mod=[mod2(0, 0, lambda i: i + 16), mod2(1, 1, lambda i: i + 4)])
            p.linear(8, KT, w_in(16), only_x, [], to_proj(16, ACT.Silu, False),
                     mod=[mod2(0, 0, lambda i: i + 20), mod2(1, 1, lambda i: i + 8)])
        projected = [*p.banks_read, p.mod_last, p.product_done]
        t = TA if update_ctx else TX
        load_tables(p, l, projected)
        qk_done = norm_rope(p, l, proj, qk_gain, projected, gains_ready)
        fourier(p, l, proj, wblk, t, qk_done, groups_ready)
        pool_done = pooling(p, l, proj, wblk, t, qk_done)
        p.S.wait(*pool_done)
        heads_done = attention(p, l, proj, lam, t, pool_done)
        p.prime(KT)
        h_tiles, mixed = mix(p, l, proj, sub_gain, t, heads_done)

        def w_out(i, j):
            return p.dram["w_out"][l].rearrange("(k p) n -> p k n", p=P)[:, :, bass.ds(i * (2 * P) + j * P, P)]

        def residual(i, j, use):
            V.wait((p.used[j], use))
            xk = p.xT[:, bass.ds(i * 2 + j, 1), X_].rearrange("p o t -> p (o t)")
            x = V.e.scalar_tensor_tensor(xk, p.ps[:, j, :], p.mod1[:, l, 0, bass.ds(i * 2 + (16 + j), 1)], xk,
                                         ALU.mult, ALU.add)
            if update_ctx:
                xk = p.xT[:, bass.ds(i * 2 + j, 1), C_].rearrange("p o t -> p (o t)")
                x = V.e.scalar_tensor_tensor(xk, p.ps[:, 2 + j, 0:TC], p.mod1[:, l, 1, bass.ds(i * 2 + (16 + j), 1)],
                                             xk, ALU.mult, ALU.add)
            x.then_inc(p.freed[j], 1)
            V.wait((p.freed[j], use))
            whole = slice(0, TA if update_ctx else TX)
            p.add_squares(flat(p.xT[:, bass.ds(i * 2 + j, 1), whole]), whole, square[:, whole])

        V.wait(*mixed)
        V.wait(V.did(V.e.memset(p.ssq[:, 0:t], 0.0)))
        mods = ([mod2(1, 1, lambda i: i + 12)] if l == 0 else
                [mod2(1, 0, lambda i: i + 16), mod2(1, 1, lambda i: i + 20)])
        p.linear(8, KT, w_out, both if update_ctx else only_x, [], lambda i, j, use: None, residual, vec_counts=4,
                 ready_tiles=h_tiles,
                 then_k=KT if l == 0 else None, mod=mods)
        x_ready, free = [*p.banks_read, V.now()], [*p.banks_read, p.mod_last, p.product_done, *mixed]
    return x_ready


def load_tables(p, l, ready):
    if l == 0:
        p.tables_in = p.nc.alloc_semaphore("tables_landed")
    p.dft_x = p.place(f"dft_x{l}", [P, 2, 4, TX], at=p.lower)
    p.dft_ctx = p.place(f"dft_ctx{l}", [P, 2, 2, TC], at=p.lower + 16384)
    p.inv_count = p.place(f"inv_count{l}", [P, 2, TA], at=p.lower + 20480)
    p.S.wait(*ready)
    p.S.e.dma_start(p.dft_x[:, :, :, :], p.dram["dft_x"]).then_inc(p.tables_in, 16)
    p.S.e.dma_start(p.dft_ctx[:, :, :, :], p.dram["dft_ctx"]).then_inc(p.tables_in, 16)
    p.S.e.dma_start(p.inv_count[:, :, :], p.dram["inv_count"]).then_inc(p.tables_in, 16)
    p.tables_ready = (p.tables_in, 48 * (l + 1))
    p.scratch = p.lower + 26624


def flat(ap):
    return ap.rearrange("p o t -> p (o t)")


def norm_rope(p, l, proj, qk_gain, ready, gains_ready):
    T, V, A, G, base = p.T, p.V, p.A, p.G, p.scratch
    sq = [p.place(f"qk_sq{l}{j}", [P, TA], at=base + j * 3072) for j in range(3)]
    cs = [p.place(f"qk_cos{l}{j}", [P, TX], at=base + 9216 + j * 2048) for j in range(3)]
    sn = [p.place(f"qk_sin{l}{j}", [P, TX], at=base + 15360 + j * 2048) for j in range(3)]
    wide = sq[0:2]
    per = 2 * TA // P
    for e in (A, V, T, G):
        e.wait(*ready, gains_ready)
    with passes(p.nc, 2, {T: 12, V: 13, A: 9, G: 4}) as i:
        start = [e.now() for e in (T, V, A, G)]
        for e in (T, V, A, G):
            e.wait(*start)
        tile = [flat(proj[:, bass.ds(i * 4 + (TILE_Q + k), 1), :]) for k in range(4)]
        tile_x = [flat(proj[:, bass.ds(i * 4 + (TILE_Q + k), 1), X_]) for k in range(4)]
        squared, summed, over, normed, turned, cosine, done = ({} for _ in range(7))
        for k in range(4):
            if k >= 3:
                A.wait(summed[k - 3])
            squared[k] = A.did(A.e.activation(sq[k % 3][:, :], tile[k], ACT.Square))
            T.wait(squared[k])
            summed[k] = p.token_sums(6, k * per, sq[k % 3], TA, p.ones_half[:, 0:P:QK])
        roots = p.inverse_roots(p.roots[:, 0:4 * per], p.ps[:, 6, 0:4 * per], QK, [summed[3]])

        def norm(k):
            b = 3 * (k % 2)
            A.wait(roots)
            if k >= 2:
                A.wait(over[k - 2])
                T.wait(normed[k - 2])
            T.wait(A.did(A.e.activation(
                wide[k % 2][:, :].rearrange("p (a o) -> p a o", o=QK),
                p.roots[:, k * per:(k + 1) * per].rearrange("p (a o) -> p a o", o=1).broadcast_to([P, per, QK]),
                ACT.Copy)))
            for c in range(TA // P):
                last = T.e.transpose(p.banks(b, TA)[:, c * P:(c + 1) * P], wide[k % 2][:, c * P:(c + 1) * P], p.ident)
            over[k] = T.did(last)
            V.wait(over[k])
            normed[k] = V.did(V.e.scalar_tensor_tensor(tile[k], tile[k], qk_gain[:, l, bass.ds(i * 4 + k, 1)],
                                                       p.banks(b, TA), ALU.mult, ALU.mult))

        def turn(k):
            T.wait(normed[k])
            if k >= 2:
                T.wait(done[k - 2])
            turned[k] = T.did(T.e.matmul(p.ps[:, 3 * (k % 2) + 2, :], p.rot_axial, tile_x[k], start=True, stop=True))
            G.wait(normed[k])
            if k >= 3:
                G.wait(done[k - 3])
            cosine[k] = G.did(G.e.tensor_tensor(cs[k % 3][:, :], tile_x[k], p.rope[:, 0, :], ALU.mult))

        def combine(k):
            V.wait(turned[k], normed[k])
            s = V.did(V.e.tensor_tensor(sn[k % 3][:, :], p.ps[:, 3 * (k % 2) + 2, :], p.rope[:, 1, :], ALU.mult))
            V.wait(s, cosine[k])
            done[k] = V.did(V.e.tensor_tensor(tile_x[k], cs[k % 3][:, :], sn[k % 3][:, :], ALU.add))

        pipeline(4, norm, turn, combine)
    return [e.now() for e in (T, V, A, G)]


def fourier(p, l, proj, wblk, t, ready, groups_ready):
    T, A, base = p.T, p.A, p.scratch
    tok = p.place(f"f_tok{l}", [P, TA // P, 2, P], at=base)
    bx = p.place(f"f_bx{l}", [P, 2, 2, TX], at=base + 6144)
    cw = p.place(f"f_cw{l}", [P, 2, 2, P], at=base + 14336)
    T.wait(groups_ready, *ready)
    A.wait(*ready)
    for g in range(2):
        for s, m in enumerate((p.dft_c, p.dft_ns)):
            last = T.e.matmul(p.ps[:, 6, (2 * g + s) * P:(2 * g + s + 1) * P], m, wblk[:, l, 1, g, :],
                              start=True, stop=True)
    A.wait(T.did(last))
    folded = A.did(A.e.activation(cw[:, :, :, :].rearrange("p g s n -> p (g s n)"), p.ps[:, 6, :], ACT.Copy))
    copied = []
    for g in range(2):
        for q in range(t // P):
            last = T.e.transpose(p.banks(2 * g, t)[:, q * P:(q + 1) * P],
                                 proj[:, TILE_A + g, q * P:(q + 1) * P], p.ident)
        A.wait(T.did(last))
        copied.append(A.did(A.e.activation(tok[:, 0:t // P, g, :],
                                           p.banks(2 * g, t).rearrange("p (q n) -> p q n", n=P), ACT.Copy)))
    T.wait(*copied, folded, p.tables_ready)
    for first, length, tab in ((0, TX, p.dft_x), (TX, TC, p.dft_ctx)):
        if first >= t:
            continue
        T.wait(A.now())
        moved = []
        for g in range(2):
            for s in range(2):
                for q in range(length // P):
                    last = T.e.matmul(p.ps[:, 2 * g + s, 0:length], tok[:, first // P + q, g, :], tab[:, s, q, :],
                                      start=(q == 0), stop=(q == length // P - 1))
                A.wait(T.did(last))
                moved.append(A.did(A.e.activation(bx[:, g, s, 0:length], p.ps[:, 2 * g + s, 0:length], ACT.Copy)))
        T.wait(*moved)
        for g in range(2):
            for s in range(2):
                last = T.e.matmul(p.ps[:, 4 + g, 0:length], cw[:, g, s, :], bx[:, g, s, 0:length],
                                  start=(s == 0), stop=(s == 1))
            A.wait(T.did(last))
            A.did(A.e.activation(proj[:, TILE_A + g, first:first + length], p.ps[:, 4 + g, 0:length], ACT.Copy))
    return [T.now(), A.now()]


def pooling(p, l, proj, wblk, t, ready):
    T, V, A, base = p.T, p.V, p.A, p.pool_scratch
    edge, width = 16, TX + 32
    pad = p.place(f"pool_pad{l}", [P, 3, width], at=base)
    mean = p.place(f"pool_mean{l}", [P, 2, TA], at=base + 12 * width)
    V.wait(*ready, p.tables_ready)
    low, high, whole = slice(0, 64), slice(64, P), slice(0, P)
    parts = [(first, length, g) for first, length in ((0, TX), (TX, TC)) if first < t for g in range(2)]
    done, free = {}, []
    for first, length, g in parts:
        cut = slice(first, first + length)
        if g == 0:
            V.wait(*free)
            V.wait(V.did(V.e.memset(pad[:, :, :].rearrange("p a w -> p (a w)"), 0.0)))
        V.wait(*free)
        c = V.did(V.e.tensor_copy(pad[:, 0, edge:edge + length], proj[:, TILE_B + g, cut]))
        plan = [(1, 0, -1, 0, 7, whole), (2, 1, -1, 1, 6, high if g == 0 else whole)]
        if g == 1:
            plan += [(1, 2, -2, 2, 4, whole), (2, 1, -4, 4, 0, high)]
        for dst, src, d0, d1, reach, rows in plan:
            a, b = edge - reach, edge + length + reach
            V.wait(c)
            c = V.did(V.e.tensor_tensor(pad[rows, dst, a:b], pad[rows, src, a + d0:b + d0],
                                        pad[rows, src, a + d1:b + d1], ALU.add))
        free = []
        for rows, src in ((low, 1), (high, 2)):
            V.wait(c)
            V.wait(V.did(V.e.tensor_tensor(mean[rows, g, cut], pad[rows, src, edge:edge + length],
                                           p.inv_count[rows, g, cut], ALU.mult)))
            free.append(V.did(V.e.tensor_tensor(mean[rows, g, cut], mean[rows, g, cut],
                                                pad[rows, 0, edge:edge + length], ALU.subtract)))
        done[first, g] = free
    for first, length, g in parts:
        cut = slice(first, first + length)
        T.wait(*done[first, g], A.now())
        A.wait(T.did(T.e.matmul(p.ps[:, 6 + g, 0:length], wblk[:, l, 0, g, :], mean[:, g, cut], start=True, stop=True)))
        A.did(A.e.activation(proj[:, TILE_B + g, cut], p.ps[:, 6 + g, 0:length], ACT.Copy,
                             scale=p.column("pool_scale", 2 * l + g)))
    return [V.now(), A.now(), T.now()]


def attention(p, l, proj, neg_lam, t, ready):
    T, V, A, G, base = p.T, p.V, p.A, p.G, p.lower
    vt = p.ssq
    st = p.roots[:, 0:16].rearrange("p (b n) -> p b n", b=2)
    v = p.place(f"a_v{l}", [P, TA // P, P], at=base)
    prob = [[p.place(f"a_p{l}{b}{m}", [P, TA], at=base + (2 * b + m + 1) * 3072) for m in (0, 1)] for b in (0, 1)]
    pt = p.place(f"a_pt{l}", [P, TA // P, TA], at=base + 5 * 3072)
    q_pair = [p.place(f"a_q{l}{m}", [P, TA], F32R, at=base + (11 + m) * 3072) for m in (0, 1)]
    k_hi = [p.place(f"a_khi{l}{m}", [P, TA], F32R, at=base + (13 + m) * 3072) for m in (0, 1)]
    k_lo = p.place(f"a_klo{l}", [P, TA], F32R, at=base + 15 * 3072)
    queries = t // P
    for e in (T, V, A, G):
        e.wait(*ready)
    n = queries
    outs = 1 if t == TX else 2
    halves = [slice(0, QK), slice(QK, P)]

    def prepare(h, free):
        tile = lambda first: flat(proj[:, h + first:h + first + 1, :] if isinstance(h, int)
                                  else proj[:, bass.ds(h + first, 1), :])
        q, k, vv = tile(TILE_Q), tile(TILE_K), tile(TILE_V)
        for e in (V, A, G):
            e.wait(*free)
        high, low = {}, []
        for m in (0, 1):
            own, other = halves[m], halves[1 - m]
            high["q", m] = A.did(A.e.activation(q_pair[m][own, 0:t], q[own, 0:t], ACT.Copy))
            high["k", m] = V.did(V.e.tensor_copy(k_hi[m][own, :], k[own, :]))
            low.append(A.did(A.e.activation(k_hi[m][other, :], k[own, :], ACT.Copy)))
        for m in (0, 1):
            own, other = halves[m], halves[1 - m]
            V.wait(high["q", m])
            low.append(V.did(V.e.tensor_tensor(q_pair[m][other, 0:t], q[own, 0:t], q_pair[m][own, 0:t].bitcast(F32),
                                               ALU.subtract)))
            G.wait(high["k", m])
            low.append(G.did(G.e.tensor_tensor(k_lo[own, :], k[own, :], k_hi[m][own, :].bitcast(F32),
                                               ALU.subtract)))
        low.append(A.did(A.e.activation(vt[:, :], vv, ACT.Copy)))

    def head(i, following):
        start = [e.now() for e in (T, V, A, G)]
        for e in (T, V, A):
            e.wait(*start)
        soft, turned, exps, moved, combined = {}, {}, {}, {}, {}
        ring = lambda q, m: 2 * ((2 * q + m) % 3)

        def keys(q):
            return (0, TA) if q < TX // P else (TX, TC)

        def scores(q):
            first, count = keys(q)
            cut = slice(q * P, (q + 1) * P)
            for m in (0, 1):
                if 2 * q + m >= 3:
                    T.wait(exps[2 * q + m - 3])
                for b in range(0, count, 512):
                    w = min(512, count - b)
                    out, keys_ = p.ps[:, ring(q, m) + b // 512, 0:w], slice(first + b, first + b + w)
                    T.e.matmul(out, q_pair[m][:, cut], k_hi[m][:, keys_], start=True, stop=False)
                    last = T.e.matmul(out, q_pair[m][halves[m], cut], k_lo[halves[m], keys_], start=False, stop=True)
                soft[q, m] = T.did(last)

        def softmax(q):
            count, s, b = keys(q)[1], st[:, q % 2, :], q % 2
            if q >= 2:
                V.wait(turned[q - 2])
                A.wait(turned[q - 2])
            for m in (0, 1):
                V.wait(soft[q, m])
                mx = V.did(V.e.tensor_reduce(s[:, m:m + 1], p.banks(ring(q, m), count), AX, ALU.max))
                V.wait(mx)
                neg = V.did(V.e.tensor_scalar(s[:, 2 + m:3 + m], s[:, m:m + 1], -QK ** -0.5, None, ALU.mult))
                A.wait(neg)
                exps[2 * q + m] = A.did(A.e.activation(prob[b][m][:, 0:count], p.banks(ring(q, m), count), ACT.Exp,
                                                       bias=s[:, 2 + m:3 + m], scale=QK ** -0.5,
                                                       accum_out=s[:, 4 + m:5 + m]))

        def combine(q):
            count, s, b = keys(q)[1], st[:, q % 2, :], q % 2
            V.wait(exps[2 * q], exps[2 * q + 1])
            V.wait(V.did(V.e.reciprocal(s[:, 6:8], s[:, 4:6])))
            V.wait(V.did(V.e.tensor_scalar(prob[b][1][:, 0:count], prob[b][1][:, 0:count], s[:, 7:8],
                                           neg_lam[:, l:l + 1], ALU.mult, ALU.mult)))
            combined[q] = V.did(V.e.scalar_tensor_tensor(prob[b][0][:, 0:count], prob[b][0][:, 0:count], s[:, 6:7],
                                                         prob[b][1][:, 0:count], ALU.mult, ALU.add))

        def transpose(q):
            first, count = keys(q)
            b, k0 = q % 2, first // P
            T.wait(combined[q], moved[q - 1] if q else v_ready)
            for k in range(count // P):
                last = T.e.transpose(p.banks(6, count)[:, k * P:(k + 1) * P], prob[b][0][:, k * P:(k + 1) * P], p.ident)
            turned[q] = T.did(last)
            A.wait(turned[q])
            moved[q] = A.did(A.e.activation(pt[:, k0:k0 + count // P, q * P:(q + 1) * P],
                                            p.banks(6, count).rearrange("p (k n) -> p k n", n=P), ACT.Copy))

        scores(0)
        for k in range(TA // P):
            last = T.e.transpose(p.banks(6, TA)[:, k * P:(k + 1) * P], vt[:, k * P:(k + 1) * P], p.ident)
        A.wait(T.did(last))
        v_ready = A.did(A.e.activation(v[:, :, :].rearrange("p k n -> p (k n)"), p.banks(6, TA), ACT.Copy))
        softmax(0)
        for q in range(1, queries + 1):
            if q < queries:
                scores(q)
            combine(q - 1)
            if q < queries:
                softmax(q)
            transpose(q - 1)
        if following is not None:
            prepare(following, [soft[queries - 1, 1], v_ready])
        for out, (first, count, k0) in enumerate(((0, TX, 0), (TX, TC, TX // P))[:outs]):
            T.wait(moved[queries - 1])
            for k in range(k0, TA // P):
                last = T.e.matmul(p.ps[:, 6 + out, 0:count], v[:, k, :], pt[:, k, first:first + count],
                                  start=(k == k0), stop=(k == TA // P - 1))
            A.wait(T.did(last))
            at = proj[:, i + TILE_Q:i + TILE_Q + 1, :] if isinstance(i, int) else proj[:, bass.ds(i + TILE_Q, 1), :]
            A.did(A.e.activation(flat(at)[:, first:first + count], p.ps[:, 6 + out, 0:count], ACT.Copy))

    prepare(0, [])
    with passes(p.nc, HEADS - 1, {T: 1 + 3 * n + outs, V: 4 + 7 * n, A: 6 + 3 * n + outs, G: 2}) as i:
        head(i, i + 1)
    head(HEADS - 1, None)
    return [e.now() for e in (T, V, A, G)]


def mix(p, l, proj, sub_gain, t, ready):
    T, V, A, G, base = p.T, p.V, p.A, p.G, p.mix_scratch
    sq = [p.place(f"m_sq{l}{b}", [P, TA], at=base + 3072 * b) for b in range(3)]
    for e in (T, V, A, G):
        e.wait(*ready)
    heads = [(proj[:, TILE_Q + h, 0:t], sub_gain[:, l:l + 1], proj[:, TILE_G + 4 + h, 0:t]) for h in range(HEADS)]
    plain = [(proj[:, tile, 0:t], None, proj[:, TILE_G + k, 0:t])
             for k, tile in enumerate((TILE_A, TILE_A + 1, TILE_B, TILE_B + 1))]
    return norm_gate_split(p, plain + heads, t, [s[:, 0:t] for s in sq])


def norm_gate_split(p, items, t, sq):
    T, V, A, G = p.T, p.V, p.A, p.G
    heads = [k for k, (_, gain, _) in enumerate(items) if gain is not None]
    squared, summed, scaled, gated, hi, lo = ({} for _ in range(6))
    per = t // P
    for n, k in enumerate(heads):
        if n >= 3:
            A.wait(summed[heads[n - 3]])
        squared[k] = A.did(A.e.activation(sq[n % 3], items[k][0], ACT.Square))
        T.wait(squared[k])
        summed[k] = p.token_sums(4, n * per, sq[n % 3], t, p.ones[:, 0:1])
    roots = p.inverse_roots(p.roots[:, 0:len(heads) * per], p.ps[:, 4, 0:len(heads) * per], P, [summed[heads[-1]]])

    def scale(k):
        o, gain, _ = items[k]
        if k in squared:
            n = heads.index(k)
            b = 6 - 2 * (n % 2)
            T.wait(roots)
            if n >= 2:
                T.wait(scaled[k - 2])
            V.wait(p.spread(b, p.roots, n * per, t))
            scaled[k] = V.did(V.e.scalar_tensor_tensor(o, o, gain, p.banks(b, t), ALU.mult, ALU.mult))

    def gate(k):
        o, _, g = items[k]
        if k in scaled:
            V.wait(scaled[k])
        gated[k] = V.did(V.e.tensor_tensor(o, o, g, ALU.mult))

    def high(k):
        A.wait(gated[k])
        hi[k] = A.did(A.e.activation(p.h_hi[:, k, 0:t], items[k][0], ACT.Copy))

    def low(k):
        e = V if k % 3 == 0 else G
        e.wait(gated[k], hi[k])
        lo[k] = e.did(e.e.tensor_tensor(p.h_lo[:, k, 0:t], items[k][0], p.h_hi[:, k, 0:t].bitcast(F32),
                                        ALU.subtract))

    pipeline(len(items), scale, gate, high, low)
    return [[hi[k], lo[k]] for k in range(len(items))], [V.now(), A.now(), G.now()]


RQ, RK, RV, RG, HQ, HF, HI, HG = range(0, 32, 4)
SH1, SC1, G1, SH2, SC2, G2 = range(0, 48, 8)


def second_block(p):
    nc, T, V, A, G, S = p.nc, p.T, p.V, p.A, p.G, p.S
    p.place_ring("second", SLOT)
    rope = p.place("rope_half", [P, 2, TX])
    decay = p.place("decay", [P, HEADS, TX])
    masks = p.place("level_masks", [P, 8, P], I32)
    vec = p.place("layer_vectors", [P, 176])
    bounds = p.place("lower_bounds", [P, 2, HEADS])
    proj = p.place("proj_second", [P, 32, TX])
    room = p.top - 32 * TX * 4
    buffers = [p.place(f"norm_second{b}", [P, TX], at=room + b * 2048) for b in range(1, 7)]
    p.norm_buffers = (buffers[0:3], buffers[3:6])
    square = p.place("square_second", [P, TX], at=room + 50 * 1024)
    act_hi = p.place("act_hi", [P, FFH, TX], F32R, at=room)
    act_lo = p.place("act_lo", [P, FFH, TX], F32R, at=room + FFH * 2048)
    conv = p.place("conv", [P, TX], at=room + 2 * FFH * 2048)
    actf = p.place("act_value", [P, TX], at=room + 2 * FFH * 2048 + 2048)
    conv_linear = nc.alloc_semaphore("conv_linear")
    conv_silu = nc.alloc_semaphore("conv_silu")
    tables_in = nc.alloc_semaphore("second_tables_landed")
    for dst, name in ((rope, "rope_half"), (decay, "decay"), (masks, "level_masks")):
        S.e.dma_start(dst[:, :, :], p.dram[name]).then_inc(tables_in, 16)

    lg, e = p.column("hgrn_lb_logits_2", 0, 8), p.small[:, 16:24]
    mx, tot = p.small[:, 24:28], p.small[:, 28:32]
    t = V.did(V.e.tensor_tensor(mx, lg[:, 0:4], lg[:, 4:8], ALU.max))
    for l in range(2):
        V.wait(t)
        V.did(V.e.tensor_tensor(e[:, 4 * l:4 * l + 4], lg[:, 4 * l:4 * l + 4], mx, ALU.subtract))
    A.wait(V.now())
    t = A.did(A.e.activation(e, e, ACT.Exp))
    V.wait(t)
    t = V.did(V.e.tensor_tensor(tot, e[:, 0:4], e[:, 4:8], ALU.add))
    V.wait(t)
    t = V.did(V.e.reciprocal(tot, tot))
    V.wait(t)
    for l in range(2):
        V.did(V.e.tensor_tensor(e[:, 4 * l:4 * l + 4], e[:, 4 * l:4 * l + 4], tot, ALU.mult))
    V.wait(V.now())
    t = V.did(V.e.tensor_tensor(mx, e[:, 0:4], e[:, 4:8], ALU.add))
    V.did(V.e.tensor_tensor(bounds[:, 0, :], e[:, 0:4], e[:, 0:4], ALU.subtract))
    V.wait(t)
    V.did(V.e.tensor_tensor(bounds[:, 1, :], mx, e[:, 0:4], ALU.subtract))
    for en in (V, A, T, G, S):
        en.wait(V.now(), (tables_in, 48))

    layer_sems = [x.sem for x in (T, V, A, G)] + [A.hold, S.hold, conv_linear, conv_silu,
                  *p.landed, *p.rounded, *p.split, *p.used, *p.freed]

    def new_layer():
        nc.all_engine_barrier()
        for s in layer_sems:
            G.e.sem_clear(s)
        nc.all_engine_barrier()

    new_layer()
    with nc.Fori(0, 2) as l:
        for en in (T, V, A, G):
            en.e.sem_inc(en.sem, 1)
            en.n = 1
        p.grant_slots(V)
        fields, places, at = {}, {}, 0
        def take(name, src, n):
            nonlocal at
            fields[name], places[name] = vec[:, at:at + n], at
            V.did(V.e.tensor_copy(vec[:, at:at + n], src))
            at += n
        c = p.col
        take("mod", p.mod2[:, bass.ds(l * 48, 48)], 48)
        take("norm1", p.colsf[:, bass.ds(l * 8 + c["norm1_w_2"], 8)], 8)
        take("norm2", p.colsf[:, bass.ds(l * 8 + c["norm2_w_2"], 8)], 8)
        take("head_gain_r", p.colsf[:, bass.ds(l * 4 + c["ret_norm_w_2"], 4)], 4)
        take("head_gain_h", p.colsf[:, bass.ds(l * 4 + c["hgrn_norm_w_2"], 4)], 4)
        take("conv_b", p.colsf[:, bass.ds(l * 22 + c["conv_b_2"], 22)], 22)
        take("conv_w", p.colsf[:, bass.ds(l * (c["conv_w1"] - c["conv_w0"]) + c["conv_w0"], 66)], 66)
        take("lb", bounds[:, bass.ds(l, 1), :].rearrange("p o h -> p (o h)"), 4)
        V.wait(V.now())
        gains = p.small[:, 32:48]
        keep = p.small[:, 48:52]
        mod = fields["mod"]
        V.did(V.e.scalar_tensor_tensor(gains[:, 0:8], mod[:, SC1:SC1 + 8], 1.0, fields["norm1"], ALU.add, ALU.mult))
        V.did(V.e.scalar_tensor_tensor(gains[:, 8:16], mod[:, SC2:SC2 + 8], 1.0, fields["norm2"], ALU.add, ALU.mult))
        vectors = V.did(V.e.tensor_scalar(keep, fields["lb"], -1.0, 1.0, ALU.mult, ALU.add))

        def columns_of(name, first):
            def source(i, j):
                return p.dram[name].rearrange("l (k p) n -> p l k n", p=P)[
                    :, bass.ds(l, 1), :, bass.ds(i * (2 * P) + (first + j) * P, P)].rearrange("p o k n -> p (o k) n")
            return source

        p.prime(KT)
        V.wait(vectors); A.wait(vectors)
        h_tiles = p.norm(TX, [vectors], [(0, TX, gains[:, 0:8], mod[:, SH1:SH1 + 8])], [])
        only_x = [(0, 0, TX)]

        def to_proj(first, func):
            def evac(i, j, use):
                A.wait((p.used[j], use))
                A.e.activation(flat(proj[:, bass.ds(i * 2 + (first + j), 1), :]), p.ps[:, j, :],
                               func).then_inc(p.freed[j], 1)
            return evac

        p.linear(12, KT, columns_of("w_in_2", RQ), only_x, [], to_proj(RQ, ACT.Identity), then_k=KT,
                 ready_tiles=h_tiles)
        counts, steps = retention(p, proj, room, rope, decay, list(p.banks_read))
        p.linear_beside(8, KT, columns_of("w_in_2", RG), only_x, to_proj(RG, ACT.Silu), counts, steps)
        retention_done = [e.now() for e in (T, V, A, G)]
        A.wait(*retention_done)
        for first, n, func in ((HF, 8, ACT.Identity), (HG, 4, ACT.Silu)):
            p.linear(n, KT, columns_of("w_in_2", first), only_x, [], to_proj(first, func), then_k=KT)
        projected = [*p.banks_read, p.product_done, *retention_done]
        hgrn_done = hgrn(p, proj, masks, fields["lb"], keep, projected)
        h_tiles, mixed = mix_heads(p, proj, fields, hgrn_done)

        def residual(gate, squares):
            def evac(i, j, use):
                V.wait((p.used[j], use))
                xk = flat(p.xT[:, bass.ds(i * 2 + j, 1), X_])
                V.e.scalar_tensor_tensor(xk, p.ps[:, j, :], vec[:, bass.ds(i * 2 + (gate + j), 1)], xk,
                                         ALU.mult, ALU.add).then_inc(p.freed[j], 1)
                V.wait((p.freed[j], use))
                if squares:
                    p.add_squares(xk, X_, square[:, :])
            return evac

        V.wait(*mixed)
        V.wait(V.did(V.e.memset(p.ssq[:, X_], 0.0)))
        p.linear(8, KT, columns_of("w_out_2", 0), only_x, [], lambda i, j, use: None, residual(G1, True),
                 vec_counts=4, then_k=KT, ready_tiles=h_tiles)

        h_tiles = p.norm(TX, [*p.banks_read, V.now()], [(0, TX, gains[:, 8:16], mod[:, SH2:SH2 + 8])],
                         [*p.banks_read, p.product_done, *mixed])
        for half in range(2):
            done0 = half * FFH

            def gate_val(i, j, half=half):
                name = ("w_gate_2", "w_val_2")[j]
                return p.dram[name].rearrange("l (k p) n -> p l k n", p=P)[
                    :, bass.ds(l, 1), :, bass.ds(i * P + half * FFH * P, P)].rearrange("p o k n -> p (o k) n")

            def conv_col(i, k, half=half):
                return vec[:, bass.ds(i + (places["conv_w"] + k * 2 * FFH + half * FFH), 1)]

            def bias_col(i, half=half):
                return vec[:, bass.ds(i + (places["conv_b"] + half * FFH), 1)]

            def act_side(i, j, use):
                if j == 0:
                    A.wait((p.used[0], use), (p.freed[1], use - 1))
                    A.e.activation(conv[:, :], p.ps[:, 0, :], ACT.Identity, bias=bias_col(i),
                                   scale=conv_col(i, 2)).then_inc(conv_linear, 1)
                else:
                    A.wait((p.freed[0], use))
                    A.e.activation(conv[:, :], conv[:, :], ACT.Silu).then_inc(conv_silu, 1)

            def vec_side(i, j, use, done0=done0):
                if j == 0:
                    V.wait((conv_linear, i + (done0 + 1)))
                    t = V.did(V.e.scalar_tensor_tensor(conv[:, 1:TX], p.ps[:, 0, 0:TX - 1], conv_col(i, 1),
                                                       conv[:, 1:TX], ALU.mult, ALU.add))
                    V.wait(t)
                    V.e.scalar_tensor_tensor(conv[:, 2:TX], p.ps[:, 0, 0:TX - 2], conv_col(i, 0), conv[:, 2:TX],
                                             ALU.mult, ALU.add).then_inc(p.freed[0], 1)
                else:
                    V.wait((conv_silu, i + (done0 + 1)), (p.used[1], use))
                    V.e.tensor_tensor(actf[:, :], conv[:, :], p.ps[:, 1, :], ALU.mult).then_inc(p.freed[1], 1)
                    V.wait((p.freed[1], use))
                    hi_t, lo_t = (flat(x[:, bass.ds(i, 1), :]) for x in (act_hi, act_lo))
                    t = V.did(V.e.tensor_copy(hi_t, actf[:, :]))
                    V.wait(t)
                    V.wait(V.did(V.e.tensor_tensor(lo_t, actf[:, :], hi_t.bitcast(F32), ALU.subtract)))

            V.wait(p.product_done)
            p.linear(2 * FFH, KT, gate_val, only_x, [], act_side, vec_side, vec_counts=3, then_k=FFH,
                     ready_tiles=h_tiles if half == 0 else None)
            act_ready = [V.now()]

            def down(i, j, half=half):
                return p.dram["w_down_2"].rearrange("l (k p) n -> p l k n", p=P)[
                    :, bass.ds(l, 1), half * FFH:(half + 1) * FFH, bass.ds(i * (2 * P) + j * P, P)].rearrange(
                    "p o k n -> p (o k) n")

            p.act_pair = (act_hi, act_lo)
            if half == 1:
                V.wait(V.did(V.e.memset(p.ssq[:, X_], 0.0)))
            p.linear(8, FFH, down, only_x, act_ready, lambda i, j, use: None, residual(G2, half == 1),
                     vec_counts=4 if half == 1 else 0,
                     then_k=KT if half == 0 else None)
            p.act_pair = None
        for en in (T, V, A, G, S):
            en.wait(*p.banks_read, p.product_done)
        new_layer()
    for en in (T, V, A, G):
        en.e.sem_inc(en.sem, 1)
        en.n = 1
    final_norm(p, proj)


def retention(p, proj, room, rope, decay, ready):
    T, V, A, G, base = p.T, p.V, p.A, p.G, room + HF * TX * 4
    q = [p.place(f"r_{n}", [P, TX], at=base + 2048 * k) for k, n in enumerate(("q", "k"))]
    t2 = [p.place(f"r_t{k}", [P, TX], at=base + 4096 + 2048 * k) for k in range(2)]
    vt = p.place("r_vt", [P, TX], at=base + 8192)
    v = p.place("r_v", [P, 4, P], at=base + 10240)
    st = p.place("r_st", [P, 4, TX], at=base + 12288)
    turn_banks, v_bank, score_banks, out_bank = (6, 7), 2, (3, 4, 6, 2), 5
    for e in (T, V, A, G):
        e.wait(*ready)

    def steps(i):
        start = [T.now(), V.now(), A.now()]
        rotated, decayed, v_ready = [], [], []

        def rotate():
            for e in (T, V, A, G):
                e.wait(start[0], start[1])
            v_in = G.did(G.e.tensor_copy(vt[:, :], flat(proj[:, bass.ds(i + RV, 1), :])))
            for k, tile in enumerate((RQ, RK)):
                x = flat(proj[:, bass.ds(i + tile, 1), :])
                turned = T.did(T.e.matmul(p.ps[:, turn_banks[k], :], p.rot_half, x, start=True, stop=True))
                a = V.did(V.e.tensor_tensor(q[k][:, :], x, rope[:, 0, :], ALU.mult))
                V.wait(turned)
                b = V.did(V.e.tensor_tensor(t2[k][:, :], p.ps[:, turn_banks[k], :], rope[:, 1, :], ALU.mult))
                V.wait(a, b)
                rotated.append(V.did(V.e.tensor_tensor(q[k][:, :], q[k][:, :], t2[k][:, :], ALU.add)))
            T.wait(v_in)
            for k in range(4):
                last = T.e.transpose(p.ps[:, v_bank, k * P:(k + 1) * P], vt[:, k * P:(k + 1) * P], p.ident)
            A.wait(T.did(last))
            v_ready.append(A.did(A.e.activation(v[:, :, :].rearrange("p k n -> p (k n)"), p.ps[:, v_bank, :],
                                                ACT.Copy)))

        def score():
            T.wait(*rotated, *v_ready)
            for j in range(4):
                w, bank = TX - j * P, score_banks[j]
                s = T.did(T.e.matmul(p.ps[:, bank, 0:w], q[1][:, j * P:(j + 1) * P], q[0][:, j * P:TX], start=True,
                                     stop=True))
                V.wait(s)
                decayed.append(V.did(V.e.tensor_tensor(st[:, j, 0:w], p.ps[:, bank, 0:w],
                                                       decay[:, bass.ds(i, 1), 0:w].rearrange("p o t -> p (o t)"),
                                                       ALU.mult)))

        def combine():
            T.wait(start[2], *decayed)
            for j in range(4):
                last = T.e.matmul(p.ps[:, out_bank, j * P:TX], v[:, j, :], st[:, j, 0:TX - j * P], start=(j == 0),
                                  stop=(j == 3))
            A.wait(T.did(last))
            A.did(A.e.activation(flat(proj[:, bass.ds(i + RQ, 1), :]), p.ps[:, out_bank, :], ACT.Copy))

        return rotate, score, combine

    return {T: 8, V: 10, A: 2, G: 1}, steps


def hgrn(p, proj, masks, lb, keep, ready):
    T, V, A, G, base = p.T, p.V, p.A, p.G, p.lower
    N = HEADS * TX
    names = ("fwd", "bwd", "key", "q_level", "k_level")
    fwd, bwd, key, ql, kl = (p.place(f"h_{n}", [P, N], at=base + 8192 * k) for k, n in enumerate(names))
    diag = p.place("h_diag", [P, N], at=base + 8192 * 5)
    z = proj[:, HF:HF + 4, :].rearrange("p h t -> p (h t)")
    q = proj[:, HQ:HQ + 4, :].rearrange("p h t -> p (h t)")
    room = proj[:, RK:RK + 8, :].rearrange("p h t -> p (h t)")
    v = room[:, 0:N].rearrange("p (h k n) -> p h k n", h=4, k=4)
    near = room[:, N:2 * N]
    far = z
    for e in (T, V, A, G):
        e.wait(*ready)
    copied = []
    for h in range(HEADS):
        for k in range(4):
            last = T.e.transpose(p.ps[:, 4 + h, k * P:(k + 1) * P], proj[:, HI + h, k * P:(k + 1) * P], p.ident)
        t_ = T.did(last)
        A.wait(t_)
        copied.append(A.did(A.e.activation(v[:, h, :, :].rearrange("p k n -> p (k n)"), p.ps[:, 4 + h, :], ACT.Copy)))
    sp = A.did(A.e.activation(fwd[:, :], z, ACT.Sigmoid))
    sn = A.did(A.e.activation(kl[:, :], z, ACT.Sigmoid, scale=-1.0))
    V.wait(sp, sn)
    V.did(V.e.memset(bwd[:, :], 1.0))
    for h in range(HEADS):
        cut = slice(h * TX, (h + 1) * TX)
        V.did(V.e.scalar_tensor_tensor(fwd[:, cut], kl[:, cut], lb[:, h:h + 1], fwd[:, cut], ALU.mult, ALU.add))
        last_key = V.did(V.e.tensor_scalar(key[:, cut], kl[:, cut], keep[:, h:h + 1], None, ALU.mult))
    zero = V.did(V.e.memset(diag[:, :], 0.0))
    scored, grown, split = {}, last_key, N * 5 // 8
    ql_, kl_ = [ql[:, :], z], [kl[:, :], near]
    T.wait(*copied, last_key)
    taken = {}

    def take(level):
        V.wait(scored[level], zero, *([taken[level - 1]] if level else []))
        taken[level] = V.did(V.e.copy_predicated(
            diag[:, :].rearrange("p (c n) -> p c n", n=P),
            masks[:, level:level + 1, :].broadcast_to([P, 16, P]),
            p.banks(4 * (level % 2), N).rearrange("p (c n) -> p c n", n=P)))

    for level in range(len(LEVELS) + 1):
        set_ = 4 * (level % 2)
        ql, kl = ql_[level % 2], kl_[level % 2]
        if level == 0:
            rhs, lhs = q, key[:, :]
        else:
            if level >= 2:
                V.wait(scored[level - 2])
                G.wait(scored[level - 2])
            V.wait(grown)
            a = V.did(V.e.tensor_tensor(ql, q, fwd[:, :], ALU.mult))
            G.wait(grown, last_key)
            b = G.did(G.e.tensor_tensor(kl[:, 0:split], key[:, 0:split], bwd[:, 0:split], ALU.mult))
            b_rest = V.did(V.e.tensor_tensor(kl[:, split:N], key[:, split:N], bwd[:, split:N], ALU.mult))
            T.wait(a, b, b_rest)
            rhs, lhs = ql, kl
            half = LEVELS[level - 1]
            fb, bb = (x[:, :].rearrange("p (b t) -> p b t", t=2 * half) for x in (fwd, bwd))
            shape = [P, N // (2 * half), half]
            G.wait(b, b_rest)
            w = G.did(G.e.tensor_tensor(bb[:, :, 0:half], bb[:, :, 0:half],
                                        fb[:, :, 2 * half - 1:2 * half].broadcast_to(shape), ALU.mult))
            V.wait(a, w)
            grown = V.did(V.e.tensor_tensor(fb[:, :, half:2 * half], fb[:, :, half:2 * half],
                                            fb[:, :, half - 1:half].broadcast_to(shape), ALU.mult))
            take(level - 1)
        if level >= 2:
            T.wait(taken[level - 2])
        for c in range(16):
            last = T.e.matmul(p.ps[:, set_ + c // 4, (c % 4) * P:(c % 4 + 1) * P], lhs[:, c * P:(c + 1) * P],
                              rhs[:, c * P:(c + 1) * P], start=True, stop=True)
        scored[level] = T.did(last)
    ql, kl = ql_[0], kl_[0]
    V.wait(grown, scored[6])
    a = V.did(V.e.tensor_tensor(ql, q, fwd[:, :], ALU.mult))
    G.wait(grown, scored[6])
    b = G.did(G.e.tensor_tensor(kl[:, 0:split], key[:, 0:split], bwd[:, 0:split], ALU.mult))
    b_rest = V.did(V.e.tensor_tensor(kl[:, split:N], key[:, split:N], bwd[:, split:N], ALU.mult))
    take(7)
    T.wait(a, b, b_rest, taken[6])
    for h in range(HEADS):
        for c in range(2):
            at = (4 * h + 2 * c) * P
            last = T.e.matmul(p.ps[:, h // 2, ((h % 2) * 2 + c) * P:((h % 2) * 2 + c + 1) * P], kl[:, at:at + P],
                              ql[:, at + P:at + 2 * P], start=True, stop=True)
    near_scored = T.did(last)
    A.wait(near_scored, scored[7])
    near_in = A.did(A.e.activation(near[:, 0:1024], p.banks(0, 1024), ACT.Copy))
    V.wait(a, b, b_rest)
    fb, bb = (x[:, :].rearrange("p (b t) -> p b t", t=2 * P) for x in (fwd, bwd))
    shape = [P, N // (2 * P), P]
    w = V.did(V.e.tensor_tensor(bb[:, :, 0:P], bb[:, :, 0:P], fb[:, :, 2 * P - 1:2 * P].broadcast_to(shape), ALU.mult))
    V.wait(w)
    w = V.did(V.e.tensor_tensor(fb[:, :, P:2 * P], fb[:, :, P:2 * P], fb[:, :, P - 1:P].broadcast_to(shape), ALU.mult))
    V.wait(w, near_scored)
    a = V.did(V.e.tensor_tensor(ql[:, :], q, fwd[:, :], ALU.mult))
    G.wait(w, near_scored)
    b = G.did(G.e.tensor_tensor(kl[:, 0:split], key[:, 0:split], bwd[:, 0:split], ALU.mult))
    b_rest = V.did(V.e.tensor_tensor(kl[:, split:N], key[:, split:N], bwd[:, split:N], ALU.mult))
    T.wait(a, b, b_rest, taken[7], near_in)
    for h in range(HEADS):
        for c in range(2):
            at = 4 * h * P
            last = T.e.matmul(p.ps[:, 4 + h, c * 256:(c + 1) * 256], kl[:, at + c * P:at + (c + 1) * P],
                              ql[:, at + 2 * P:at + 4 * P], start=True, stop=True)
    A.wait(T.did(last), scored[7])
    far_in = A.did(A.e.activation(far, p.banks(4, N), ACT.Copy))
    T.wait(near_in, far_in, taken[7])
    sources = lambda h, tq: (
        [(k, far[:, h * TX + k * 256 + (tq - 2) * P:][:, 0:P]) for k in (0, 1)] if tq >= 2 else []) + (
        [(tq - 1, near[:, (2 * h + tq // 2) * P:][:, 0:P])] if tq % 2 else []) + [
        (tq, diag[:, (4 * h + tq) * P:][:, 0:P])]
    for h in range(HEADS):
        for tq in range(4):
            terms = sources(h, tq)
            for n, (k, s) in enumerate(terms):
                last = T.e.matmul(p.ps[:, h, tq * P:(tq + 1) * P], v[:, h, k, :], s, start=(n == 0),
                                  stop=(n == len(terms) - 1))
        A.wait(T.did(last))
        A.did(A.e.activation(proj[:, HQ + h, :], p.ps[:, h, :], ACT.Copy))
    return [T.now(), V.now(), A.now(), G.now()]


def mix_heads(p, proj, fields, ready):
    T, V, A, G = p.T, p.V, p.A, p.G
    for e in (T, V, A, G):
        e.wait(*ready)
    items = [(proj[:, RQ + h, :], fields["head_gain_r"][:, h:h + 1], proj[:, RG + h, :]) for h in range(HEADS)] + \
            [(proj[:, HQ + h, :], fields["head_gain_h"][:, h:h + 1], proj[:, HG + h, :]) for h in range(HEADS)]
    return norm_gate_split(p, items, TX, [proj[:, RK + b, :] for b in range(3)])


def final_norm(p, proj):
    T, V, A, S = p.T, p.V, p.A, p.S
    y = [proj[:, 3 + b, :] for b in (0, 1)]
    rows = proj[:, 8:16, :].rearrange("p a t -> p (a t)").rearrange("p (t d) -> p t d", d=D)
    sums = p.token_sums(0, 0, p.ssq, TX, p.ones[:, 0:1])
    T.wait(p.inverse_roots(p.roots[:, 0:TX // P], p.ps[:, 0, 0:TX // P], D, [sums]))
    V.wait(p.spread(1, p.roots, 0, TX))
    turned, copied = [], []
    for k in range(KT):
        b = k % 2
        if k >= 2:
            V.wait(turned[k - 2])
            T.wait(copied[k - 2])
        T.wait(V.did(V.e.scalar_tensor_tensor(y[b], p.xT[:, k, X_], p.column("final_norm_w_2", k), p.ps[:, 1, :],
                                              ALU.mult, ALU.mult)))
        for t in range(4):
            last = T.e.transpose(p.ps[:, 2 + b, t * P:(t + 1) * P], y[b][:, t * P:(t + 1) * P], p.ident)
        turned.append(T.did(last))
        A.wait(turned[-1])
        copied.append(A.did(A.e.activation(rows[:, :, k * P:(k + 1) * P],
                                           p.ps[:, 2 + b, :].rearrange("p (t n) -> p t n", n=P), ACT.Copy)))
    S.wait(A.now())
    S.e.dma_start(p.dram["out"].rearrange("b (t p) d -> p (b t) d", p=P), rows).then_inc(p.out_stored, 16)
    S.wait((p.out_stored, 16))


def kernel(**inputs):
    import concourse.bacc as bacc
    from concourse.bass_utils import run_bass_kernel_spmd as run

    nc = bacc.Bacc("TRN2", target_bir_lowering=False, num_devices=1)
    arrays = {k: np.ascontiguousarray(v) for k, v in inputs.items()}
    arrays.update(tables())
    dram = {k: nc.dram_tensor(f"in_{k}", v.shape, mybir.dt.from_np(v.dtype), kind="ExternalInput").ap()
            for k, v in arrays.items()}
    dram["out"] = nc.dram_tensor("out", (1, TX, D), F32, kind="ExternalOutput").ap()
    p = Program(nc, dram)
    x_ready = first_block(p)
    for e in (p.T, p.V, p.A, p.G, p.S):
        e.wait(*x_ready, p.mod_last)
    second_block(p)
    r = run(nc, [{f"in_{k}": v for k, v in arrays.items()}], core_ids=[0])
    return r.results[0]["out"]
```
